# Optimizing a Trainium2 kernel written in Bass

```python
import math
import jax, jax.numpy as jnp
from jax import lax
import numpy as np

D_MODEL = 1024
BATCH = 1
SEQ = 512
DEPTH = 1
DEC_BATCH = 8
DEC_SEQ = 16
PAST_LEN = 256

CHUNK = 64
QBLOCK = 128
HEAD_DIM = 64
FOX_HEADS = 8
DIFF_HEADS = 4
DIFF_V_DIM = 2 * HEAD_DIM
ROT_DIM = HEAD_DIM // 4
ROPE_THETA = 500000.0
MEM_LEN = 256
MEM_HEADS = 4
MEM_HEAD_DIM = D_MODEL // MEM_HEADS
N_GROUPS = 4
EXPERTS_PER_GROUP = 8
N_EXPERTS = N_GROUPS * EXPERTS_PER_GROUP
TOP_K = 2
D_EXPERT = 512
MOE_BLOCK = 128
EPS = 1e-6
FORGET_BIAS_INIT = 3.0

FOX_W = FOX_HEADS * HEAD_DIM
DIFF_QK_W = DIFF_HEADS * 2 * HEAD_DIM
DIFF_V_W = DIFF_HEADS * DIFF_V_DIM
MIX_W = FOX_W + DIFF_V_W
IN_W = 3 * FOX_W + FOX_HEADS + 2 * DIFF_QK_W + DIFF_V_W
SPLITS = [FOX_W, 2 * FOX_W, 3 * FOX_W, 3 * FOX_W + FOX_HEADS,
          3 * FOX_W + FOX_HEADS + DIFF_QK_W, 3 * FOX_W + FOX_HEADS + 2 * DIFF_QK_W]

kernel_name = "streaming_fox_diffattn_hiermoe_step"

F32 = jnp.float32

def _rmsnorm(x, g):
    xf = x.astype(F32)
    y = xf * lax.rsqrt(jnp.mean(xf * xf, axis=-1, keepdims=True) + EPS)
    return (y * g.astype(F32)).astype(x.dtype)

def _partial_rope(x, pos):
    half = ROT_DIM // 2
    inv = jnp.power(ROPE_THETA, -jnp.arange(half, dtype=F32) / half)
    ang = pos.astype(F32)[:, None] * inv[None, :]
    ang = ang.reshape((pos.shape[0],) + (1,) * (x.ndim - 3) + (half,))
    cos, sin = jnp.cos(ang), jnp.sin(ang)
    xr = x[..., :ROT_DIM].astype(F32)
    x1, x2 = xr[..., :half], xr[..., half:]
    rot = jnp.concatenate([x1 * cos - x2 * sin, x2 * cos + x1 * sin], axis=-1).astype(x.dtype)
    return jnp.concatenate([rot, x[..., ROT_DIM:]], axis=-1)

def _sweep_queries(fn, q_args, T):
    if T <= QBLOCK:
        return fn(*q_args)
    nb = T // QBLOCK
    blocks = tuple(jnp.moveaxis(a.reshape((a.shape[0], nb, QBLOCK) + a.shape[2:]), 1, 0) for a in q_args)
    out = lax.map(lambda args: fn(*args), blocks)
    return jnp.moveaxis(out, 0, 1).reshape((out.shape[1], T) + out.shape[3:])

def _fox_attention(q, k, v, cq, ck, qpos, kpos):
    scale = HEAD_DIM ** -0.5
    ckT = jnp.swapaxes(ck, 1, 2)

    def block(qb, cqb, qposb):
        s = jnp.einsum('bqhd,bkhd->bhqk', qb, k, preferred_element_type=F32) * scale
        s = s + jnp.swapaxes(cqb, 1, 2)[..., :, None] - ckT[:, :, None, :]
        mask = kpos[None, :] <= qposb[0][:, None]
        p = jax.nn.softmax(jnp.where(mask, s, -jnp.inf), axis=-1)
        return jnp.einsum('bhqk,bkhd->bqhd', p.astype(v.dtype), v)

    return _sweep_queries(block, (q, cq, qpos[None, :]), q.shape[1])

def _diff_attention(q, k, v, lam, qpos, kpos):
    scale = HEAD_DIM ** -0.5

    def block(qb, qposb):
        s = jnp.einsum('bqhcd,bkhcd->bhcqk', qb, k, preferred_element_type=F32) * scale
        mask = (kpos[None, :] // CHUNK) <= (qposb[0][:, None] // CHUNK)
        p = jax.nn.softmax(jnp.where(mask, s, -jnp.inf), axis=-1)
        a = p[:, :, 0] - lam * p[:, :, 1]
        return jnp.einsum('bhqk,bkhe->bqhe', a.astype(v.dtype), v)

    return _sweep_queries(block, (q, qpos[None, :]), q.shape[1])

def _mem_attention(q, k, v):
    scale = MEM_HEAD_DIM ** -0.5

    def block(qb):
        s = jnp.einsum('bqhd,bkhd->bhqk', qb, k, preferred_element_type=F32) * scale
        p = jax.nn.softmax(s, axis=-1)
        return jnp.einsum('bhqk,bkhd->bqhd', p.astype(v.dtype), v)

    return _sweep_queries(block, (q,), q.shape[1])

def _memory_kv(mem, g_mem_kv, w_mk, w_mv):
    B = mem.shape[0]
    m = _rmsnorm(mem, g_mem_kv)
    k = (m @ w_mk).reshape(B, MEM_LEN, MEM_HEADS, MEM_HEAD_DIM)
    v = (m @ w_mv).reshape(B, MEM_LEN, MEM_HEADS, MEM_HEAD_DIM)
    return k, v

def _hier_moe(h, w_group, b_group, w_erouter, b_erouter, w1, w3, w2):
    B, T, D = h.shape
    N = B * T
    x = h.reshape(N, D)
    g_logits = (x @ w_group).astype(F32) + b_group.astype(F32)
    g_prob = jax.nn.softmax(g_logits, axis=-1)
    g_idx = jnp.argmax(g_logits, axis=-1)
    g_p = jnp.take_along_axis(g_prob, g_idx[:, None], axis=-1)
    e_logits = ((x @ w_erouter).astype(F32) + b_erouter.astype(F32)).reshape(N, N_GROUPS, EXPERTS_PER_GROUP)
    e_logits = jnp.take_along_axis(e_logits, g_idx[:, None, None], axis=1)[:, 0]
    top_p, top_i = lax.top_k(jax.nn.softmax(e_logits, axis=-1), TOP_K)
    gate = g_p * top_p / jnp.sum(top_p, axis=-1, keepdims=True)
    eid = (g_idx[:, None] * EXPERTS_PER_GROUP + top_i).reshape(-1).astype(jnp.int32)
    tok = jnp.repeat(jnp.arange(N, dtype=jnp.int32), TOP_K)
    wgt = gate.reshape(-1)
    order = jnp.argsort(eid)
    eid_s, tok_s, wgt_s = eid[order], tok[order], wgt[order]
    counts = jnp.bincount(eid, length=N_EXPERTS)
    padded = (counts + MOE_BLOCK - 1) // MOE_BLOCK * MOE_BLOCK
    start = jnp.cumsum(counts) - counts
    pend = jnp.cumsum(padded)
    pstart = pend - padded
    dest = pstart[eid_s] + jnp.arange(N * TOP_K, dtype=jnp.int32) - start[eid_s]
    n_rows = -(-(N * TOP_K) // MOE_BLOCK) * MOE_BLOCK + N_EXPERTS * MOE_BLOCK
    n_blocks = n_rows // MOE_BLOCK
    row_tok = jnp.full((n_rows,), N, dtype=jnp.int32).at[dest].set(tok_s)
    row_w = jnp.zeros((n_rows,), F32).at[dest].set(wgt_s)
    block_e = jnp.minimum(jnp.searchsorted(pend, jnp.arange(n_blocks) * MOE_BLOCK, side='right'),
                          N_EXPERTS - 1)
    xs = jnp.concatenate([x, jnp.zeros((1, D), x.dtype)], axis=0)[row_tok].reshape(n_blocks, MOE_BLOCK, D)

    def expert_block(args):
        xb, e = args
        return (jax.nn.silu(xb @ w1[e]) * (xb @ w3[e])) @ w2[e]

    ys = lax.map(expert_block, (xs, block_e)).reshape(n_rows, D)
    out = jnp.zeros((N + 1, D), F32).at[row_tok].add(ys.astype(F32) * row_w[:, None])[:N]
    return out.astype(h.dtype).reshape(B, T, D)

def _mixer(n, past, prm, lam_init):
    B, T, _ = n.shape
    P = 0 if past is None else past[0].shape[1]
    qpos = P + jnp.arange(T)
    kpos = jnp.arange(P + T)
    proj = n @ prm['w_in']
    fq, fk, fv, ff, dq, dk, dv = jnp.split(proj, SPLITS, axis=-1)
    fq = fq.reshape(B, T, FOX_HEADS, HEAD_DIM)
    fk = fk.reshape(B, T, FOX_HEADS, HEAD_DIM)
    fv = fv.reshape(B, T, FOX_HEADS, HEAD_DIM)
    logf = jax.nn.log_sigmoid(ff.astype(F32) + prm['b_forget'].astype(F32))
    dq = _partial_rope(dq.reshape(B, T, DIFF_HEADS, 2, HEAD_DIM), qpos)
    dk = _partial_rope(dk.reshape(B, T, DIFF_HEADS, 2, HEAD_DIM), qpos)
    dv = dv.reshape(B, T, DIFF_HEADS, DIFF_V_DIM)
    new = (fk, fv, logf, dk, dv)
    if past is None:
        a_fk, a_fv, a_logf, a_dk, a_dv = fk, fv, logf, dk, dv
    else:
        a_fk = jnp.concatenate([past[0], fk], axis=1)
        a_fv = jnp.concatenate([past[1], fv], axis=1)
        a_logf = jnp.concatenate([past[2].astype(F32), logf], axis=1)
        a_dk = jnp.concatenate([past[3], dk], axis=1)
        a_dv = jnp.concatenate([past[4], dv], axis=1)
    c = jnp.cumsum(a_logf, axis=1)
    fox_o = _fox_attention(fq, a_fk, a_fv, c[:, P:], c, qpos, kpos)
    lam = (jnp.exp(jnp.sum(prm['lam_q1'].astype(F32) * prm['lam_k1'].astype(F32)))
           - jnp.exp(jnp.sum(prm['lam_q2'].astype(F32) * prm['lam_k2'].astype(F32))) + lam_init)
    diff_o = _diff_attention(dq, a_dk, a_dv, lam, qpos, kpos)
    diff_o = _rmsnorm(diff_o, prm['g_diff']) * (1.0 - lam_init)
    mix = jnp.concatenate([fox_o.reshape(B, T, FOX_W), diff_o.reshape(B, T, DIFF_V_W)], axis=-1)
    return mix @ prm['w_o'], new

def _layer(x, past, mem_k, mem_v, prm, lam_init):
    B, T, D = x.shape
    a, new = _mixer(_rmsnorm(x, prm['g_mix']), past, prm, lam_init)
    h = x + a
    q = (_rmsnorm(h, prm['g_mem_q']) @ prm['w_mq']).reshape(B, T, MEM_HEADS, MEM_HEAD_DIM)
    h = h + _mem_attention(q, mem_k, mem_v).reshape(B, T, D) @ prm['w_mo']
    h = h + _hier_moe(_rmsnorm(h, prm['g_ffn']), prm['w_group'], prm['b_group'], prm['w_erouter'],
                      prm['b_erouter'], prm['w1'], prm['w3'], prm['w2'])
    return h, new

def setup_inputs(seed: int = 0) -> dict:
    key = jax.random.key(seed)
    ks = iter(jax.random.split(key, 48))

    def nrm(shape, scale):
        return scale * jax.random.normal(next(ks), shape, jnp.float32)

    L, D = DEPTH, D_MODEL
    return {
        'x_prompt': nrm((BATCH, SEQ, D), 1.0),
        'x_sample': nrm((DEC_BATCH, DEC_SEQ, D), 1.0),
        'cache_fox_k': nrm((L, DEC_BATCH, PAST_LEN, FOX_HEADS, HEAD_DIM), 1.0),
        'cache_fox_v': nrm((L, DEC_BATCH, PAST_LEN, FOX_HEADS, HEAD_DIM), 1.0),
        'cache_fox_logf': jax.nn.log_sigmoid(FORGET_BIAS_INIT + nrm((L, DEC_BATCH, PAST_LEN, FOX_HEADS), 1.0)),
        'cache_diff_k': nrm((L, DEC_BATCH, PAST_LEN, DIFF_HEADS, 2, HEAD_DIM), 1.0),
        'cache_diff_v': nrm((L, DEC_BATCH, PAST_LEN, DIFF_HEADS, DIFF_V_DIM), 1.0),
        'cache_mem_k': nrm((L, DEC_BATCH, MEM_LEN, MEM_HEADS, MEM_HEAD_DIM), 1.0),
        'cache_mem_v': nrm((L, DEC_BATCH, MEM_LEN, MEM_HEADS, MEM_HEAD_DIM), 1.0),
        'mem_prompt': nrm((BATCH, MEM_LEN, D), 1.0),
        'g_mix': 1.0 + nrm((L, D), 0.02),
        'w_in': nrm((L, D, IN_W), D ** -0.5),
        'b_forget': FORGET_BIAS_INIT + nrm((L, FOX_HEADS), 0.5),
        'lam_q1': nrm((L, HEAD_DIM), 0.1),
        'lam_k1': nrm((L, HEAD_DIM), 0.1),
        'lam_q2': nrm((L, HEAD_DIM), 0.1),
        'lam_k2': nrm((L, HEAD_DIM), 0.1),
        'g_diff': 1.0 + nrm((L, DIFF_V_DIM), 0.02),
        'w_o': nrm((L, MIX_W, D), MIX_W ** -0.5),
        'g_mem_q': 1.0 + nrm((L, D), 0.02),
        'g_mem_kv': 1.0 + nrm((L, D), 0.02),
        'w_mq': nrm((L, D, D), D ** -0.5),
        'w_mk': nrm((L, D, D), D ** -0.5),
        'w_mv': nrm((L, D, D), D ** -0.5),
        'w_mo': nrm((L, D, D), D ** -0.5),
        'g_ffn': 1.0 + nrm((L, D), 0.02),
        'w_group': nrm((L, D, N_GROUPS), D ** -0.5),
        'b_group': nrm((L, N_GROUPS), 0.01),
        'w_erouter': nrm((L, D, N_EXPERTS), D ** -0.5),
        'b_erouter': nrm((L, N_EXPERTS), 0.01),
        'w1': nrm((L, N_EXPERTS, D, D_EXPERT), D ** -0.5),
        'w3': nrm((L, N_EXPERTS, D, D_EXPERT), D ** -0.5),
        'w2': nrm((L, N_EXPERTS, D_EXPERT, D), D_EXPERT ** -0.5),
        'g_final': 1.0 + nrm((D,), 0.02),
    }

def reference(x_prompt, x_sample, cache_fox_k, cache_fox_v, cache_fox_logf, cache_diff_k, cache_diff_v,
              cache_mem_k, cache_mem_v, mem_prompt, g_mix, w_in, b_forget, lam_q1, lam_k1, lam_q2, lam_k2,
              g_diff, w_o, g_mem_q, g_mem_kv, w_mq, w_mk, w_mv, w_mo, g_ffn, w_group, b_group,
              w_erouter, b_erouter, w1, w3, w2, g_final):
    hp, hs = x_prompt, x_sample
    new_p, new_s, mem_p = [], [], []
    for l in range(DEPTH):
        prm = {
            'g_mix': g_mix[l], 'w_in': w_in[l], 'b_forget': b_forget[l],
            'lam_q1': lam_q1[l], 'lam_k1': lam_k1[l], 'lam_q2': lam_q2[l], 'lam_k2': lam_k2[l],
            'g_diff': g_diff[l], 'w_o': w_o[l], 'g_mem_q': g_mem_q[l], 'w_mq': w_mq[l], 'w_mo': w_mo[l],
            'g_ffn': g_ffn[l], 'w_group': w_group[l], 'b_group': b_group[l],
            'w_erouter': w_erouter[l], 'b_erouter': b_erouter[l], 'w1': w1[l], 'w3': w3[l], 'w2': w2[l],
        }
        lam_init = 0.8 - 0.6 * math.exp(-0.3 * l)
        mk, mv = _memory_kv(mem_prompt, g_mem_kv[l], w_mk[l], w_mv[l])
        hp, np_new = _layer(hp, None, mk, mv, prm, lam_init)
        past = (cache_fox_k[l], cache_fox_v[l], cache_fox_logf[l], cache_diff_k[l], cache_diff_v[l])
        hs, ns_new = _layer(hs, past, cache_mem_k[l], cache_mem_v[l], prm, lam_init)
        new_p.append(np_new)
        new_s.append(ns_new)
        mem_p.append((mk, mv))
    y_prompt = _rmsnorm(hp, g_final)
    y_sample = _rmsnorm(hs, g_final)
    p_fk = jnp.stack([e[0] for e in new_p])
    p_fv = jnp.stack([e[1] for e in new_p])
    p_logf = jnp.stack([e[2] for e in new_p])
    p_dk = jnp.stack([e[3] for e in new_p])
    p_dv = jnp.stack([e[4] for e in new_p])
    p_mk = jnp.stack([e[0] for e in mem_p])
    p_mv = jnp.stack([e[1] for e in mem_p])
    s_fk = jnp.stack([e[0] for e in new_s])
    s_fv = jnp.stack([e[1] for e in new_s])
    s_logf = jnp.stack([e[2] for e in new_s])
    s_dk = jnp.stack([e[3] for e in new_s])
    s_dv = jnp.stack([e[4] for e in new_s])
    return (y_prompt, y_sample, p_fk, p_fv, p_logf, p_dk, p_dv, p_mk, p_mv, s_fk, s_fv, s_logf, s_dk, s_dv)


_drawn_inputs = setup_inputs


def setup_inputs(seed=0):
    import zlib

    import numpy as np

    out = dict(_drawn_inputs(seed))
    spreads = {}
    factors = {'g_diff': 2.888,
     'g_mem_q': 7.979,
     'g_mem_kv': 2.948,
     'b_group': 19.427,
     'b_erouter': 5.201,
     'g_final': 8.081,
     'g_ffn': 5.203}
    for name, (base, spread) in spreads.items():
        noise = np.random.default_rng([zlib.crc32(name.encode()), seed]).standard_normal(out[name].shape)
        drawn = base * np.exp(spread * noise) if base else spread * noise
        out[name] = __import__('jax').numpy.asarray(drawn.astype(out[name].dtype))
    for name, factor in factors.items():
        out[name] = (out[name] * factor).astype(out[name].dtype)
    return out
```

```python
import concourse.bass as bass
import concourse.mybir as mybir
from contextlib import ExitStack

F32 = mybir.dt.float32
BF16 = mybir.dt.bfloat16
I32 = mybir.dt.int32
U32 = mybir.dt.uint32
ALU = mybir.AluOpType
ACT = mybir.ActivationFunctionType
AX = mybir.AxisListType.X

P = 128
D = 1024
KT = D // P
SEQ = 512
NB = 8
TD = 16
PAST = 256
T = 5
TP = 4
NTOK = T * P
FH = 8
HD = 64
DH = 4
MEM = 256
MH = 4
MD = 256
NG = 4
EPG = 8
NE = NG * EPG
DE = 512
ET = DE // P
CAP = 64
PAIRS = NE // 2
MAIN = NE * CAP
OVB = 2 * NTOK // CAP
NSLOT = MAIN + OVB * CAP
SCOLS = NSLOT // P
IN_W = 3 * 512 + FH + 3 * 512
EPS = 1e-6
LAM_INIT = 0.8 - 0.6
KS = PAST + TD
SC = HD ** -0.5
MSC = MD ** -0.5
SLOTS = 6
W_FOX, C_FOX, W_DIFF, C_DIFF, W_O, W_MK, W_MV, W_MQ, C_MEM, W_MO, W_MOE = 0, 3, 7, 10, 14, 16, 18, 20, 22, 30, 32


def build(nc, a):
    top = ExitStack()
    names = [0]

    def sb(ctx, name, shape, dt=F32):
        return ctx.enter_context(nc.sbuf_tensor(name, shape, dt))

    finished = []

    def sem(ctx, name):
        s = nc.alloc_semaphore(name=name)
        if ctx is not top:
            ctx.callback(finished.append, s)
        return s

    def recycle_semaphores():
        nc.clear_and_free_semaphores(finished)
        finished.clear()
        nc.all_engine_barrier()

    with top:
        ps = [top.enter_context(nc.psum_tensor(f"bank{i}", [P, 512], F32)) for i in range(8)]
        ring = sb(top, "ring", [P, SLOTS, 4096])
        ident = sb(top, "ident", [P, P])
        gcol = sb(top, "gcol", [P, 4, KT])
        landed = [sem(top, f"landed{i}") for i in range(SLOTS)]
        used = sem(top, "chunks_used")
        stored = sem(top, "stored")
        stored_v = sem(top, "stored_values")
        ns = [0]

        def store(eng, dst, src):
            ns[0] += 16
            eng.dma_start(dst, src).then_inc(stored, 16)

        w_in, w_o, w_mk, w_mv, w_mq, w_mo = (a[n][0] for n in ("w_in", "w_o", "w_mk", "w_mv", "w_mq", "w_mo"))

        def cols(w, c0):
            return w[:, c0:c0 + 512].rearrange("(k p) n -> p k n", p=P)

        fox_w = 3 * 512 + FH
        heads_of = {"cache_fox_k": "h d", "cache_fox_v": "h d", "cache_diff_k": "h c d", "cache_diff_v": "h d",
                    "cache_mem_k": "h d", "cache_mem_v": "h d"}

        def cache(name):
            f = heads_of[name]
            return a[name][0].rearrange(f"b t {f} -> b t ({f})")

        plain = {W_FOX + i: cols(w_in, 512 * i) for i in range(3)}
        plain |= {W_DIFF + i: cols(w_in, fox_w + 512 * i) for i in range(3)}
        for c, w in ((W_O, w_o), (W_MK, w_mk), (W_MV, w_mv), (W_MQ, w_mq), (W_MO, w_mo)):
            plain |= {c + i: cols(w, 512 * i) for i in range(2)}

        def slot(c):
            return ring[:, c % SLOTS, :].rearrange("p (k n) -> p k n", n=512)

        def slot2(c):
            return ring[:, c % SLOTS, :].rearrange("p (k n) -> p k n", n=1024)

        def parts(c):
            if c in plain:
                return [(slot(c), plain[c])]
            if c >= W_MOE:
                j = (c - W_MOE) % 6
                e = 2 * ((c - W_MOE) // 6) + j % 2
                name = "w1" if j < 2 else "w3" if j < 4 else "w2"
                return [(slot(c) if j < 4 else slot2(c), a[name][0, e].rearrange("(k p) n -> p k n", p=P))]
            if c >= C_MEM:
                b = c - C_MEM
                return [(slot2(c)[:, 2 * i:2 * i + 2, :], cache(n)[b].rearrange("(k p) f -> p k f", p=P))
                        for i, n in enumerate(("cache_mem_k", "cache_mem_v"))]
            kind, c0 = ("fox", C_FOX) if c < W_DIFF else ("diff", C_DIFF)
            out = []
            for s in range(2):
                for i, n in enumerate((f"cache_{kind}_k", f"cache_{kind}_v")):
                    out.append((slot(c)[:, 4 * s + 2 * i:4 * s + 2 * i + 2, :],
                                cache(n)[2 * (c - c0) + s].rearrange("(k p) f -> p k f", p=P)))
            return out

        landed_by = [0] * (W_MOE + SLOTS)
        for c in range(W_MOE + SLOTS):
            landed_by[c] = (landed_by[c - SLOTS] if c >= SLOTS else 0) + 16 * len(parts(c))

        def load_chunks(sp, c0, c1):
            for c in range(c0, c1):
                if c >= SLOTS:
                    sp.wait_ge(used, c - SLOTS + 1)
                for dst, src in parts(c):
                    sp.dma_start(dst, src).then_inc(landed[c % SLOTS], 16)

        def wait_chunk(pe, c):
            pe.wait_ge(landed[c % SLOTS], landed_by[c])

        def chain(eng, s):
            n = [0]

            def link(ins):
                n[0] += 1
                ins.then_inc(s, 1)
                eng.wait_ge(s, n[0])
            return link

        g_names = ("g_mix", "g_mem_q", "g_mem_kv", "g_ffn")

        def norm_block(tag, src, nt, gi, dst_t, load=None, extra_dram=None, first=False, chunk_range=None, prep=None):
            with ExitStack() as c:
                sq = sb(c, tag + "sq", [P, D])
                ss = sb(c, tag + "ss", [P, nt])
                rs = sb(c, tag + "rs", [P, nt])
                xs = sb(c, tag + "xs", [P, 2, D])
                ld, ssd, msd, rtd, rsd, xsd, trd, evd, ch = (
                    sem(c, tag + n) for n in ("ld", "ssd", "msd", "rtd", "rsd", "xsd", "trd", "evd", "ch"))
                wr = [sem(c, f"{tag}wr{i}") for i in range(2)] if extra_dram is not None else None
                lt = [sem(c, f"{tag}lt{t}") for t in range(nt)] if load is not None else None
                with nc.Block() as block:
                    @block.sync
                    def _(sp):
                        if load is not None:
                            for t in range(nt):
                                sp.dma_start(src[:, t, :], load(t)).then_inc(lt[t], 16)
                        if first:
                            sp.dma_start(ident[:, :], a["c_ident"]).then_inc(ld, 16)
                            for i, n in enumerate(g_names):
                                with nc.allow_non_contiguous_dma("small gain vectors"):
                                    sp.dma_start(gcol[:, i, :], a[n][0].rearrange("(k p) -> p k", p=P)).then_inc(ld, 16)
                        if chunk_range:
                            load_chunks(sp, *chunk_range)
                        if extra_dram is not None:
                            for t in range(nt):
                                sp.wait_ge(xsd, t + 1)
                                sp.dma_start(extra_dram[t * P:(t + 1) * P, :], xs[:, t % 2, :]).then_inc(wr[t % 2], 16)
                            for i in range(2):
                                sp.wait_ge(wr[i], 16 * ((nt + 1 - i) // 2))

                    @block.scalar
                    def _(act):
                        for t in range(nt):
                            if load is not None:
                                act.wait_ge(lt[t], 16)
                            if t:
                                act.wait_ge(ssd, t)
                            nc.scalar.activation(sq[:, :], src[:, t, :], ACT.Square,
                                                 accum_out=ss[:, t:t + 1]).then_inc(ssd, 1)
                        act.wait_ge(msd, 1)
                        nc.scalar.activation(rs[:, :], ss[:, :], ACT.Sqrt).then_inc(rtd, 1)
                        act.wait_ge(rsd, 1)
                        for t in range(nt):
                            if t >= 2:
                                act.wait_ge(trd, t - 1)
                                if extra_dram is not None:
                                    act.wait_ge(wr[t % 2], 16 * (t // 2))
                            nc.scalar.activation(xs[:, t % 2, :], src[:, t, :], ACT.Copy,
                                                 scale=rs[:, t:t + 1]).then_inc(xsd, 1)

                    @block.vector
                    def _(dve):
                        dve.wait_ge(ssd, nt)
                        nc.vector.tensor_scalar(ss[:, :], ss[:, :], 1.0 / D, EPS, ALU.mult, ALU.add).then_inc(msd, 1)
                        dve.wait_ge(rtd, 1)
                        nc.vector.reciprocal(rs[:, :], rs[:, :]).then_inc(rsd, 1)
                        if first:
                            dve.wait_ge(ld, 80)
                        for t in range(nt):
                            dve.wait_ge(trd, t + 1)
                            for h in range(2):
                                ins = nc.vector.tensor_tensor(
                                    dst_t[:, 4 * h:4 * h + 4, t * P:(t + 1) * P],
                                    ps[2 * (t % 2) + h][:, :].rearrange("p (k n) -> p k n", k=4),
                                    gcol[:, gi, 4 * h:4 * h + 4].unsqueeze(2).broadcast_to([P, 4, P]), ALU.mult)
                            ins.then_inc(evd, 1)

                    @block.tensor
                    def _(pe):
                        if first:
                            pe.wait_ge(ld, 80)
                        for t in range(nt):
                            pe.wait_ge(xsd, t + 1)
                            if t >= 2:
                                pe.wait_ge(evd, t - 1)
                            for k in range(KT):
                                ins = nc.tensor.transpose(ps[2 * (t % 2) + k // 4][:, (k % 4) * P:(k % 4 + 1) * P],
                                                          xs[:, t % 2, k * P:(k + 1) * P], ident[:, :])
                            ins.then_inc(trd, 1)

        def project_block(tag, nT, qT, kT, vN, c0, chunk_range, fox, k_out, v_out):
            with ExitStack() as c:
                st = sb(c, tag + "st", [P, 4, 512])
                rt = None if fox else sb(c, tag + "rt", [P, 2, 2, 8, 16])
                cs = None if fox else sb(c, tag + "cs", [P, 2, T, 16])
                mmd, eva, evd, trd, rop, csd, ch = (sem(c, tag + n) for n in ("mmd", "eva", "evd", "trd", "rop", "csd", "ch"))
                kst = [sem(c, f"{tag}kst{i}") for i in range(4)]
                groups = []
                if fox:
                    groups += [("qT", j) for j in range(4)]
                nat = ([] if fox else [("q", t) for t in range(T)]) + [("k", t) for t in range(T)]
                for i, (w, t) in enumerate(nat):
                    groups.append(("mm", w, t, i))
                    if i >= 2:
                        groups.append(("tr",) + nat[i - 2] + (i - 2,))
                vs = [("mm", "v", t, None) for t in range(T)]
                groups += [vs[0], ("tr",) + nat[-2] + (len(nat) - 2,), vs[1], ("tr",) + nat[-1] + (len(nat) - 1,)] + vs[2:]
                chunk_of = {"q": c0, "k": c0 + 1, "v": c0 + 2}
                on_act = [g[0] == "mm" and g[1] != "v" or (g[0] == "tr" and fox and i % 2 == 0) for i, g in enumerate(groups)]
                nact = [sum(on_act[:i + 1]) for i in range(len(groups))]
                ndve = [i + 1 - nact[i] for i in range(len(groups))]
                where = {g[3]: i for i, g in enumerate(groups) if g[0] == "mm" and g[3] is not None}
                trw = {g[3]: i for i, g in enumerate(groups) if g[0] == "tr"}

                def drained(eng, g):
                    if on_act[g]:
                        eng.wait_ge(eva, nact[g])
                    else:
                        eng.wait_ge(evd, ndve[g])

                with nc.Block() as block:
                    @block.sync
                    def _(sp):
                        if not fox:
                            sp.dma_start(cs[:, 0, :, :], a["c_cos"]).then_inc(csd, 16)
                            sp.dma_start(cs[:, 1, :, :], a["c_sin"]).then_inc(csd, 16)
                        load_chunks(sp, *chunk_range)

                    @block.gpsimd
                    def _(pool):
                        for i, (w, t) in enumerate(nat):
                            if w == "k":
                                if fox:
                                    drained(pool, where[i])
                                else:
                                    pool.wait_ge(rop, i + 1)
                                pool.dma_start(k_out(t), st[:, i % 4, :]).then_inc(kst[i % 4], 16)
                        for i, g in enumerate(groups):
                            if g[0] == "mm" and g[1] == "v":
                                drained(pool, i)
                                pool.dma_start(v_out(g[2]), vN[:, g[2], :]).then_inc(stored_v, 16)
                        pool.wait_ge(stored_v, 16 * T * (1 if fox else 2))
                        for i in range(4):
                            n = sum(1 for j, (w, t) in enumerate(nat) if w == "k" and j % 4 == i)
                            pool.wait_ge(kst[i], 16 * n)

                    @block.tensor
                    def _(pe):
                        for g, grp in enumerate(groups):
                            if g >= 4:
                                drained(pe, g - 4)
                            b0, b1 = ps[2 * (g % 4)], ps[2 * (g % 4) + 1]
                            if grp[0] == "qT":
                                j = grp[1]
                                if j == 0:
                                    wait_chunk(pe, c0)
                                w = slot(c0)
                                for k in range(KT):
                                    nc.tensor.matmul(b0[:, :], w[:, k, j * P:(j + 1) * P], nT[:, k, 0:SEQ],
                                                     start=k == 0, stop=k == KT - 1)
                                    ins = nc.tensor.matmul(b1[:, 0:P], w[:, k, j * P:(j + 1) * P], nT[:, k, SEQ:NTOK],
                                                           start=k == 0, stop=k == KT - 1)
                                ins.then_inc(mmd, 1)
                                if j == 3:
                                    pe.wait_ge(mmd, g + 1)
                                    pe.sem_inc(used, 1)
                            elif grp[0] == "mm":
                                _, w, t, _ = grp
                                if t == 0:
                                    wait_chunk(pe, chunk_of[w])
                                wt = slot(chunk_of[w])
                                for k in range(KT):
                                    ins = nc.tensor.matmul(b0[:, :], nT[:, k, t * P:(t + 1) * P], wt[:, k, :],
                                                           start=k == 0, stop=k == KT - 1)
                                ins.then_inc(mmd, 1)
                                if t == T - 1:
                                    pe.wait_ge(mmd, g + 1)
                                    pe.sem_inc(used, 1)
                            else:
                                _, w, t, i = grp
                                if fox:
                                    drained(pe, where[i])
                                else:
                                    pe.wait_ge(rop, i + 1)
                                for j in range(4):
                                    ins = nc.tensor.transpose(b0[:, j * P:(j + 1) * P], st[:, i % 4, j * P:(j + 1) * P],
                                                              ident[:, :])
                                ins.then_inc(mmd, 1)

                    def copy_out(eng, copy, g, grp):
                        eng.wait_ge(mmd, g + 1)
                        b0, b1 = ps[2 * (g % 4)], ps[2 * (g % 4) + 1]
                        if grp[0] == "qT":
                            copy(qT[:, grp[1], 0:SEQ], b0[:, :])
                            return copy(qT[:, grp[1], SEQ:NTOK], b1[:, 0:P])
                        if grp[0] == "mm" and grp[1] == "v":
                            return copy(vN[:, grp[2], :], b0[:, :])
                        if grp[0] == "mm":
                            i = grp[3]
                            if i >= 4:
                                eng.wait_ge(mmd, trw[i - 4] + 1)
                                n = sum(1 for j in range(i - 3) if nat[j][0] == "k" and j % 4 == i % 4)
                                if n:
                                    eng.wait_ge(kst[i % 4], 16 * n)
                            return copy(st[:, i % 4, :], b0[:, :])
                        dst = qT if grp[1] == "q" else kT
                        return copy(dst[:, :, grp[2] * P:(grp[2] + 1) * P], b0[:, :].rearrange("p (j n) -> p j n", j=4))

                    @block.scalar
                    def _(act):
                        for g, grp in enumerate(groups):
                            if on_act[g]:
                                copy_out(act, nc.scalar.copy, g, grp).then_inc(eva, 1)

                    @block.vector
                    def _(dve):
                        link = chain(dve, ch)
                        if not fox:
                            dve.wait_ge(csd, 32)
                        for g, grp in enumerate(groups):
                            if not on_act[g]:
                                copy_out(dve, nc.vector.tensor_copy, g, grp).then_inc(evd, 1)
                            elif not fox:
                                i, t = grp[3], grp[2]
                                drained(dve, g)
                                x = st[:, i % 4, :].rearrange("p (c d) -> p c d", c=8)
                                r = rt[:, i % 2]
                                cosv = cs[:, 0, t, :].unsqueeze(1).broadcast_to([P, 8, 16])
                                sinv = cs[:, 1, t, :].unsqueeze(1).broadcast_to([P, 8, 16])
                                nc.vector.tensor_tensor(r[:, 0], x[:, :, 0:16], cosv, ALU.mult)
                                nc.vector.tensor_tensor(r[:, 1, :, 0:8], x[:, :, 8:16], sinv[:, :, 0:8], ALU.mult)
                                link(nc.vector.tensor_tensor(r[:, 1, :, 8:16], x[:, :, 0:8], sinv[:, :, 8:16], ALU.mult))
                                nc.vector.tensor_tensor(x[:, :, 0:16], r[:, 0], r[:, 1], ALU.add).then_inc(rop, 1)

        def gates_block(nT, RL, RR, CT, L2, bias_l):
            with ExitStack() as c:
                wff = sb(c, "wff", [P, KT, FH])
                bf = sb(c, "bf", [FH, 1])
                z = sb(c, "gz", [FH, NTOK])
                e = sb(c, "ge", [FH, NTOK])
                lf = sb(c, "glf", [FH, NTOK])
                lfN = sb(c, "glfN", [P, T, FH])
                cc = sb(c, "gcc", [FH, 2, SEQ])
                one = sb(c, "gone", [NB * FH, SEQ])
                lc = sb(c, "glc", [P, 2, NB * FH])
                raw = sb(c, "graw", [NB * FH, KS])
                cn = sb(c, "gcn", [NB * FH, TD])
                ld, ldc, ms, mm, zd, ed, fd, cd, ctr, cev, rawd, nw, ch, ach, fin, nd, l2 = (
                    sem(c, "g" + n) for n in ("ld", "ldc", "ms", "mm", "zd", "ed", "fd", "cd", "ctr", "cev", "rawd",
                                              "nw", "ch", "ach", "fin", "nd", "l2"))
                with nc.Block() as block:
                    @block.sync
                    def _(sp):
                        with nc.allow_non_contiguous_dma("narrow gate columns"):
                            sp.dma_start(wff[:, :, :], w_in[:, 1536:1536 + FH].rearrange("(k p) n -> p k n", p=P)).then_inc(ld, 16)
                            sp.dma_start(bf[:, :], a["b_forget"][0].rearrange("(h o) -> h o", o=1)).then_inc(ld, 16)
                            for h in range(2):
                                sp.dma_start(lc[:, h, :].rearrange("p (b f) -> p b f", b=NB),
                                             a["cache_fox_logf"][0, :, h * P:(h + 1) * P, :].rearrange("b p f -> p b f")).then_inc(ldc, 16)
                        sp.dma_start(CT[64:80, :], a["c_tri16"]).then_inc(ldc, 16)
                        sp.dma_start(bias_l[:, :, :], a["c_sel"]).then_inc(ldc, 16)
                        sp.wait_ge(fd, 1)
                        for b in range(NB):
                            sp.dma_start(raw[b * FH:(b + 1) * FH, PAST:KS],
                                         lf[:, SEQ + b * TD:SEQ + (b + 1) * TD]).then_inc(nw, 16)
                        sp.wait_ge(ms, 2)
                        sp.wait_ge(cd, 1)
                        for h in range(FH):
                            p0 = 32 * (h % 4)
                            sp.dma_start(RR[p0:p0 + 1, h // 4, :], cc[h:h + 1, 1, :]).then_inc(fin, 16)
                            sp.dma_start(RL[p0 + 1:p0 + 2, h // 4, :], cc[h:h + 1, 0, :]).then_inc(fin, 16)
                        sp.wait_ge(nd, 1)
                        store(sp, a["p_logf"].rearrange("l b (t p) h -> p (l b t) h", p=P), lfN[:, 0:TP, :])
                        store(sp, a["s_logf"].rearrange("l b q h -> (l b q) h"), lfN[:, TP, :])
                        sp.wait_ge(fin, 16 * 2 * FH)

                    @block.gpsimd
                    def _(pool):
                        nc.gpsimd.memset(RR[:, :, :], 1.0).then_inc(ms, 1)
                        nc.gpsimd.memset(RL[:, :, :], 1.0).then_inc(ms, 1)
                        nc.gpsimd.memset(one[:, :], 1.0).then_inc(ms, 1)

                    @block.tensor
                    def _(pe):
                        pe.wait_ge(ld, 32)
                        for k in range(KT):
                            nc.tensor.matmul(ps[0][0:FH, :], wff[:, k, :], nT[:, k, 0:SEQ], start=k == 0, stop=k == KT - 1)
                            ins = nc.tensor.matmul(ps[1][0:FH, 0:P], wff[:, k, :], nT[:, k, SEQ:NTOK],
                                                   start=k == 0, stop=k == KT - 1)
                        ins.then_inc(mm, 1)
                        pe.wait_ge(ldc, 64)
                        for h in range(2):
                            ins = nc.tensor.transpose(ps[2][0:64, h * P:(h + 1) * P], lc[:, h, :], ident[:, :])
                        ins.then_inc(ctr, 1)
                        pe.wait_ge(fd, 1)
                        for t in range(T):
                            ins = nc.tensor.transpose(ps[3][:, t * FH:(t + 1) * FH], lf[:, t * P:(t + 1) * P],
                                                      ident[0:FH, 0:FH])
                        ins.then_inc(mm, 1)

                    @block.scalar
                    def _(act):
                        link = chain(act, ach)
                        act.wait_ge(zd, 1)
                        link(nc.scalar.activation(e[:, :], z[:, :], ACT.Abs))
                        link(nc.scalar.activation(e[:, :], e[:, :], ACT.Exp, scale=-1.0))
                        nc.scalar.activation(e[:, :], e[:, :], ACT.Ln, bias=1.0).then_inc(ed, 1)

                    @block.vector
                    def _(dve):
                        link = chain(dve, ch)
                        dve.wait_ge(mm, 1)
                        dve.wait_ge(ld, 32)
                        nc.vector.tensor_scalar(z[:, 0:SEQ], ps[0][0:FH, :], bf[:, 0:1], None, ALU.add)
                        nc.vector.tensor_scalar(z[:, SEQ:NTOK], ps[1][0:FH, 0:P], bf[:, 0:1], None, ALU.add).then_inc(zd, 1)
                        dve.wait_ge(ctr, 1)
                        nc.vector.tensor_copy(raw[:, 0:PAST], ps[2][0:64, 0:PAST]).then_inc(rawd, 1)
                        dve.wait_ge(ed, 1)
                        nc.vector.scalar_tensor_tensor(out=lf[:, :], in0=z[:, :], scalar=0.0, in1=e[:, :],
                                                       op0=ALU.min, op1=ALU.subtract).then_inc(fd, 1)
                        dve.wait_ge(fd, 1)
                        dve.wait_ge(ms, 3)
                        link(nc.vector.tensor_tensor_scan(cc[:, 0, :], one[0:FH, :], lf[:, 0:SEQ], 0.0, ALU.mult, ALU.add))
                        link(nc.vector.tensor_scalar(cc[:, 1, :], cc[:, 0, :], -1.0 / SC, None, ALU.mult))
                        nc.vector.tensor_scalar(cc[:, 0, :], cc[:, 0, :], 1.0 / SC, None, ALU.mult).then_inc(cd, 1)
                        dve.wait_ge(nw, 16 * NB)
                        dve.wait_ge(rawd, 1)
                        link(nc.vector.tensor_tensor_scan(CT[0:64, :], one[:, 0:KS], raw[:, :], 0.0, ALU.mult, ALU.add))
                        link(nc.vector.tensor_scalar(cn[:, :], CT[0:64, PAST:KS], -1.0, None, ALU.mult))
                        dve.wait_ge(ldc, 64)
                        for b in range(NB):
                            ins = nc.vector.tensor_tensor(
                                L2[:, b, :].rearrange("p (h q) -> p h q", h=FH),
                                bias_l[0:64, b, :].rearrange("p (h q) -> p h q", h=FH),
                                cn[:, :].unsqueeze(1).broadcast_to([64, FH, TD]), ALU.mult)
                        ins.then_inc(l2, 1)
                        dve.wait_ge(mm, 2)
                        nc.vector.tensor_copy(lfN[:, :, :], ps[3][:, 0:T * FH].rearrange("p (t h) -> p t h", t=T)).then_inc(nd, 1)
                        dve.wait_ge(l2, 1)

        def prompt_attention(tag, kind, qT, kT, vN, outN, outT, RL=None, RR=None, lamcol=None, chunk_range=None, blank=None):
            fox, diff, mem = kind == "fox", kind == "diff", kind == "mem"
            comps = 2 if diff else 1
            heads = FH if fox else DH
            width = {"fox": 64, "diff": 128, "mem": 256}[kind]
            scale = MSC if mem else SC
            units = [(qt, h, cc) for qt in range(TP) for h in range(heads) for cc in range(comps)]
            pairs = [(qt, h) for qt in range(TP) for h in range(heads)]
            nk = (lambda qt: 2) if mem else (lambda qt: qt + 1)
            with ExitStack() as c:
                mask = None if mem else sb(c, tag + "mask", [P, P])
                pb = sb(c, tag + "p", [P, 4, 512])
                pt = sb(c, tag + "pt", [P, 2, 512])
                mx = sb(c, tag + "mx", [P, 4])
                rs = sb(c, tag + "rs", [P, len(units)])
                rr = sb(c, tag + "rr", [P, len(units)])
                dg = sb(c, tag + "dg", [P, 4, P]) if diff else None
                on = None if diff else sb(c, tag + "on", [P, heads * width])
                if blank is not None:
                    zero = sb(c, tag + "zero", [P, D])
                    bz, bd = sem(c, tag + "bz"), sem(c, tag + "bd")
                md, sc, mxd, exd, trp, cpd, pvd, rrd, ond, otd, oed, ch, dgd = (
                    sem(c, tag + n) for n in ("md", "sc", "mxd", "exd", "trp", "cpd", "pvd", "rrd", "ond", "otd",
                                              "oed", "ch", "dgd"))

                def obank(qt, h):
                    if mem:
                        return ps[4 + h // 2], (h % 2) * 256
                    return ps[4 + qt % 2], h * width

                with nc.Block() as block:
                    @block.sync
                    def _(sp):
                        if not mem:
                            sp.dma_start(mask[:, :], a["c_causal" if fox else "c_chunk"]).then_inc(md, 16)
                        if chunk_range:
                            load_chunks(sp, *chunk_range)
                        if blank is not None:
                            sp.wait_ge(bz, 1)
                            for i in range(blank.shape[0] // P):
                                sp.dma_start(blank[i * P:(i + 1) * P, :], zero[:, :]).then_inc(bd, 16)
                            sp.wait_ge(bd, 16 * (blank.shape[0] // P))

                    if blank is not None:
                        @block.gpsimd
                        def _(pool):
                            nc.gpsimd.memset(zero[:, :], 0.0).then_inc(bz, 1)

                    @block.tensor
                    def _(pe):
                        def scores(u):
                            qt, h, cc = units[u]
                            n = nk(qt) * P
                            b = ps[u % 2]
                            if u >= 2:
                                pe.wait_ge(exd, u - 1)
                            if mem:
                                for j in range(2):
                                    ins = nc.tensor.matmul(b[:, 0:n], qT[:, 2 * h + j, qt * P:(qt + 1) * P],
                                                           kT[:, 2 * h + j, :], start=j == 0, stop=j == 1)
                            else:
                                x = h if fox else 2 * h + cc
                                r0, j = 64 * (x % 2), x // 2
                                nc.tensor.matmul(b[:, n - P:n], ident[:, :], mask[:, :], start=True, stop=False,
                                                 skip_group_check=True)
                                ins = nc.tensor.matmul(b[:, 0:n], qT[r0:r0 + 64, j, qt * P:(qt + 1) * P],
                                                       kT[r0:r0 + 64, j, 0:n], start=False, stop=not fox,
                                                       skip_group_check=True)
                                if fox:
                                    p0 = 32 * (h % 4)
                                    ins = nc.tensor.matmul(b[:, 0:n], RL[p0:p0 + 2, h // 4, qt * P:(qt + 1) * P],
                                                           RR[p0:p0 + 2, h // 4, 0:n], start=False, stop=True,
                                                           skip_group_check=True)
                            ins.then_inc(sc, 1)

                        def turn(i):
                            qt, h = pairs[i]
                            if i >= 2:
                                pe.wait_ge(cpd, i - 1)
                            b = ps[2 + i % 2]
                            if diff:
                                pe.wait_ge(dgd, i + 1)
                            else:
                                pe.wait_ge(exd, i + 1)
                            for k in range(nk(qt)):
                                if diff:
                                    for cc in range(2):
                                        s = (2 * i + cc) % 4
                                        ins = nc.tensor.matmul(b[:, k * P:(k + 1) * P], pb[:, s, k * P:(k + 1) * P],
                                                               dg[:, s, :], start=cc == 0, stop=cc == 1)
                                else:
                                    ins = nc.tensor.transpose(b[:, k * P:(k + 1) * P], pb[:, i % 4, k * P:(k + 1) * P],
                                                              ident[:, :])
                            ins.then_inc(trp, 1)

                        def values(i):
                            qt, h = pairs[i]
                            pe.wait_ge(cpd, i + 1)
                            b, o = obank(qt, h)
                            if h == 0 and (mem and qt or qt >= 2):
                                pe.wait_ge(ond, qt if mem else qt - 1)
                            for k in range(nk(qt)):
                                ins = nc.tensor.matmul(b[:, o:o + width], pt[:, i % 2, k * P:(k + 1) * P],
                                                       vN[:, k, h * width:(h + 1) * width], start=k == 0,
                                                       stop=k == nk(qt) - 1)
                            ins.then_inc(pvd, 1)
                            if h == heads - 1 and not diff:
                                finish.append(qt)

                        def out_turn(qt):
                            pe.wait_ge(ond, qt + 1)
                            for j in range(heads * width // P):
                                if j % 4 == 0:
                                    n = max(0, 2 * qt + j // 4 - 1) if mem else qt
                                    if n:
                                        pe.wait_ge(oed, n)
                                ins = nc.tensor.transpose(ps[6 if not mem else 6 + j // 4][:, (j % 4) * P:(j % 4 + 1) * P],
                                                          on[:, j * P:(j + 1) * P], ident[:, :])
                                if j % 4 == 3:
                                    ins.then_inc(otd, 1)

                        finish = []
                        if not mem:
                            pe.wait_ge(md, 16)
                        for u in range(min(comps, len(units))):
                            scores(u)
                        for i in range(len(pairs)):
                            for u in range((i + 1) * comps, min((i + 2) * comps, len(units))):
                                scores(u)
                            turn(i)
                            if i:
                                values(i - 1)
                            if len(finish) and i % heads == 2:
                                out_turn(finish.pop(0))
                        values(len(pairs) - 1)
                        if finish:
                            out_turn(finish.pop(0))

                    def copy_pt(act, i):
                        qt, h = pairs[i]
                        act.wait_ge(trp, i + 1)
                        if i >= 2:
                            act.wait_ge(pvd, i - 1)
                        nc.scalar.copy(pt[:, i % 2, 0:nk(qt) * P], ps[2 + i % 2][:, 0:nk(qt) * P]).then_inc(cpd, 1)

                    @block.scalar
                    def _(act):
                        for u, (qt, h, cc) in enumerate(units):
                            n = nk(qt) * P
                            act.wait_ge(mxd, u + 1)
                            if u >= 4:
                                act.wait_ge(trp, (u - 4) // comps + 1)
                            nc.scalar.activation(pb[:, u % 4, 0:n], ps[u % 2][:, 0:n], ACT.Exp, bias=mx[:, u % 4:u % 4 + 1],
                                                 scale=scale, accum_out=rs[:, u:u + 1]).then_inc(exd, 1)
                            if u % comps == comps - 1 and u // comps >= 1:
                                copy_pt(act, u // comps - 1)
                        copy_pt(act, len(pairs) - 1)

                    def after_exp(dve, link, u):
                        dve.wait_ge(exd, u + 1)
                        link(nc.vector.reciprocal(rr[:, u:u + 1], rs[:, u:u + 1]))
                        if diff:
                            if u >= 4:
                                dve.wait_ge(trp, (u - 4) // 2 + 1)
                            if u % 2:
                                link(nc.vector.tensor_tensor(rr[:, u:u + 1], rr[:, u:u + 1], lamcol, ALU.mult))
                            ins = nc.vector.tensor_scalar(dg[:, u % 4, :], ident[:, :], rr[:, u:u + 1], None, ALU.mult)
                            if u % 2:
                                ins.then_inc(dgd, 1)

                    @block.vector
                    def _(dve):
                        link = chain(dve, ch)
                        done = [0]

                        def tile_out(qt):
                            dve.wait_ge(pvd, heads * (qt + 1))
                            if diff:
                                nc.vector.tensor_copy(outN[:, qt, :], ps[4 + qt % 2][:, :]).then_inc(ond, 1)
                                return
                            if qt:
                                dve.wait_ge(otd, (heads * width // 512) * qt)
                            u0 = qt * heads
                            half = 1 if not mem else 2
                            for g in range(half):
                                hh = heads // half
                                ins = nc.vector.tensor_tensor(
                                    on[:, g * 512:(g + 1) * 512].rearrange("p (h d) -> p h d", h=hh),
                                    (ps[4 + qt % 2] if not mem else ps[4 + g])[:, :].rearrange("p (h d) -> p h d", h=hh),
                                    rr[:, u0 + g * hh:u0 + (g + 1) * hh].unsqueeze(2).broadcast_to([P, hh, width]), ALU.mult)
                            ins.then_inc(ond, 1)

                        def tile_turned(qt):
                            for g in range(heads * width // 512):
                                dve.wait_ge(otd, (heads * width // 512) * qt + g + 1)
                                nc.vector.tensor_copy(outT[:, 4 * g:4 * g + 4, qt * P:(qt + 1) * P],
                                                      ps[6 + g][:, :].rearrange("p (j n) -> p j n", j=4)).then_inc(oed, 1)

                        todo = []
                        for u, (qt, h, cc) in enumerate(units):
                            n = nk(qt) * P
                            dve.wait_ge(sc, u + 1)
                            if u >= 4:
                                dve.wait_ge(exd, u - 3)
                            link(nc.vector.reduce_max(mx[:, u % 4:u % 4 + 1], ps[u % 2][:, 0:n], AX))
                            nc.vector.tensor_scalar(mx[:, u % 4:u % 4 + 1], mx[:, u % 4:u % 4 + 1], -scale, None,
                                                    ALU.mult).then_inc(mxd, 1)
                            if u >= comps:
                                after_exp(dve, link, u - comps)
                            if todo and todo[0][0] <= u:
                                t = todo.pop(0)
                                (tile_out if t[1] == 0 else tile_turned)(t[2])
                            if h == heads - 1 and cc == comps - 1:
                                todo += [(u + 2 * comps, 0, qt)] + ([] if diff else [(u + 4 * comps, 1, qt)])
                        for u in range(len(units) - comps, len(units)):
                            after_exp(dve, link, u)
                        for t in todo:
                            (tile_out if t[1] == 0 else tile_turned)(t[2])

        def decode_attention(tag, kind, qT, kT, vN, outN, c0, bias_l=None, CT=None, L2=None, lamcol=None,
                             chunk_range=None):
            fox, diff, mem = kind == "fox", kind == "diff", kind == "mem"
            J = 8 if mem else 4
            W = 256 if mem else 128
            n = PAST if mem else KS
            kb = 2 if mem else 3
            scale = MSC if mem else SC
            with ExitStack() as c:
                qb = sb(c, tag + "qb", [P, J, NB, 32])
                kt = sb(c, tag + "kt", [P, 1 if mem else 2, J, n])
                vn = None if mem else sb(c, tag + "vn", [TD, 2, 512])
                pb = sb(c, tag + "p", [P, 2, n])
                at = sb(c, tag + "at", [P, kb, P])
                ob = sb(c, tag + "o", [P, 2, W])
                mx = sb(c, tag + "mx", [P, NB])
                rs = sb(c, tag + "rs", [P, NB])
                dg = sb(c, tag + "dg", [P, 2, P])
                ones = sb(c, tag + "ones", [64, KS]) if fox else None
                comb = sb(c, tag + "comb", [P, P]) if diff else ident
                sgn = sb(c, tag + "sgn", [P, 3]) if diff else None

                def chunk(b):
                    return c0 + (b if mem else b // 2)

                def cached(b, i):
                    if mem:
                        return slot2(chunk(b))[:, 2 * i:2 * i + 2, :]
                    return slot(chunk(b))[:, 4 * (b % 2) + 2 * i:4 * (b % 2) + 2 * i + 2, :]

                vl = [sem(c, f"{tag}vl{i}") for i in range(2)]
                od = [sem(c, f"{tag}od{i}") for i in range(2)]
                qz, qd, tr, eva, evd, kn, sc, mxd, exd, dgd, atd, acp, pvd, ocd, ch, cl = (
                    sem(c, tag + x) for x in ("qz", "qd", "tr", "eva", "evd", "kn", "sc", "mxd", "exd", "dgd", "atd",
                                              "acp", "pvd", "ocd", "ch", "cl"))
                banks = J // 2
                KS2 = 1 if mem else 2
                with nc.Block() as block:
                    @block.sync
                    def _(sp):
                        if diff:
                            sp.dma_start(comb[:, :], a["c_comb"]).then_inc(cl, 16)
                            sp.dma_start(sgn[:, 0:2], a["c_sgn"]).then_inc(cl, 16)
                        if chunk_range:
                            load_chunks(sp, *chunk_range)

                    def send(pool, b):
                        pool.wait_ge(ocd, b + 1)
                        for h in range(8 if fox else 4):
                            p0 = TD * h if fox else 32 * h
                            o0 = (h % 2) * HD if fox else 0
                            w = HD if fox else W
                            pool.dma_start(outN[b * TD:(b + 1) * TD, h * w:(h + 1) * w],
                                           ob[p0:p0 + TD, b % 2, o0:o0 + w]).then_inc(od[b % 2], 16)

                    @block.gpsimd
                    def _(pool):
                        nc.gpsimd.memset(qb[:, :, :, :], 0.0).then_inc(qz, 1)
                        if not mem:
                            for b in range(2):
                                pool.dma_start(vn[:, b, :], vN[b * TD:(b + 1) * TD, TP, :]).then_inc(vl[b], 16)
                        if fox:
                            nc.gpsimd.memset(ones[:, :], 1.0).then_inc(qz, 1)
                        for b in range(NB):
                            if not mem:
                                if b >= 2:
                                    pool.wait_ge(sc, b - 1)
                                nc.gpsimd.tensor_copy(kt[:, b % 2, :, PAST:KS],
                                                      kT[:, :, SEQ + b * TD:SEQ + (b + 1) * TD]).then_inc(kn, 1)
                            if b:
                                send(pool, b - 1)
                                if b + 1 < NB and not mem:
                                    s = (b + 1) % 2
                                    pool.dma_start(vn[:, s, :], vN[(b + 1) * TD:(b + 2) * TD, TP, :]).then_inc(vl[s], 16)
                        send(pool, NB - 1)
                        for s in range(2):
                            pool.wait_ge(od[s], 16 * (8 if fox else 4) * (NB // 2))

                    @block.tensor
                    def _(pe):
                        def turn_keys(b):
                            s = b % 2
                            wait_chunk(pe, chunk(b))
                            for g in range(banks):
                                if b:
                                    pe.wait_ge(evd if g % 2 == 0 else eva, (banks // 2) * (b - 1) + g // 2 + 1)
                                for jj in range(2):
                                    for k in range(2):
                                        ins = nc.tensor.transpose(
                                            ps[g][:, jj * PAST + k * P:jj * PAST + (k + 1) * P],
                                            cached(b, 0)[:, k, (2 * g + jj) * P:(2 * g + jj + 1) * P], ident[:, :])
                                ins.then_inc(tr, 1)

                        def scores(b):
                            pe.wait_ge(evd, (banks // 2) * (b + 1))
                            pe.wait_ge(eva, (banks // 2) * (b + 1))
                            S = ps[4 + b % 2]
                            if b >= 2:
                                pe.wait_ge(exd, b - 1)
                            if not mem:
                                pe.wait_ge(kn, b + 1)
                            for step in range(2 if mem else 1):
                                for j in range(4):
                                    f = 2 * j + step if mem else j
                                    ins = nc.tensor.matmul(S[32 * j:32 * j + 32, 0:n], qb[:, f, b, :],
                                                           kt[:, b % KS2, f, :], start=step == 0,
                                                           stop=not fox and step == (1 if mem else 0),
                                                           skip_group_check=True)
                            if fox:
                                nc.tensor.matmul(S[:, 0:n], bias_l[:, b, :], CT[:, :], start=False, stop=False,
                                                 skip_group_check=True)
                                ins = nc.tensor.matmul(S[:, 0:n], L2[:, b, :], ones[:, :], start=False, stop=True,
                                                       skip_group_check=True)
                            ins.then_inc(sc, 1)

                        def turn(b):
                            pe.wait_ge(dgd, b + 1)
                            if b:
                                pe.wait_ge(acp, b)
                            for k in range(kb):
                                m = P if k < 2 else TD
                                ins = nc.tensor.matmul(ps[6][0:m, k * P:(k + 1) * P], pb[:, b % 2, k * P:k * P + m],
                                                       dg[:, b % 2, :], start=True, stop=True)
                            ins.then_inc(atd, 1)

                        def values(b):
                            s = b % 2
                            pe.wait_ge(acp, b + 1)
                            if not mem:
                                pe.wait_ge(vl[s], 16 * (b // 2 + 1))
                            if b:
                                pe.wait_ge(ocd, b)
                            for k in range(kb):
                                for j in range(4):
                                    if k < 2:
                                        ins = nc.tensor.matmul(ps[7][32 * j:32 * j + 32, 0:W], at[:, k, 32 * j:32 * j + 32],
                                                               cached(b, 1)[:, k, j * W:(j + 1) * W], start=k == 0,
                                                               stop=k == kb - 1, skip_group_check=True)
                                    else:
                                        ins = nc.tensor.matmul(ps[7][32 * j:32 * j + 32, 0:W],
                                                               at[0:TD, k, 32 * j:32 * j + 32],
                                                               vn[:, s, j * W:(j + 1) * W], start=False, stop=True,
                                                               skip_group_check=True)
                            ins.then_inc(pvd, 1)
                            if mem or b % 2:
                                pe.wait_ge(pvd, b + 1)
                                pe.sem_inc(used, 1)

                        pe.wait_ge(qd, 1)
                        if fox:
                            pe.wait_ge(qz, 2)
                        turn_keys(0)
                        for b in range(NB):
                            scores(b)
                            if b + 1 < NB:
                                turn_keys(b + 1)
                            if b:
                                values(b - 1)
                            turn(b)
                        values(NB - 1)

                    @block.scalar
                    def _(act):
                        def keys(b):
                            for g in range(1, banks, 2):
                                act.wait_ge(tr, banks * b + g + 1)
                                if b >= KS2:
                                    act.wait_ge(sc, b - KS2 + 1)
                                nc.scalar.copy(kt[:, b % KS2, 2 * g:2 * g + 2, 0:PAST],
                                               ps[g][:, :].rearrange("p (j n) -> p j n", j=2)).then_inc(eva, 1)

                        keys(0)
                        for b in range(NB):
                            if b + 1 < NB and not mem:
                                keys(b + 1)
                            act.wait_ge(mxd, b + 1)
                            if b >= 2:
                                act.wait_ge(atd, b - 1)
                            nc.scalar.activation(pb[:, b % 2, :], ps[4 + b % 2][:, 0:n], ACT.Exp, bias=mx[:, b:b + 1],
                                                 scale=scale, accum_out=rs[:, b:b + 1]).then_inc(exd, 1)
                            if b + 1 < NB and mem:
                                keys(b + 1)
                            act.wait_ge(atd, b + 1)
                            if b:
                                act.wait_ge(pvd, b)
                            if not mem:
                                nc.scalar.copy(at[0:TD, 2, :], ps[6][0:TD, 2 * P:3 * P])
                            nc.scalar.copy(at[:, 0:2, :], ps[6][:, 0:2 * P].rearrange("p (k n) -> p k n", k=2)).then_inc(acp, 1)

                    @block.vector
                    def _(dve):
                        link = chain(dve, ch)

                        def keys(b):
                            for g in range(0, banks, 2):
                                dve.wait_ge(tr, banks * b + g + 1)
                                if b >= KS2:
                                    dve.wait_ge(sc, b - KS2 + 1)
                                nc.vector.tensor_copy(kt[:, b % KS2, 2 * g:2 * g + 2, 0:PAST],
                                                      ps[g][:, :].rearrange("p (j n) -> p j n", j=2)).then_inc(evd, 1)

                        def out(b):
                            dve.wait_ge(pvd, b + 1)
                            if b >= 2:
                                dve.wait_ge(od[b % 2], 16 * (8 if fox else 4) * (b // 2))
                            nc.vector.tensor_copy(ob[:, b % 2, :], ps[7][:, 0:W]).then_inc(ocd, 1)

                        dve.wait_ge(qz, 1)
                        q = qT[:, :, SEQ:NTOK].rearrange("p j (b t) -> p j b t", b=NB)
                        if mem:
                            for j in range(J):
                                ins = nc.vector.tensor_copy(qb[:, j, :, 0:TD], q[:, j])
                        else:
                            for j in range(J):
                                nc.vector.tensor_copy(qb[0:64, j, :, 0:TD], q[0:64, j])
                                ins = nc.vector.tensor_copy(qb[64:P, j, :, TD:32], q[64:P, j])
                        ins.then_inc(qd, 1)
                        if diff:
                            dve.wait_ge(cl, 32)
                            link(nc.vector.scalar_tensor_tensor(out=sgn[:, 2:3], in0=sgn[:, 1:2], scalar=lamcol,
                                                                in1=sgn[:, 0:1], op0=ALU.mult, op1=ALU.add))
                        keys(0)
                        for b in range(NB):
                            if b + 1 < NB and not mem:
                                keys(b + 1)
                            dve.wait_ge(sc, b + 1)
                            link(nc.vector.reduce_max(mx[:, b:b + 1], ps[4 + b % 2][:, 0:n], AX))
                            nc.vector.tensor_scalar(mx[:, b:b + 1], mx[:, b:b + 1], -scale, None, ALU.mult).then_inc(mxd, 1)
                            if b + 1 < NB and mem:
                                keys(b + 1)
                            if b:
                                out(b - 1)
                            dve.wait_ge(exd, b + 1)
                            link(nc.vector.reciprocal(rs[:, b:b + 1], rs[:, b:b + 1]))
                            if diff:
                                link(nc.vector.tensor_tensor(rs[:, b:b + 1], rs[:, b:b + 1], sgn[:, 2:3], ALU.mult))
                            if b >= 2:
                                dve.wait_ge(atd, b - 1)
                            nc.vector.tensor_scalar(dg[:, b % 2, :], comb[:, :], rs[:, b:b + 1], None, ALU.mult).then_inc(dgd, 1)
                        out(NB - 1)

        def mix_block(foxN, diffN, mixT, chunk_range):
            with ExitStack() as c:
                sq = sb(c, "msq", [P, T, 512])
                ss = sb(c, "mss", [P, T * DH])
                gd = sb(c, "mgd", [P, P])
                sqd, ssd, sr, rd, nd, tr, ev, ld, ch = (sem(c, "m" + n) for n in ("sqd", "ssd", "sr", "rd", "nd", "tr",
                                                                                  "ev", "ld", "ch"))
                with nc.Block() as block:
                    @block.sync
                    def _(sp):
                        sp.dma_start(gd[:, :], a["g_diff"].partition_broadcast(P).rearrange("p l d -> p (l d)")).then_inc(ld, 16)
                        load_chunks(sp, *chunk_range)
                        sp.wait_ge(ld, 16)

                    @block.scalar
                    def _(act):
                        nc.scalar.activation(sq[:, :, :], diffN[:, :, :], ACT.Square).then_inc(sqd, 1)
                        act.wait_ge(ssd, 1)
                        nc.scalar.activation(ss[:, :], ss[:, :], ACT.Sqrt).then_inc(sr, 1)

                    @block.vector
                    def _(dve):
                        link = chain(dve, ch)
                        dve.wait_ge(sqd, 1)
                        link(nc.vector.reduce_sum(ss[:, :], sq[:, :, :].rearrange("p t (h d) -> p (t h) d", h=DH), AX))
                        nc.vector.tensor_scalar(ss[:, :], ss[:, :], 1.0 / 128, EPS, ALU.mult, ALU.add).then_inc(ssd, 1)
                        dve.wait_ge(ld, 16)
                        link(nc.vector.tensor_scalar(gd[:, :], gd[:, :], 1.0 - LAM_INIT, None, ALU.mult))
                        dve.wait_ge(sr, 1)
                        link(nc.vector.reciprocal(ss[:, :], ss[:, :]))
                        for t in range(T):
                            x = diffN[:, t, :].rearrange("p (h d) -> p h d", h=DH)
                            link(nc.vector.tensor_tensor(x, x, ss[:, t * DH:(t + 1) * DH].unsqueeze(2).broadcast_to([P, DH, P]),
                                                         ALU.mult))
                            nc.vector.tensor_tensor(x, x, gd[:, :].unsqueeze(1).broadcast_to([P, DH, P]), ALU.mult).then_inc(nd, 1)
                        for i in range(T + 1):
                            dve.wait_ge(tr, i + 1)
                            j0, t = (0, TP) if i == 0 else (4, i - 1)
                            nc.vector.tensor_copy(mixT[:, j0:j0 + 4, t * P:(t + 1) * P],
                                                  ps[i % 2][:, :].rearrange("p (j n) -> p j n", j=4)).then_inc(ev, 1)

                    @block.tensor
                    def _(pe):
                        for i in range(T + 1):
                            if i:
                                pe.wait_ge(nd, i)
                            if i >= 2:
                                pe.wait_ge(ev, i - 1)
                            src = foxN if i == 0 else diffN[:, i - 1, :]
                            for j in range(4):
                                ins = nc.tensor.transpose(ps[i % 2][:, j * P:(j + 1) * P], src[:, j * P:(j + 1) * P],
                                                          ident[:, :])
                            ins.then_inc(tr, 1)

        def residual_block(tag, xT, hN, c0, chunk_range, load=None):
            with ExitStack() as c:
                mm, ev = sem(c, tag + "mm"), sem(c, tag + "ev")
                ld = [sem(c, f"{tag}ld{t}") for t in range(T)]
                groups = [(half, t) for half in range(2) for t in range(T)]
                with nc.Block() as block:
                    @block.sync
                    def _(sp):
                        if load is not None:
                            for t in range(T):
                                sp.dma_start(hN[:, t, :], load(t)).then_inc(ld[t], 16)
                        load_chunks(sp, *chunk_range)

                    @block.tensor
                    def _(pe):
                        for g, (half, t) in enumerate(groups):
                            if t == 0:
                                wait_chunk(pe, c0 + half)
                            if g >= 8:
                                pe.wait_ge(ev, g - 7)
                            for k in range(KT):
                                ins = nc.tensor.matmul(ps[g % 8][:, :], xT[:, k, t * P:(t + 1) * P],
                                                       slot(c0 + half)[:, k, :], start=k == 0, stop=k == KT - 1)
                            ins.then_inc(mm, 1)
                            if t == T - 1:
                                pe.wait_ge(mm, g + 1)
                                pe.sem_inc(used, 1)

                    @block.vector
                    def _(dve):
                        for g, (half, t) in enumerate(groups):
                            dve.wait_ge(mm, g + 1)
                            if load is not None:
                                dve.wait_ge(ld[t], 16)
                            h = hN[:, t, half * 512:(half + 1) * 512]
                            nc.vector.tensor_tensor(h, ps[g % 8][:, :], h, ALU.add).then_inc(ev, 1)

        def memory_block(mT, mkT, mvN, chunk_range):
            with ExitStack() as c:
                mkN = sb(c, "mkN", [P, 2, D])
                mm, ev = sem(c, "kmm"), sem(c, "kev")
                out = [a["p_mk"], a["p_mv"]]
                groups = [("mm", m, half, t) for m in range(2) for half in range(2) for t in range(2)]
                groups = groups[:4] + groups[4:] + [("tr", t, half) for t in range(2) for half in range(2)]
                with nc.Block() as block:
                    @block.sync
                    def _(sp):
                        load_chunks(sp, *chunk_range)
                        for m, buf in enumerate((mkN, mvN)):
                            sp.wait_ge(ev, 4 * m + 4)
                            store(sp, out[m].rearrange("l b (k p) h d -> p (l b k) (h d)", p=P), buf[:, :, :])
                        sp.wait_ge(stored, ns[0])

                    @block.tensor
                    def _(pe):
                        for g, grp in enumerate(groups):
                            if g >= 8:
                                pe.wait_ge(ev, g - 7)
                            if grp[0] == "mm":
                                _, m, half, t = grp
                                ch = (W_MK, W_MV)[m] + half
                                if t == 0:
                                    wait_chunk(pe, ch)
                                for k in range(KT):
                                    ins = nc.tensor.matmul(ps[g % 8][:, :], mT[:, k, t * P:(t + 1) * P], slot(ch)[:, k, :],
                                                           start=k == 0, stop=k == KT - 1)
                            else:
                                _, t, half = grp
                                pe.wait_ge(ev, 4)
                                for j in range(4):
                                    o = half * 512 + j * P
                                    ins = nc.tensor.transpose(ps[g % 8][:, j * P:(j + 1) * P], mkN[:, t, o:o + P], ident[:, :])
                            ins.then_inc(mm, 1)
                            if grp[0] == "mm" and grp[3] == 1:
                                pe.wait_ge(mm, g + 1)
                                pe.sem_inc(used, 1)

                    @block.vector
                    def _(dve):
                        for g, grp in enumerate(groups):
                            dve.wait_ge(mm, g + 1)
                            if grp[0] == "mm":
                                _, m, half, t = grp
                                dst, src = (mkN, mvN)[m][:, t, half * 512:(half + 1) * 512], ps[g % 8][:, :]
                            else:
                                _, t, half = grp
                                dst = mkT[:, 4 * half:4 * half + 4, t * P:(t + 1) * P]
                                src = ps[g % 8][:, :].rearrange("p (j n) -> p j n", j=4)
                            nc.vector.tensor_copy(dst, src).then_inc(ev, 1)

        def query_block(nT, qT, chunk_range):
            with ExitStack() as c:
                mm, eva, evd = sem(c, "qmm"), sem(c, "qeva"), sem(c, "qevd")
                with nc.Block() as block:
                    @block.sync
                    def _(sp):
                        load_chunks(sp, *chunk_range)

                    @block.tensor
                    def _(pe):
                        for g in range(KT):
                            if g % 4 == 0:
                                wait_chunk(pe, W_MQ + g // 4)
                            if g >= 4:
                                pe.wait_ge(eva, g - 3)
                                pe.wait_ge(evd, g - 3)
                            w = slot(W_MQ + g // 4)
                            j = g % 4
                            for k in range(KT):
                                nc.tensor.matmul(ps[2 * (g % 4)][:, :], w[:, k, j * P:(j + 1) * P], nT[:, k, 0:SEQ],
                                                 start=k == 0, stop=k == KT - 1)
                                ins = nc.tensor.matmul(ps[2 * (g % 4) + 1][:, 0:P], w[:, k, j * P:(j + 1) * P],
                                                       nT[:, k, SEQ:NTOK], start=k == 0, stop=k == KT - 1)
                            ins.then_inc(mm, 1)
                            if j == 3:
                                pe.wait_ge(mm, g + 1)
                                pe.sem_inc(used, 1)

                    @block.scalar
                    def _(act):
                        for g in range(KT):
                            act.wait_ge(mm, g + 1)
                            nc.scalar.copy(qT[:, g, 0:SEQ], ps[2 * (g % 4)][:, :]).then_inc(eva, 1)

                    @block.vector
                    def _(dve):
                        for g in range(KT):
                            dve.wait_ge(mm, g + 1)
                            nc.vector.tensor_copy(qT[:, g, SEQ:NTOK], ps[2 * (g % 4) + 1][:, 0:P]).then_inc(evd, 1)

        def turn_block(xN, dstT):
            with ExitStack() as c:
                tr, ev = sem(c, "ttr"), sem(c, "tev")
                with nc.Block() as block:
                    @block.tensor
                    def _(pe):
                        for k in range(KT):
                            ins = nc.tensor.transpose(ps[k // 4][:, (k % 4) * P:(k % 4 + 1) * P], xN[:, k * P:(k + 1) * P],
                                                      ident[:, :])
                        ins.then_inc(tr, 1)

                    @block.vector
                    def _(dve):
                        dve.wait_ge(tr, 1)
                        for h in range(2):
                            ins = nc.vector.tensor_copy(dstT[:, 4 * h:4 * h + 4, SEQ:NTOK],
                                                        ps[h][:, :].rearrange("p (k n) -> p k n", k=4))
                        ins.then_inc(ev, 1)
                        dve.wait_ge(ev, 1)

        def lambda_block(lamcol, chunk_range):
            with ExitStack() as c:
                lv = sb(c, "lv", [P, 4, HD])
                pr = sb(c, "lpr", [P, 2, HD])
                s = sb(c, "ls", [P, 2])
                ld, ch, ed, sd = (sem(c, "l" + n) for n in ("ld", "ch", "ed", "sd"))
                with nc.Block() as block:
                    @block.sync
                    def _(sp):
                        for i, n in enumerate(("lam_q1", "lam_q2", "lam_k1", "lam_k2")):
                            sp.dma_start(lv[:, i, :], a[n].partition_broadcast(P).rearrange("p l d -> p (l d)")).then_inc(ld, 16)
                        load_chunks(sp, *chunk_range)

                    @block.vector
                    def _(dve):
                        link = chain(dve, ch)
                        dve.wait_ge(ld, 64)
                        link(nc.vector.tensor_tensor(pr[:, :, :], lv[:, 0:2, :], lv[:, 2:4, :], ALU.mult))
                        nc.vector.reduce_sum(s[:, :], pr[:, :, :], AX).then_inc(sd, 1)
                        dve.wait_ge(ed, 1)
                        link(nc.vector.tensor_tensor(lamcol, s[:, 1:2], s[:, 0:1], ALU.subtract))
                        link(nc.vector.tensor_scalar(lamcol, lamcol, -LAM_INIT, None, ALU.add))

                    @block.scalar
                    def _(act):
                        act.wait_ge(sd, 1)
                        nc.scalar.activation(s[:, :], s[:, :], ACT.Exp).then_inc(ed, 1)

        def route_block(nT, xg, gate, slots, idx, ovn, ove, tab):
            with ExitStack() as c:
                wr = sb(c, "wr", [P, KT, NG + NE])
                br = sb(c, "br", [P, NG + NE])
                cst = sb(c, "cst", [P, 128])
                tri = sb(c, "tri", [P, P])
                trib = sb(c, "trib", [P, P], BF16)
                oneb = sb(c, "oneb", [P, P], BF16)
                L = sb(c, "rL", [P, T, NG + NE])
                s5 = sb(c, "s5", [P, 12, T])
                g4 = sb(c, "g4", [P, 3, T, NG])
                Lm = sb(c, "Lm", [P, T, NG, EPG])
                e8 = sb(c, "e8", [P, 8, T, EPG])
                oh = sb(c, "oh", [P, 2, T, NE])
                pr = sb(c, "rpr", [P, 2, T, NE])
                M = sb(c, "rM", [P, T, NE], BF16)
                rk = sb(c, "rrk", [P, 4, 2, T])
                ov = sb(c, "rov", [P, 6, NE])
                cmp9 = sb(c, "cmp9", [P, NE, 9])
                ovx = sb(c, "ovx", [1, OVB, NE])
                ovs = sb(c, "ovs", [1, OVB + 2])
                one32 = sb(c, "one32", [P, NE])
                ii = sb(c, "rii", [P, 4, 2, T], I32)
                addr = sb(c, "raddr", [P, 2 * T], U32)
                tok = sb(c, "rtok", [P, T], I32)
                blank = sb(c, "blank", [P, SCOLS], U32)
                ld, mm, ex, exd, md, rd, pz, tin, sd, sc, ch, ach, ixl = (
                    sem(c, "r" + n) for n in ("ld", "mm", "ex", "exd", "md", "rd", "pz", "tin", "sd", "sc", "ch", "ach", "ixl"))
                with nc.Block() as block:
                    @block.sync
                    def _(sp):
                        with nc.allow_non_contiguous_dma("narrow router"):
                            sp.dma_start(wr[:, :, 0:NG], a["w_group"][0].rearrange("(k p) n -> p k n", p=P)).then_inc(ld, 16)
                            sp.dma_start(wr[:, :, NG:], a["w_erouter"][0].rearrange("(k p) n -> p k n", p=P)).then_inc(ld, 16)
                            sp.dma_start(br[:, 0:NG], a["b_group"].partition_broadcast(P).rearrange("p l d -> p (l d)")).then_inc(ld, 16)
                            sp.dma_start(br[:, NG:], a["b_erouter"].partition_broadcast(P).rearrange("p l d -> p (l d)")).then_inc(ld, 16)
                        sp.dma_start(cst[:, :], a["c_route"]).then_inc(ld, 16)
                        sp.dma_start(tri[:, :], a["c_tri"]).then_inc(ld, 16)
                        sp.dma_start(tok[:, :], a["c_tok"]).then_inc(ld, 16)
                        sp.wait_ge(pz, 2)
                        sp.dma_start(tab.rearrange("(p c) o -> p (c o)", p=P), blank[:, :]).then_inc(tin, 16)
                        sp.wait_ge(sc, 16 * 2 * T)
                        sp.dma_start(idx[:, :], tab.rearrange("(p c) o -> p (c o)", p=P)).then_inc(ixl, 16)
                        sp.wait_ge(ixl, 16)

                    @block.gpsimd
                    def _(pool):
                        nc.gpsimd.memset(oneb[:, :], 1.0).then_inc(pz, 1)
                        nc.gpsimd.memset(blank[:, :], 2 * NTOK).then_inc(pz, 1)
                        nc.gpsimd.memset(one32[:, :], 1.0).then_inc(pz, 1)
                        nc.gpsimd.memset(xg[:, :, :], 0.0).then_inc(pz, 1)
                        pool.wait_ge(tin, 16)
                        pool.wait_ge(ld, 112)
                        pool.wait_ge(sd, 1)
                        for k in range(2):
                            for t in range(T):
                                pool.indirect_dma_start(
                                    out=tab, out_offset=bass.IndirectOffsetOnAxis(ap=addr[:, k * T + t:k * T + t + 1], axis=0),
                                    in_=tok[:, t:t + 1], in_offset=None).then_inc(sc, 16)
                        pool.wait_ge(pz, 4)

                    @block.tensor
                    def _(pe):
                        pe.wait_ge(ld, 112)
                        for t in range(T):
                            for k in range(KT):
                                ins = nc.tensor.matmul(ps[0][:, t * 36:(t + 1) * 36], nT[:, k, t * P:(t + 1) * P], wr[:, k, :],
                                                       start=k == 0, stop=k == KT - 1)
                        ins.then_inc(mm, 1)
                        pe.wait_ge(md, 1)
                        pe.wait_ge(pz, 1)
                        for t in range(T):
                            for u in range(t + 1):
                                nc.tensor.matmul(ps[1][:, t * NE:(t + 1) * NE], (trib if u == t else oneb)[:, :], M[:, u, :],
                                                 start=u == 0, stop=u == t)
                        for t in range(T):
                            ins = nc.tensor.matmul(ps[2][:, 0:NE], oneb[:, :], M[:, t, :], start=t == 0, stop=t == T - 1)
                        ins.then_inc(mm, 1)

                    @block.scalar
                    def _(act):
                        act.wait_ge(ex, 1)
                        nc.scalar.activation(g4[:, 1], g4[:, 0], ACT.Exp).then_inc(exd, 1)
                        act.wait_ge(ex, 2)
                        nc.scalar.activation(e8[:, 1], e8[:, 0], ACT.Exp).then_inc(exd, 1)

                    @block.vector
                    def _(dve):
                        link = chain(dve, ch)
                        v = nc.vector
                        def bc(x, n):
                            return x.unsqueeze(2).broadcast_to([P, T, n])

                        def first(dst, src, top, w, n, eq, tmp):
                            link(v.tensor_tensor(eq, src, bc(top, n), ALU.is_equal))
                            link(v.tensor_tensor(eq, eq, w.unsqueeze(1).broadcast_to([P, T, n]), ALU.mult))
                            link(v.reduce_max(tmp, eq, AX))
                            link(v.tensor_tensor(dst, eq, bc(tmp, n), ALU.is_equal))

                        dve.wait_ge(ld, 112)
                        link(v.tensor_copy(trib[:, :], tri[:, :]))
                        dve.wait_ge(mm, 1)
                        link(v.tensor_tensor(L[:, :, :], ps[0][:, 0:T * 36].rearrange("p (t n) -> p t n", t=T),
                                             br[:, :].unsqueeze(1).broadcast_to([P, T, 36]), ALU.add))
                        g = L[:, :, 0:NG]
                        link(v.reduce_max(s5[:, 0], g, AX))
                        v.tensor_tensor(g4[:, 0], g, bc(s5[:, 0], NG), ALU.subtract).then_inc(ex, 1)
                        first(g4[:, 2], g, s5[:, 0], cst[:, 0:4], NG, e8[:, 7, :, 0:4], s5[:, 1])
                        dve.wait_ge(exd, 1)
                        link(v.reduce_sum(s5[:, 2], g4[:, 1], AX))
                        link(v.reciprocal(s5[:, 3], s5[:, 2]))
                        link(v.tensor_tensor(Lm[:, :, :, :], L[:, :, NG:].rearrange("p t (g j) -> p t g j", g=NG),
                                             g4[:, 2].unsqueeze(3).broadcast_to([P, T, NG, EPG]), ALU.mult))
                        link(v.reduce_sum(e8[:, 2], Lm[:, :, :, :].rearrange("p t g j -> p t j g"), AX))
                        link(v.reduce_max(s5[:, 4], e8[:, 2], AX))
                        v.tensor_tensor(e8[:, 0], e8[:, 2], bc(s5[:, 4], EPG), ALU.subtract).then_inc(ex, 1)
                        dve.wait_ge(exd, 2)
                        link(v.reduce_sum(s5[:, 5], e8[:, 1], AX))
                        link(v.reciprocal(s5[:, 5], s5[:, 5]))
                        link(v.tensor_tensor(e8[:, 3], e8[:, 1], bc(s5[:, 5], EPG), ALU.mult))
                        link(v.reduce_max(s5[:, 6], e8[:, 3], AX))
                        first(e8[:, 4], e8[:, 3], s5[:, 6], cst[:, 4:12], EPG, e8[:, 7], s5[:, 1])
                        link(v.scalar_tensor_tensor(out=e8[:, 6], in0=e8[:, 4], scalar=-2.0, in1=e8[:, 3], op0=ALU.mult,
                                                    op1=ALU.add))
                        link(v.reduce_max(s5[:, 7], e8[:, 6], AX))
                        first(e8[:, 5], e8[:, 6], s5[:, 7], cst[:, 4:12], EPG, e8[:, 7], s5[:, 1])
                        for k in range(2):
                            ins = v.tensor_tensor(oh[:, k].rearrange("p t (g j) -> p t g j", g=NG),
                                                  g4[:, 2].unsqueeze(3).broadcast_to([P, T, NG, EPG]),
                                                  e8[:, 4 + k].unsqueeze(2).broadcast_to([P, T, NG, EPG]), ALU.mult)
                        link(ins)
                        v.tensor_tensor(M[:, :, :], oh[:, 0], oh[:, 1], ALU.add).then_inc(md, 1)
                        link(v.tensor_tensor(s5[:, 8], s5[:, 6], s5[:, 7], ALU.add))
                        link(v.reciprocal(s5[:, 8], s5[:, 8]))
                        link(v.tensor_tensor(s5[:, 9:11], s5[:, 6:8], s5[:, 3].unsqueeze(1).broadcast_to([P, 2, T]), ALU.mult))
                        link(v.tensor_tensor(gate[:, :, :], s5[:, 9:11], s5[:, 8].unsqueeze(1).broadcast_to([P, 2, T]), ALU.mult))
                        dve.wait_ge(mm, 2)
                        dve.wait_ge(pz, 3)
                        link(v.tensor_copy(ov[:, 0], ps[2][:, 0:NE]))
                        link(v.tensor_tensor(cmp9[:, :, :], ov[:, 0].unsqueeze(2).broadcast_to([P, NE, 9]),
                                             cst[:, 44:53].unsqueeze(1).broadcast_to([P, NE, 9]), ALU.is_gt))
                        link(v.reduce_sum(ov[:, 1], cmp9[:, :, :], AX))
                        link(v.tensor_tensor_scan(ov[:, 2], one32[:, :], ov[:, 1], 0.0, ALU.mult, ALU.add))
                        link(v.tensor_tensor(ov[:, 3], ov[:, 2], ov[:, 1], ALU.subtract))
                        link(v.tensor_scalar(ov[:, 4], ov[:, 3], float(CAP), float(MAIN - CAP), ALU.mult, ALU.add))
                        for i, src in enumerate((ps[1][:, 0:T * NE].rearrange("p (t e) -> p t e", t=T),
                                                 cst[:, 12:44].unsqueeze(1).broadcast_to([P, T, NE]),
                                                 ov[:, 4].unsqueeze(1).broadcast_to([P, T, NE]))):
                            for k in range(2):
                                ins = v.tensor_tensor(pr[:, k], oh[:, k], src, ALU.mult)
                            link(ins)
                            link(v.reduce_sum(rk[:, i], pr[:, :, :, :], AX))
                        link(v.tensor_tensor(rk[:, 2], rk[:, 2], rk[:, 1], ALU.subtract))
                        link(v.tensor_scalar(rk[:, 3], rk[:, 0], float(CAP), None, ALU.is_ge))
                        link(v.tensor_tensor(rk[:, 2], rk[:, 2], rk[:, 3], ALU.mult))
                        link(v.tensor_tensor(rk[:, 0], rk[:, 0], rk[:, 1], ALU.add))
                        link(v.tensor_tensor(rk[:, 0], rk[:, 0], rk[:, 2], ALU.add))
                        link(v.tensor_copy(slots[:, :], rk[:, 0].rearrange("p k t -> p (k t)")))
                        link(v.tensor_copy(ii[:, 0], rk[:, 0]))
                        link(v.tensor_scalar(ii[:, 1], ii[:, 0], P - 1, None, ALU.bitwise_and))
                        link(v.tensor_scalar(ii[:, 2], ii[:, 0], 7, None, ALU.logical_shift_right))
                        v.scalar_tensor_tensor(out=addr[:, :], in0=ii[:, 1].rearrange("p k t -> p (k t)"), scalar=float(SCOLS),
                                               in1=ii[:, 2].rearrange("p k t -> p (k t)"), op0=ALU.mult,
                                               op1=ALU.add).then_inc(sd, 1)
                        link(v.tensor_tensor(ovx[:, :, :], ov[0:1, 2].unsqueeze(1).broadcast_to([1, OVB, NE]),
                                             cst[0:1, 53:53 + OVB].unsqueeze(2).broadcast_to([1, OVB, NE]), ALU.is_le))
                        link(v.reduce_sum(ovs[:, 0:OVB], ovx[:, :, :], AX))
                        link(v.tensor_scalar(ovs[:, 0:OVB], ovs[:, 0:OVB], float(NE - 1), None, ALU.min))
                        link(v.tensor_scalar(ovs[:, OVB:OVB + 1], ov[0:1, 2, NE - 1:NE], 1.0, None, ALU.add))
                        link(v.tensor_copy(ove[:, :], ovs[:, 0:OVB]))
                        link(v.tensor_copy(ii[0:1, 3, 0, 0:1], ovs[:, OVB:OVB + 1]))
                        link(v.tensor_scalar(ovn[:, :], ii[0:1, 3, 0, 0:1], 1, None, ALU.logical_shift_right))

        def expert_block(xg, idx, xs, ys, ovn, ove):
            with ExitStack() as c:
                xT = sb(c, "xT", [P, 2, KT, P])
                sg = sb(c, "sg", [P, 512])
                hh = sb(c, "hh", [P, 512])
                hT = sb(c, "hT", [P, ET, P])
                yb = sb(c, "yb", [P, 2, D])
                ix = sb(c, "ix", [P, 2], U32)
                ixd, gd, xt, xe, sgd, hd, htr, hev, yd = (
                    sem(c, "e" + n) for n in ("ixd", "gd0", "xt", "xe", "sgd", "hd", "htr", "hev", "yd"))
                yw = [sem(c, f"eyw{i}") for i in range(2)]
                waited = [sem(c, f"ewaited{i}") for i in range(2)]
                gds = [gd, sem(c, "egd1")]

                def wait_apart(eng, k, s, value):
                    eng.wait_ge(s, value)
                    eng.sem_inc(waited[k], 1)

                def pool_pair(pool, col, n, s, first, bound):
                    if not first:
                        pool.wait_ge(xt, n - 1)
                    nc.gpsimd.tensor_copy(ix[:, s:s + 1], idx[:, col]).then_inc(ixd, 1)
                    wait_apart(pool, 0, ixd, n + 1)
                    pool.indirect_dma_start(out=xg[:, s, :], out_offset=None, in_=xs,
                                            in_offset=bass.IndirectOffsetOnAxis(ap=ix[:, s:s + 1], axis=0),
                                            bounds_check=bound, oob_is_err=False).then_inc(gds[s], 16)

                def w(j):
                    return slot(W_MOE + j) if j < 4 else slot2(W_MOE + j)

                def pe_turn(pe, n, s, rounds):
                    pe.wait_ge(gds[s], rounds)
                    pe.wait_ge(xe, n)
                    for k in range(KT):
                        ins = nc.tensor.transpose(ps[k // 4][:, (k % 4) * P:(k % 4 + 1) * P], xg[:, s, k * P:(k + 1) * P],
                                                  ident[:, :])
                    ins.then_inc(xt, 1)

                def pe_pair(pe, n, s, got):
                    pe.wait_ge(xe, n + 1)
                    for m in range(2):
                        got(2 * m)
                        pe.wait_ge(hd, n)
                        for k in range(KT):
                            for x in range(2):
                                ins = nc.tensor.matmul(ps[2 + m][64 * x:64 * x + 64, :], xT[:, s, k, 64 * x:64 * x + 64],
                                                       w(2 * m + x)[:, k, :], start=k == 0, stop=k == KT - 1)
                        ins.then_inc(used, 2)

                def pe_down(pe, n, s, got):
                    pe.wait_ge(hd, n + 1)
                    pe.wait_ge(hev, n)
                    for k in range(ET):
                        ins = nc.tensor.transpose(ps[4][:, k * P:(k + 1) * P], hh[:, k * P:(k + 1) * P], ident[:, :])
                    ins.then_inc(htr, 1)
                    got(4)
                    pe.wait_ge(hev, n + 1)
                    pe.wait_ge(yd, n)
                    for half in range(2):
                        for k in range(ET):
                            for x in range(2):
                                ins = nc.tensor.matmul(ps[5 + half][64 * x:64 * x + 64, :], hT[:, k, 64 * x:64 * x + 64],
                                                       w(4 + x)[:, k, half * 512:(half + 1) * 512], start=k == 0,
                                                       stop=k == ET - 1)
                    ins.then_inc(used, 2)

                def act_pair(act, n, s, u0):
                    act.wait_ge(used, u0 + 2)
                    act.wait_ge(hd, n)
                    nc.scalar.activation(sg[:, :], ps[2][:, :], ACT.Silu).then_inc(sgd, 1)
                    act.wait_ge(htr, n + 1)
                    nc.scalar.copy(hT[:, :, :], ps[4][:, :].rearrange("p (k n) -> p k n", k=ET)).then_inc(hev, 1)

                def dve_turn(dve, n, s):
                    dve.wait_ge(xt, n + 1)
                    for h in range(2):
                        ins = nc.vector.tensor_tensor(xT[:, s, 4 * h:4 * h + 4, :],
                                                      ps[h][:, :].rearrange("p (k n) -> p k n", k=4),
                                                      gcol[:, 3, 4 * h:4 * h + 4].unsqueeze(2).broadcast_to([P, 4, P]), ALU.mult)
                    ins.then_inc(xe, 1)

                def dve_mid(dve, n, s, u0):
                    dve.wait_ge(sgd, n + 1)
                    dve.wait_ge(used, u0 + 4)
                    dve.wait_ge(htr, n)
                    nc.vector.tensor_tensor(hh[:, :], ps[3][:, :], sg[:, :], ALU.mult).then_inc(hd, 1)

                def dve_out(dve, n, s, u0, free):
                    dve.wait_ge(used, u0 + 6)
                    free()
                    nc.vector.tensor_copy(yb[:, s, 0:512], ps[5][:, :])
                    nc.vector.tensor_copy(yb[:, s, 512:D], ps[6][:, :]).then_inc(yd, 1)

                HALF = PAIRS // 2

                def two_pairs(eng, both):
                    with eng.Fori(0, HALF - 1) as i:
                        both(i, False)
                    both(HALF - 1, True)

                with nc.Block() as block:
                    @block.sync
                    def _(sp):
                        def both(i, last):
                            for s in range(2):
                                if not (last and s == 1):
                                    for j in range(6):
                                        sp.wait_ge(used, i * 12 + (W_MOE + 6 * s + j + 1))
                                        src = a["w1" if j < 2 else "w3" if j < 4 else "w2"][0][bass.ds(i * 4 + (2 * s + 2 + j % 2), 1)]
                                        sp.dma_start(w(j), src.rearrange("a (k p) n -> p (a k) n", p=P)).then_inc(
                                            landed[(W_MOE + j) % SLOTS], 16)
                                sp.wait_ge(yd, i * 2 + (s + 1))
                                sp.dma_start(ys[bass.ds(i * (2 * P) + s * P, P), :], yb[:, s, :]).then_inc(yw[s], 16)
                        two_pairs(sp, both)
                        for s in range(2):
                            sp.wait_ge(yw[s], 16 * HALF)

                    @block.gpsimd
                    def _(pool):
                        bound = pool.to_reg(NTOK - 1)
                        for s in range(2):
                            pool_pair(pool, slice(s, s + 1), s, s, True, bound)
                        with pool.Fori(1, HALF) as i:
                            for s in range(2):
                                pool_pair(pool, bass.ds(i * 2 + s, 1), i * 2 + s, s, False, bound)

                    @block.tensor
                    def _(pe):
                        pe.wait_ge(gds[0], 16)
                        for k in range(KT):
                            ins = nc.tensor.transpose(ps[k // 4][:, (k % 4) * P:(k % 4 + 1) * P], xg[:, 0, k * P:(k + 1) * P],
                                                      ident[:, :])
                        ins.then_inc(xt, 1)

                        def both(i, last):
                            for s in range(2):
                                def got(j, s=s):
                                    for x in range(2):
                                        c = W_MOE + j + x
                                        pe.wait_ge(landed[c % SLOTS], i * 32 + (landed_by[c] + 16 * s))
                                n = i * 2 + s
                                pe_pair(pe, n, s, got)
                                if s == 0:
                                    pe_turn(pe, n + 1, 1, i * 16 + 16)
                                elif not last:
                                    pe_turn(pe, n + 1, 0, i * 16 + 32)
                                pe_down(pe, n, s, got)
                        two_pairs(pe, both)

                    @block.scalar
                    def _(act):
                        def both(i, last):
                            for s in range(2):
                                act_pair(act, i * 2 + s, s, i * 12 + (W_MOE + 6 * s))
                        two_pairs(act, both)

                    @block.vector
                    def _(dve):
                        dve_turn(dve, 0, 0)

                        def both(i, last):
                            for s in range(2):
                                n = i * 2 + s
                                u0 = i * 12 + (W_MOE + 6 * s)
                                if not (last and s == 1):
                                    dve_turn(dve, n + 1, 1 - s)
                                dve_mid(dve, n, s, u0)
                                dve_out(dve, n, s, u0, lambda: dve.wait_ge(yw[s], i * 16))

                        for s in range(2):
                            dve_turn(dve, s + 1, 1 - s)
                            dve_mid(dve, s, s, W_MOE + 6 * s)
                            dve_out(dve, s, s, W_MOE + 6 * s, lambda: None)
                        with dve.Fori(1, HALF - 1) as i:
                            both(i, False)
                        both(HALF - 1, True)

                U1 = W_MOE + 6 * PAIRS
                with nc.Block() as block:
                    def loop(eng, body):
                        n = eng.value_load(ovn[0:1, 0:1], min_val=0, max_val=OVB // 2)
                        with eng.If(n > 0):
                            with eng.Fori(0, n) as q:
                                body(q)

                    @block.sync
                    def _(sp):
                        def body(q):
                            e = [sp.value_load(ove[0:1, bass.ds(q * 2 + x, 1)], min_val=0, max_val=NE - 1) for x in range(2)]
                            for j in range(6):
                                src = a["w1" if j < 2 else "w3" if j < 4 else "w2"][0][bass.ds(e[j % 2], 1)]
                                sp.dma_start(w(j), src.rearrange("a (k p) n -> p (a k) n", p=P)).then_inc(
                                    landed[(W_MOE + j) % SLOTS], 16)
                            sp.wait_ge(yd, q + (PAIRS + 1))
                            sp.dma_start(ys[bass.ds(q * P + MAIN, P), :], yb[:, 0, :]).then_inc(yw[0], 16)
                            wait_apart(sp, 1, yw[0], q * 16 + 16 * (HALF + 1))
                        loop(sp, body)

                    @block.gpsimd
                    def _(pool):
                        bound = pool.to_reg(NTOK - 1)

                        def body(q):
                            n = q + PAIRS
                            pool.wait_ge(xt, n)
                            nc.gpsimd.tensor_copy(ix[:, 0:1], idx[:, bass.ds(q + PAIRS, 1)]).then_inc(ixd, 1)
                            wait_apart(pool, 0, ixd, n + 1)
                            pool.indirect_dma_start(out=xg[:, 0, :], out_offset=None, in_=xs,
                                                    in_offset=bass.IndirectOffsetOnAxis(ap=ix[:, 0:1], axis=0),
                                                    bounds_check=bound, oob_is_err=False).then_inc(gds[0], 16)
                            pool.wait_ge(yd, n + 1)
                        loop(pool, body)

                    @block.tensor
                    def _(pe):
                        def body(q):
                            n = q + PAIRS

                            def got(j):
                                for x in range(2):
                                    c = W_MOE + j + x
                                    pe.wait_ge(landed[c % SLOTS], q * 16 + (landed_by[c] + 16 * PAIRS))
                            pe_turn(pe, n, 0, q * 16 + 16 * (HALF + 1))
                            pe_pair(pe, n, 0, got)
                            pe_down(pe, n, 0, got)
                        loop(pe, body)

                    @block.scalar
                    def _(act):
                        loop(act, lambda q: act_pair(act, q + PAIRS, 0, q * 6 + U1))

                    @block.vector
                    def _(dve):
                        def body(q):
                            n = q + PAIRS
                            dve_turn(dve, n, 0)
                            dve_mid(dve, n, 0, q * 6 + U1)
                            dve_out(dve, n, 0, q * 6 + U1, lambda: dve.wait_ge(yw[0], q * 16 + 16 * HALF))
                        loop(dve, body)

        def final_block(hN, gate, slots, ys):
            with ExitStack() as c:
                yg = sb(c, "yg", [P, 2 * T, D])
                sq = sb(c, "fsq", [P, D])
                ss = sb(c, "fss", [P, T])
                gf = sb(c, "gf", [P, D])
                gl = [sem(c, f"fgl{i}") for i in range(2 * T)]
                ld, sd, sqd, rd, yd, ch, sr = (sem(c, "f" + n) for n in ("ld", "sd", "sqd", "rd", "yd", "ch", "sr"))
                with nc.Block() as block:
                    @block.sync
                    def _(sp):
                        sp.dma_start(gf[:, :], a["g_final"].partition_broadcast(P)).then_inc(ld, 16)
                        for t in range(T):
                            sp.wait_ge(yd, t + 1)
                            dst = a["y_prompt"][0, t * P:(t + 1) * P, :] if t < TP else a["y_sample"].rearrange("b q d -> (b q) d")
                            store(sp, dst, hN[:, t, :])
                        sp.wait_ge(stored, ns[0])

                    @block.gpsimd
                    def _(pool):
                        for t in range(T):
                            for k in range(2):
                                i = 2 * t + k
                                pool.indirect_dma_start(
                                    out=yg[:, i, :], out_offset=None, in_=ys,
                                    in_offset=bass.IndirectOffsetOnAxis(ap=slots[:, k * T + t:k * T + t + 1], axis=0),
                                    bounds_check=NSLOT - 1, oob_is_err=False).then_inc(gl[i], 16)

                    @block.scalar
                    def _(act):
                        for t in range(T):
                            act.wait_ge(sd, t + 1)
                            if t:
                                act.wait_ge(sqd, t)
                            nc.scalar.activation(sq[:, :], hN[:, t, :], ACT.Square, accum_out=ss[:, t:t + 1]).then_inc(sqd, 1)
                        act.wait_ge(rd, 1)
                        nc.scalar.activation(ss[:, :], ss[:, :], ACT.Sqrt).then_inc(sr, 1)

                    @block.vector
                    def _(dve):
                        link = chain(dve, ch)
                        for t in range(T):
                            for k in range(2):
                                dve.wait_ge(gl[2 * t + k], 16)
                                ins = nc.vector.scalar_tensor_tensor(out=hN[:, t, :], in0=yg[:, 2 * t + k, :],
                                                                     scalar=gate[:, k, t:t + 1], in1=hN[:, t, :],
                                                                     op0=ALU.mult, op1=ALU.add)
                                if k == 0:
                                    link(ins)
                            ins.then_inc(sd, 1)
                        dve.wait_ge(sqd, T)
                        nc.vector.tensor_scalar(ss[:, :], ss[:, :], 1.0 / D, EPS, ALU.mult, ALU.add).then_inc(rd, 1)
                        dve.wait_ge(sr, 1)
                        link(nc.vector.reciprocal(ss[:, :], ss[:, :]))
                        dve.wait_ge(ld, 16)
                        for t in range(T):
                            nc.vector.scalar_tensor_tensor(out=hN[:, t, :], in0=hN[:, t, :], scalar=ss[:, t:t + 1],
                                                           in1=gf[:, :], op0=ALU.mult, op1=ALU.mult).then_inc(yd, 1)

        def x_tile(t):
            return a["x_prompt"][0, t * P:(t + 1) * P, :] if t < TP else a["x_sample"].rearrange("b q d -> (b q) d")

        def per_tile(prompt, sample, f):
            def at(t):
                if t < TP:
                    return a[prompt].rearrange(f"l b t {f} -> (l b t) ({f})")[t * P:(t + 1) * P, :]
                return a[sample].rearrange(f"l b t {f} -> (l b t) ({f})")
            return at

        tab = nc.dram_tensor("row_tokens", [NSLOT, 1], U32, kind="Internal").ap()
        xs = nc.dram_tensor("ffn_rows", [NTOK, D], F32, kind="Internal").ap()
        ys = nc.dram_tensor("expert_rows", [NSLOT, D], F32, kind="Internal").ap()

        lamcol = sb(top, "lamcol", [P, 1])[:, :]
        with ExitStack() as c1:
            mixT = sb(c1, "mixT", [P, KT, NTOK])
            foxN = sb(c1, "foxN", [P, 512])
            with ExitStack() as c2:
                nT = sb(c2, "nT", [P, KT, NTOK])
                with ExitStack() as c3:
                    xN = sb(c3, "xN", [P, T, D])
                    norm_block("n1", xN, T, 0, nT, load=x_tile, first=True, chunk_range=(0, 6))
                with ExitStack() as c3:
                    qT, kT, vN = (sb(c3, n, [P, 4, NTOK]) for n in ("fqT", "fkT", "fvN_"))
                    vN = vN[:, :, :].rearrange("p a b -> p (a b)").rearrange("p (t n) -> p t n", t=T)
                    project_block("pf", nT, qT, kT, vN, W_FOX, (6, 9), True,
                                  per_tile("p_fk", "s_fk", "h d"), per_tile("p_fv", "s_fv", "h d"))
                    CT = sb(c3, "CT", [80, KS])
                    L2 = sb(c3, "L2", [64, NB, P])
                    bias_l = sb(c3, "bias_l", [80, NB, P])
                    with ExitStack() as c4:
                        RL, RR = sb(c4, "RL", [P, 2, SEQ]), sb(c4, "RR", [P, 2, SEQ])
                        gates_block(nT, RL, RR, CT, L2, bias_l)
                        prompt_attention("fp", "fox", qT, kT, vN, None, mixT, RL=RL, RR=RR, blank=ys[MAIN:, :])
                    decode_attention("fd", "fox", qT, kT, vN, foxN, C_FOX, bias_l=bias_l, CT=CT, L2=L2, chunk_range=(9, 13))
                recycle_semaphores()
                with ExitStack() as c3:
                    qT, kT, vN = (sb(c3, n, [P, 4, NTOK]) for n in ("dqT", "dkT", "dvN_"))
                    vN = vN[:, :, :].rearrange("p a b -> p (a b)").rearrange("p (t n) -> p t n", t=T)
                    project_block("pd", nT, qT, kT, vN, W_DIFF, (13, 16), False,
                                  per_tile("p_dk", "s_dk", "h c d"), per_tile("p_dv", "s_dv", "h d"))
                    lambda_block(lamcol, (16, 16))
                    diffN = nT[:, 0:4, :].rearrange("p a b -> p (a b)").rearrange("p (t n) -> p t n", t=T)
                    prompt_attention("dp", "diff", qT, kT, vN, diffN, None, lamcol=lamcol)
                    decode_attention("dd", "diff", qT, kT, vN, diffN[:, TP, :], C_DIFF, lamcol=lamcol, chunk_range=(16, 20))
                    mix_block(foxN, diffN, mixT, (20, 20))
            hN = sb(c1, "hN", [P, T, D])
            recycle_semaphores()
            residual_block("ro", mixT, hN, W_O, (20, 22), load=x_tile)
            nT = mixT
            with ExitStack() as c2:
                mkT, mvN = sb(c2, "mkT", [P, KT, MEM]), sb(c2, "mvN", [P, 2, D])
                with ExitStack() as c3:
                    memN, mT = sb(c3, "memN", [P, 2, D]), sb(c3, "mT", [P, KT, MEM])
                    norm_block("n2", memN, 2, 2, mT, load=lambda t: a["mem_prompt"][0, t * P:(t + 1) * P, :])
                    memory_block(mT, mkT, mvN, (22, 26))
                norm_block("n3", hN, T, 1, nT)
                qT = sb(c2, "mqT", [P, KT, NTOK])
                query_block(nT, qT, (26, 28))
                prompt_attention("mp", "mem", qT, mkT, mvN, None, nT)
                with ExitStack() as c3:
                    oN = sb(c3, "moN", [P, D])
                    decode_attention("md", "mem", qT, None, None, oN, C_MEM, chunk_range=(28, 36))
                    turn_block(oN, nT)
            recycle_semaphores()
            residual_block("rm", nT, hN, W_MO, (36, 38))
            norm_block("n4", hN, T, 3, nT, extra_dram=xs)
            with ExitStack() as c2:
                gate = sb(c2, "gate", [P, 2, T])
                slots = sb(c2, "slots", [P, 2 * T], U32)
                ovn, ove = sb(c2, "ovn", [1, 1], I32), sb(c2, "ove", [1, OVB], I32)
                with ExitStack() as c3:
                    xg = sb(c3, "xg", [P, 2, D])
                    idx = sb(c3, "idx", [P, SCOLS], U32)
                    route_block(nT, xg, gate, slots, idx, ovn, ove, tab)
                    expert_block(xg, idx, xs, ys, ovn, ove)
                final_block(hN, gate, slots, ys)


_INS = ["x_prompt", "x_sample", "cache_fox_k", "cache_fox_v", "cache_fox_logf", "cache_diff_k", "cache_diff_v",
        "cache_mem_k", "cache_mem_v", "mem_prompt", "g_mix", "w_in", "b_forget", "lam_q1", "lam_k1", "lam_q2", "lam_k2",
        "g_diff", "w_o", "g_mem_q", "g_mem_kv", "w_mq", "w_mk", "w_mv", "w_mo", "g_ffn", "w_group", "b_group",
        "w_erouter", "b_erouter", "w1", "w3", "w2", "g_final"]
_OUTS = [("y_prompt", (1, SEQ, D)), ("y_sample", (NB, TD, D)),
         ("p_fk", (1, 1, SEQ, FH, HD)), ("p_fv", (1, 1, SEQ, FH, HD)), ("p_logf", (1, 1, SEQ, FH)),
         ("p_dk", (1, 1, SEQ, DH, 2, HD)), ("p_dv", (1, 1, SEQ, DH, 128)),
         ("p_mk", (1, 1, MEM, MH, MD)), ("p_mv", (1, 1, MEM, MH, MD)),
         ("s_fk", (1, NB, TD, FH, HD)), ("s_fv", (1, NB, TD, FH, HD)), ("s_logf", (1, NB, TD, FH)),
         ("s_dk", (1, NB, TD, DH, 2, HD)), ("s_dv", (1, NB, TD, DH, 128))]


def constants(np):
    f = np.float32
    i = np.arange(P)
    big = f(-1e30)
    out = {"c_ident": np.eye(P, dtype=f),
           "c_causal": np.where(i[None, :] <= i[:, None], f(0), big),
           "c_chunk": np.where(i[None, :] // 64 <= i[:, None] // 64, f(0), big)}
    pos = np.concatenate([np.arange(SEQ), np.tile(PAST + np.arange(TD), NB)]).astype(f)
    inv = np.power(f(500000.0), -np.arange(8, dtype=f) / f(8)).astype(f)
    ang = (pos[:, None] * inv[None, :]).astype(f)
    cos, sin = np.cos(ang), np.sin(ang)
    tiles = lambda x: np.ascontiguousarray(x.reshape(T, P, 16).transpose(1, 0, 2)).astype(f)
    out["c_cos"] = tiles(np.concatenate([cos, cos], 1))
    out["c_sin"] = tiles(np.concatenate([-sin, sin], 1))
    sel = np.zeros((80, NB, FH, TD), f)
    for b in range(NB):
        for h in range(FH):
            sel[b * FH + h, b, h, :] = -1.0 / SC
    for q in range(TD):
        sel[64 + q, :, :, q] = 1.0
    out["c_sel"] = sel.reshape(80, NB, P)
    tri16 = np.zeros((TD, KS), f)
    tri16[:, PAST:] = np.where(np.arange(TD)[None, :] > np.arange(TD)[:, None], big, f(0))
    out["c_tri16"] = tri16
    comb = np.zeros((P, P), f)
    sgn = np.zeros((P, 2), f)
    for h in range(DH):
        for cc in range(2):
            for q in range(TD):
                comb[32 * h + 16 * cc + q, 32 * h + q] = 1.0
                sgn[32 * h + 16 * cc + q, cc] = 1.0
    out["c_comb"], out["c_sgn"] = comb, sgn
    out["c_tri"] = (i[:, None] < i[None, :]).astype(f)
    cst = np.zeros((P, 128), f)
    cst[:, 0:4] = np.arange(4, 0, -1)
    cst[:, 4:12] = np.arange(8, 0, -1)
    cst[:, 12:44] = CAP * np.arange(NE)
    cst[:, 44:53] = CAP * np.arange(1, 10)
    cst[:, 53:53 + OVB] = np.arange(OVB)
    out["c_route"] = cst
    out["c_tok"] = (np.arange(T, dtype=np.int32)[None, :] * P + i[:, None].astype(np.int32)).astype(np.int32)
    return {k: np.ascontiguousarray(v) for k, v in out.items()}


def kernel(**inputs):
    import numpy as np
    import concourse.bacc as bacc
    from concourse.bass_utils import run_bass_kernel_spmd

    nc = bacc.Bacc("TRN2", target_bir_lowering=False, num_devices=1)
    arrays, aps = {}, {}
    given = {n: np.ascontiguousarray(inputs[n]) for n in _INS}
    for n, x in {**given, **constants(np)}.items():
        arrays[f"in_{n}"] = x
        aps[n] = nc.dram_tensor(f"in_{n}", x.shape, mybir.dt.from_np(x.dtype), kind="ExternalInput").ap()
    for n, shape in _OUTS:
        aps[n] = nc.dram_tensor(f"out_{n}", shape, F32, kind="ExternalOutput").ap()
    build(nc, aps)
    r = run_bass_kernel_spmd(nc, [arrays], core_ids=[0])
    return tuple(r.results[0][f"out_{n}"] for n, _ in _OUTS)
```

```python
import concourse.bass as bass
import concourse.mybir as mybir
from contextlib import ExitStack

F32 = mybir.dt.float32
BF16 = mybir.dt.bfloat16
I32 = mybir.dt.int32
U32 = mybir.dt.uint32
ALU = mybir.AluOpType
ACT = mybir.ActivationFunctionType
AX = mybir.AxisListType.X

P = 128
D = 1024
KT = D // P
SEQ = 512
NB = 8
TD = 16
PAST = 256
T = 5
TP = 4
NTOK = T * P
FH = 8
HD = 64
DH = 4
MEM = 256
MH = 4
MD = 256
NG = 4
EPG = 8
NE = NG * EPG
DE = 512
ET = DE // P
CAP = 64
PAIRS = NE // 2
MAXB = NTOK // CAP
NBLK = PAIRS + 2 * NTOK // CAP
NSLOT = NBLK * P
IN_W = 3 * 512 + FH + 3 * 512
EPS = 1e-6
LAM_INIT = 0.8 - 0.6
KS = PAST + TD
SC = HD ** -0.5
MSC = MD ** -0.5
SLOTS = 6
W_FOX, C_FOX, W_DIFF, C_DIFF, W_O, W_MK, W_MV, W_MQ, C_MEM, W_MO, W_MOE = 0, 3, 7, 10, 14, 16, 18, 20, 22, 30, 32


def build(nc, a):
    top = ExitStack()
    names = [0]

    def sb(ctx, name, shape, dt=F32):
        return ctx.enter_context(nc.sbuf_tensor(name, shape, dt))

    finished = []

    def sem(ctx, name):
        s = nc.alloc_semaphore(name=name)
        if ctx is not top:
            ctx.callback(finished.append, s)
        return s

    def recycle_semaphores():
        nc.clear_and_free_semaphores(finished)
        finished.clear()
        nc.all_engine_barrier()

    with top:
        ps = [top.enter_context(nc.psum_tensor(f"bank{i}", [P, 512], F32)) for i in range(8)]
        ring = sb(top, "ring", [P, SLOTS, 4096])
        ident = sb(top, "ident", [P, P])
        gcol = sb(top, "gcol", [P, 4, KT])
        landed = [sem(top, f"landed{i}") for i in range(SLOTS)]
        used = sem(top, "chunks_used")
        stored = sem(top, "stored")
        stored_v = sem(top, "stored_values")
        ns = [0]

        def store(eng, dst, src):
            ns[0] += 16
            eng.dma_start(dst, src).then_inc(stored, 16)

        w_in, w_o, w_mk, w_mv, w_mq, w_mo = (a[n][0] for n in ("w_in", "w_o", "w_mk", "w_mv", "w_mq", "w_mo"))

        def cols(w, c0):
            return w[:, c0:c0 + 512].rearrange("(k p) n -> p k n", p=P)

        fox_w = 3 * 512 + FH
        heads_of = {"cache_fox_k": "h d", "cache_fox_v": "h d", "cache_diff_k": "h c d", "cache_diff_v": "h d",
                    "cache_mem_k": "h d", "cache_mem_v": "h d"}

        def cache(name):
            f = heads_of[name]
            return a[name][0].rearrange(f"b t {f} -> b t ({f})")

        plain = {W_FOX + i: cols(w_in, 512 * i) for i in range(3)}
        plain |= {W_DIFF + i: cols(w_in, fox_w + 512 * i) for i in range(3)}
        for c, w in ((W_O, w_o), (W_MK, w_mk), (W_MV, w_mv), (W_MQ, w_mq), (W_MO, w_mo)):
            plain |= {c + i: cols(w, 512 * i) for i in range(2)}

        def slot(c):
            return ring[:, c % SLOTS, :].rearrange("p (k n) -> p k n", n=512)

        def slot2(c):
            return ring[:, c % SLOTS, :].rearrange("p (k n) -> p k n", n=1024)

        def parts(c):
            if c in plain:
                return [(slot(c), plain[c])]
            if c >= W_MOE:
                j = (c - W_MOE) % 6
                e = 2 * ((c - W_MOE) // 6) + j % 2
                name = "w1" if j < 2 else "w3" if j < 4 else "w2"
                return [(slot(c) if j < 4 else slot2(c), a[name][0, e].rearrange("(k p) n -> p k n", p=P))]
            if c >= C_MEM:
                b = c - C_MEM
                return [(slot2(c)[:, 2 * i:2 * i + 2, :], cache(n)[b].rearrange("(k p) f -> p k f", p=P))
                        for i, n in enumerate(("cache_mem_k", "cache_mem_v"))]
            kind, c0 = ("fox", C_FOX) if c < W_DIFF else ("diff", C_DIFF)
            out = []
            for s in range(2):
                for i, n in enumerate((f"cache_{kind}_k", f"cache_{kind}_v")):
                    out.append((slot(c)[:, 4 * s + 2 * i:4 * s + 2 * i + 2, :],
                                cache(n)[2 * (c - c0) + s].rearrange("(k p) f -> p k f", p=P)))
            return out

        landed_by = [0] * (W_MOE + SLOTS)
        for c in range(W_MOE + SLOTS):
            landed_by[c] = (landed_by[c - SLOTS] if c >= SLOTS else 0) + 16 * len(parts(c))

        def load_chunks(sp, c0, c1):
            for c in range(c0, c1):
                if c >= SLOTS:
                    sp.wait_ge(used, c - SLOTS + 1)
                for dst, src in parts(c):
                    sp.dma_start(dst, src).then_inc(landed[c % SLOTS], 16)

        def wait_chunk(pe, c):
            pe.wait_ge(landed[c % SLOTS], landed_by[c])

        def chain(eng, s):
            n = [0]

            def link(ins):
                n[0] += 1
                ins.then_inc(s, 1)
                eng.wait_ge(s, n[0])
            return link

        def warm_up(bank):
            for _ in range(9):
                nc.tensor.matmul(bank[:, 0:P], ident[:, :], ident[:, :], start=True, stop=True)

        g_names = ("g_mix", "g_mem_q", "g_mem_kv", "g_ffn")

        def norm_block(tag, src, nt, gi, dst_t, load=None, extra_dram=None, first=False, chunk_range=None, prep=None):
            with ExitStack() as c:
                sq = sb(c, tag + "sq", [P, D])
                ss = sb(c, tag + "ss", [P, nt])
                rs = sb(c, tag + "rs", [P, nt])
                xs = sb(c, tag + "xs", [P, 2, D])
                ld, ssd, msd, rtd, rsd, xsd, trd, evd, ch = (
                    sem(c, tag + n) for n in ("ld", "ssd", "msd", "rtd", "rsd", "xsd", "trd", "evd", "ch"))
                wr = [sem(c, f"{tag}wr{i}") for i in range(2)] if extra_dram is not None else None
                lt = [sem(c, f"{tag}lt{t}") for t in range(nt)] if load is not None else None
                with nc.Block() as block:
                    @block.sync
                    def _(sp):
                        if load is not None:
                            for t in range(nt):
                                sp.dma_start(src[:, t, :], load(t)).then_inc(lt[t], 16)
                        if first:
                            sp.dma_start(ident[:, :], a["c_ident"]).then_inc(ld, 16)
                            for i, n in enumerate(g_names):
                                with nc.allow_non_contiguous_dma("small gain vectors"):
                                    sp.dma_start(gcol[:, i, :], a[n][0].rearrange("(k p) -> p k", p=P)).then_inc(ld, 16)
                        if chunk_range:
                            load_chunks(sp, *chunk_range)
                        if extra_dram is not None:
                            for t in range(nt):
                                sp.wait_ge(xsd, t + 1)
                                sp.dma_start(extra_dram[t * P:(t + 1) * P, :], xs[:, t % 2, :]).then_inc(wr[t % 2], 16)
                            for i in range(2):
                                sp.wait_ge(wr[i], 16 * ((nt + 1 - i) // 2))

                    @block.scalar
                    def _(act):
                        for t in range(nt):
                            if load is not None:
                                act.wait_ge(lt[t], 16)
                            if t:
                                act.wait_ge(ssd, t)
                            nc.scalar.activation(sq[:, :], src[:, t, :], ACT.Square,
                                                 accum_out=ss[:, t:t + 1]).then_inc(ssd, 1)
                        act.wait_ge(msd, 1)
                        nc.scalar.activation(rs[:, :], ss[:, :], ACT.Sqrt).then_inc(rtd, 1)
                        act.wait_ge(rsd, 1)
                        for t in range(nt):
                            if t >= 2:
                                act.wait_ge(trd, t - 1)
                                if extra_dram is not None:
                                    act.wait_ge(wr[t % 2], 16 * (t // 2))
                            nc.scalar.activation(xs[:, t % 2, :], src[:, t, :], ACT.Copy,
                                                 scale=rs[:, t:t + 1]).then_inc(xsd, 1)

                    @block.vector
                    def _(dve):
                        dve.wait_ge(ssd, nt)
                        nc.vector.tensor_scalar(ss[:, :], ss[:, :], 1.0 / D, EPS, ALU.mult, ALU.add).then_inc(msd, 1)
                        dve.wait_ge(rtd, 1)
                        nc.vector.reciprocal(rs[:, :], rs[:, :]).then_inc(rsd, 1)
                        if first:
                            dve.wait_ge(ld, 80)
                        for t in range(nt):
                            dve.wait_ge(trd, t + 1)
                            for h in range(2):
                                ins = nc.vector.tensor_tensor(
                                    dst_t[:, 4 * h:4 * h + 4, t * P:(t + 1) * P],
                                    ps[2 * (t % 2) + h][:, :].rearrange("p (k n) -> p k n", k=4),
                                    gcol[:, gi, 4 * h:4 * h + 4].unsqueeze(2).broadcast_to([P, 4, P]), ALU.mult)
                            ins.then_inc(evd, 1)

                    @block.tensor
                    def _(pe):
                        if first:
                            pe.wait_ge(ld, 80)
                        for t in range(nt):
                            pe.wait_ge(xsd, t + 1)
                            if t >= 2:
                                pe.wait_ge(evd, t - 1)
                            for k in range(KT):
                                ins = nc.tensor.transpose(ps[2 * (t % 2) + k // 4][:, (k % 4) * P:(k % 4 + 1) * P],
                                                          xs[:, t % 2, k * P:(k + 1) * P], ident[:, :])
                            ins.then_inc(trd, 1)

        def project_block(tag, nT, qT, kT, vN, c0, chunk_range, fox, k_out, v_out):
            with ExitStack() as c:
                st = sb(c, tag + "st", [P, 4, 512])
                rt = None if fox else sb(c, tag + "rt", [P, 2, 2, 8, 16])
                cs = None if fox else sb(c, tag + "cs", [P, 2, T, 16])
                mmd, eva, evd, trd, rop, csd, ch = (sem(c, tag + n) for n in ("mmd", "eva", "evd", "trd", "rop", "csd", "ch"))
                kst = [sem(c, f"{tag}kst{i}") for i in range(4)]
                groups = []
                if fox:
                    groups += [("qT", j) for j in range(4)]
                nat = ([] if fox else [("q", t) for t in range(T)]) + [("k", t) for t in range(T)]
                for i, (w, t) in enumerate(nat):
                    groups.append(("mm", w, t, i))
                    if i >= 2:
                        groups.append(("tr",) + nat[i - 2] + (i - 2,))
                vs = [("mm", "v", t, None) for t in range(T)]
                groups += [vs[0], ("tr",) + nat[-2] + (len(nat) - 2,), vs[1], ("tr",) + nat[-1] + (len(nat) - 1,)] + vs[2:]
                chunk_of = {"q": c0, "k": c0 + 1, "v": c0 + 2}
                on_act = [g[0] == "mm" and g[1] != "v" or (g[0] == "tr" and fox and i % 2 == 0) for i, g in enumerate(groups)]
                nact = [sum(on_act[:i + 1]) for i in range(len(groups))]
                ndve = [i + 1 - nact[i] for i in range(len(groups))]
                where = {g[3]: i for i, g in enumerate(groups) if g[0] == "mm" and g[3] is not None}
                trw = {g[3]: i for i, g in enumerate(groups) if g[0] == "tr"}

                def drained(eng, g):
                    if on_act[g]:
                        eng.wait_ge(eva, nact[g])
                    else:
                        eng.wait_ge(evd, ndve[g])

                with nc.Block() as block:
                    @block.sync
                    def _(sp):
                        if not fox:
                            sp.dma_start(cs[:, 0, :, :], a["c_cos"]).then_inc(csd, 16)
                            sp.dma_start(cs[:, 1, :, :], a["c_sin"]).then_inc(csd, 16)
                        load_chunks(sp, *chunk_range)

                    @block.gpsimd
                    def _(pool):
                        for i, (w, t) in enumerate(nat):
                            if w == "k":
                                if fox:
                                    drained(pool, where[i])
                                else:
                                    pool.wait_ge(rop, i + 1)
                                pool.dma_start(k_out(t), st[:, i % 4, :]).then_inc(kst[i % 4], 16)
                        for i, g in enumerate(groups):
                            if g[0] == "mm" and g[1] == "v":
                                drained(pool, i)
                                pool.dma_start(v_out(g[2]), vN[:, g[2], :]).then_inc(stored_v, 16)
                        pool.wait_ge(stored_v, 16 * T * (1 if fox else 2))
                        for i in range(4):
                            n = sum(1 for j, (w, t) in enumerate(nat) if w == "k" and j % 4 == i)
                            pool.wait_ge(kst[i], 16 * n)

                    @block.tensor
                    def _(pe):
                        for g, grp in enumerate(groups):
                            if g >= 4:
                                drained(pe, g - 4)
                            b0, b1 = ps[2 * (g % 4)], ps[2 * (g % 4) + 1]
                            if grp[0] == "qT":
                                j = grp[1]
                                if j == 0:
                                    wait_chunk(pe, c0)
                                w = slot(c0)
                                for k in range(KT):
                                    nc.tensor.matmul(b0[:, :], w[:, k, j * P:(j + 1) * P], nT[:, k, 0:SEQ],
                                                     start=k == 0, stop=k == KT - 1)
                                    ins = nc.tensor.matmul(b1[:, 0:P], w[:, k, j * P:(j + 1) * P], nT[:, k, SEQ:NTOK],
                                                           start=k == 0, stop=k == KT - 1)
                                ins.then_inc(mmd, 1)
                                if j == 3:
                                    pe.wait_ge(mmd, g + 1)
                                    pe.sem_inc(used, 1)
                            elif grp[0] == "mm":
                                _, w, t, _ = grp
                                if t == 0:
                                    wait_chunk(pe, chunk_of[w])
                                wt = slot(chunk_of[w])
                                for k in range(KT):
                                    ins = nc.tensor.matmul(b0[:, :], nT[:, k, t * P:(t + 1) * P], wt[:, k, :],
                                                           start=k == 0, stop=k == KT - 1)
                                ins.then_inc(mmd, 1)
                                if t == T - 1:
                                    pe.wait_ge(mmd, g + 1)
                                    pe.sem_inc(used, 1)
                            else:
                                _, w, t, i = grp
                                if fox:
                                    drained(pe, where[i])
                                else:
                                    pe.wait_ge(rop, i + 1)
                                for j in range(4):
                                    ins = nc.tensor.transpose(b0[:, j * P:(j + 1) * P], st[:, i % 4, j * P:(j + 1) * P],
                                                              ident[:, :])
                                ins.then_inc(mmd, 1)

                    def copy_out(eng, copy, g, grp):
                        eng.wait_ge(mmd, g + 1)
                        b0, b1 = ps[2 * (g % 4)], ps[2 * (g % 4) + 1]
                        if grp[0] == "qT":
                            copy(qT[:, grp[1], 0:SEQ], b0[:, :])
                            return copy(qT[:, grp[1], SEQ:NTOK], b1[:, 0:P])
                        if grp[0] == "mm" and grp[1] == "v":
                            return copy(vN[:, grp[2], :], b0[:, :])
                        if grp[0] == "mm":
                            i = grp[3]
                            if i >= 4:
                                eng.wait_ge(mmd, trw[i - 4] + 1)
                                n = sum(1 for j in range(i - 3) if nat[j][0] == "k" and j % 4 == i % 4)
                                if n:
                                    eng.wait_ge(kst[i % 4], 16 * n)
                            return copy(st[:, i % 4, :], b0[:, :])
                        dst = qT if grp[1] == "q" else kT
                        return copy(dst[:, :, grp[2] * P:(grp[2] + 1) * P], b0[:, :].rearrange("p (j n) -> p j n", j=4))

                    @block.scalar
                    def _(act):
                        for g, grp in enumerate(groups):
                            if on_act[g]:
                                copy_out(act, nc.scalar.copy, g, grp).then_inc(eva, 1)

                    @block.vector
                    def _(dve):
                        link = chain(dve, ch)
                        if not fox:
                            dve.wait_ge(csd, 32)
                        for g, grp in enumerate(groups):
                            if not on_act[g]:
                                copy_out(dve, nc.vector.tensor_copy, g, grp).then_inc(evd, 1)
                            elif not fox:
                                i, t = grp[3], grp[2]
                                drained(dve, g)
                                x = st[:, i % 4, :].rearrange("p (c d) -> p c d", c=8)
                                r = rt[:, i % 2]
                                cosv = cs[:, 0, t, :].unsqueeze(1).broadcast_to([P, 8, 16])
                                sinv = cs[:, 1, t, :].unsqueeze(1).broadcast_to([P, 8, 16])
                                nc.vector.tensor_tensor(r[:, 0], x[:, :, 0:16], cosv, ALU.mult)
                                nc.vector.tensor_tensor(r[:, 1, :, 0:8], x[:, :, 8:16], sinv[:, :, 0:8], ALU.mult)
                                link(nc.vector.tensor_tensor(r[:, 1, :, 8:16], x[:, :, 0:8], sinv[:, :, 8:16], ALU.mult))
                                nc.vector.tensor_tensor(x[:, :, 0:16], r[:, 0], r[:, 1], ALU.add).then_inc(rop, 1)

        def gates_block(nT, RL, RR, CT, L2, bias_l):
            with ExitStack() as c:
                wff = sb(c, "wff", [P, KT, FH])
                bf = sb(c, "bf", [FH, 1])
                z = sb(c, "gz", [FH, NTOK])
                e = sb(c, "ge", [FH, NTOK])
                lf = sb(c, "glf", [FH, NTOK])
                lfN = sb(c, "glfN", [P, T, FH])
                cc = sb(c, "gcc", [FH, 2, SEQ])
                one = sb(c, "gone", [NB * FH, SEQ])
                lc = sb(c, "glc", [P, 2, NB * FH])
                raw = sb(c, "graw", [NB * FH, KS])
                cn = sb(c, "gcn", [NB * FH, TD])
                ld, ldc, ms, mm, zd, ed, fd, cd, ctr, cev, rawd, nw, ch, ach, fin, nd, l2 = (
                    sem(c, "g" + n) for n in ("ld", "ldc", "ms", "mm", "zd", "ed", "fd", "cd", "ctr", "cev", "rawd",
                                              "nw", "ch", "ach", "fin", "nd", "l2"))
                with nc.Block() as block:
                    @block.sync
                    def _(sp):
                        with nc.allow_non_contiguous_dma("narrow gate columns"):
                            sp.dma_start(wff[:, :, :], w_in[:, 1536:1536 + FH].rearrange("(k p) n -> p k n", p=P)).then_inc(ld, 16)
                            sp.dma_start(bf[:, :], a["b_forget"][0].rearrange("(h o) -> h o", o=1)).then_inc(ld, 16)
                            for h in range(2):
                                sp.dma_start(lc[:, h, :].rearrange("p (b f) -> p b f", b=NB),
                                             a["cache_fox_logf"][0, :, h * P:(h + 1) * P, :].rearrange("b p f -> p b f")).then_inc(ldc, 16)
                        sp.dma_start(CT[64:80, :], a["c_tri16"]).then_inc(ldc, 16)
                        sp.dma_start(bias_l[:, :, :], a["c_sel"]).then_inc(ldc, 16)
                        sp.wait_ge(fd, 1)
                        for b in range(NB):
                            sp.dma_start(raw[b * FH:(b + 1) * FH, PAST:KS],
                                         lf[:, SEQ + b * TD:SEQ + (b + 1) * TD]).then_inc(nw, 16)
                        sp.wait_ge(ms, 2)
                        sp.wait_ge(cd, 1)
                        for h in range(FH):
                            p0 = 32 * (h % 4)
                            sp.dma_start(RR[p0:p0 + 1, h // 4, :], cc[h:h + 1, 1, :]).then_inc(fin, 16)
                            sp.dma_start(RL[p0 + 1:p0 + 2, h // 4, :], cc[h:h + 1, 0, :]).then_inc(fin, 16)
                        sp.wait_ge(nd, 1)
                        store(sp, a["p_logf"].rearrange("l b (t p) h -> p (l b t) h", p=P), lfN[:, 0:TP, :])
                        store(sp, a["s_logf"].rearrange("l b q h -> (l b q) h"), lfN[:, TP, :])
                        sp.wait_ge(fin, 16 * 2 * FH)

                    @block.gpsimd
                    def _(pool):
                        nc.gpsimd.memset(RR[:, :, :], 1.0).then_inc(ms, 1)
                        nc.gpsimd.memset(RL[:, :, :], 1.0).then_inc(ms, 1)
                        nc.gpsimd.memset(one[:, :], 1.0).then_inc(ms, 1)

                    @block.tensor
                    def _(pe):
                        pe.wait_ge(ld, 32)
                        for k in range(KT):
                            nc.tensor.matmul(ps[0][0:FH, :], wff[:, k, :], nT[:, k, 0:SEQ], start=k == 0, stop=k == KT - 1)
                            ins = nc.tensor.matmul(ps[1][0:FH, 0:P], wff[:, k, :], nT[:, k, SEQ:NTOK],
                                                   start=k == 0, stop=k == KT - 1)
                        ins.then_inc(mm, 1)
                        pe.wait_ge(ldc, 64)
                        for h in range(2):
                            ins = nc.tensor.transpose(ps[2][0:64, h * P:(h + 1) * P], lc[:, h, :], ident[:, :])
                        ins.then_inc(ctr, 1)
                        pe.wait_ge(fd, 1)
                        for t in range(T):
                            ins = nc.tensor.transpose(ps[3][:, t * FH:(t + 1) * FH], lf[:, t * P:(t + 1) * P],
                                                      ident[0:FH, 0:FH])
                        ins.then_inc(mm, 1)

                    @block.scalar
                    def _(act):
                        link = chain(act, ach)
                        act.wait_ge(zd, 1)
                        link(nc.scalar.activation(e[:, :], z[:, :], ACT.Abs))
                        link(nc.scalar.activation(e[:, :], e[:, :], ACT.Exp, scale=-1.0))
                        nc.scalar.activation(e[:, :], e[:, :], ACT.Ln, bias=1.0).then_inc(ed, 1)

                    @block.vector
                    def _(dve):
                        link = chain(dve, ch)
                        dve.wait_ge(mm, 1)
                        dve.wait_ge(ld, 32)
                        nc.vector.tensor_scalar(z[:, 0:SEQ], ps[0][0:FH, :], bf[:, 0:1], None, ALU.add)
                        nc.vector.tensor_scalar(z[:, SEQ:NTOK], ps[1][0:FH, 0:P], bf[:, 0:1], None, ALU.add).then_inc(zd, 1)
                        dve.wait_ge(ctr, 1)
                        nc.vector.tensor_copy(raw[:, 0:PAST], ps[2][0:64, 0:PAST]).then_inc(rawd, 1)
                        dve.wait_ge(ed, 1)
                        nc.vector.scalar_tensor_tensor(out=lf[:, :], in0=z[:, :], scalar=0.0, in1=e[:, :],
                                                       op0=ALU.min, op1=ALU.subtract).then_inc(fd, 1)
                        dve.wait_ge(fd, 1)
                        dve.wait_ge(ms, 3)
                        link(nc.vector.tensor_tensor_scan(cc[:, 0, :], one[0:FH, :], lf[:, 0:SEQ], 0.0, ALU.mult, ALU.add))
                        link(nc.vector.tensor_scalar(cc[:, 1, :], cc[:, 0, :], -1.0 / SC, None, ALU.mult))
                        nc.vector.tensor_scalar(cc[:, 0, :], cc[:, 0, :], 1.0 / SC, None, ALU.mult).then_inc(cd, 1)
                        dve.wait_ge(nw, 16 * NB)
                        dve.wait_ge(rawd, 1)
                        link(nc.vector.tensor_tensor_scan(CT[0:64, :], one[:, 0:KS], raw[:, :], 0.0, ALU.mult, ALU.add))
                        link(nc.vector.tensor_scalar(cn[:, :], CT[0:64, PAST:KS], -1.0, None, ALU.mult))
                        dve.wait_ge(ldc, 64)
                        for b in range(NB):
                            ins = nc.vector.tensor_tensor(
                                L2[:, b, :].rearrange("p (h q) -> p h q", h=FH),
                                bias_l[0:64, b, :].rearrange("p (h q) -> p h q", h=FH),
                                cn[:, :].unsqueeze(1).broadcast_to([64, FH, TD]), ALU.mult)
                        ins.then_inc(l2, 1)
                        dve.wait_ge(mm, 2)
                        nc.vector.tensor_copy(lfN[:, :, :], ps[3][:, 0:T * FH].rearrange("p (t h) -> p t h", t=T)).then_inc(nd, 1)
                        dve.wait_ge(l2, 1)

        def prompt_attention(tag, kind, qT, kT, vN, outN, outT, RL=None, RR=None, lamcol=None, chunk_range=None, blank=None):
            fox, diff, mem = kind == "fox", kind == "diff", kind == "mem"
            comps = 2 if diff else 1
            heads = FH if fox else DH
            width = {"fox": 64, "diff": 128, "mem": 256}[kind]
            scale = MSC if mem else SC
            units = [(qt, h, cc) for qt in range(TP) for h in range(heads) for cc in range(comps)]
            pairs = [(qt, h) for qt in range(TP) for h in range(heads)]
            nk = (lambda qt: 2) if mem else (lambda qt: qt + 1)
            score_banks = {"fox": (0, 1, 7), "diff": (0, 1, 6, 7), "mem": (0, 1)}[kind]
            ahead = 1 if mem else 2
            nsb = len(score_banks)

            def sbank(u):
                return ps[score_banks[u % nsb]]

            with ExitStack() as c:
                mask = None if mem else sb(c, tag + "mask", [P, P])
                pb = sb(c, tag + "p", [P, 4, 512])
                pt = sb(c, tag + "pt", [P, 2, 512])
                mx = sb(c, tag + "mx", [P, 4])
                rs = sb(c, tag + "rs", [P, len(units)])
                rr = sb(c, tag + "rr", [P, len(units)])
                dg = sb(c, tag + "dg", [P, 4, P]) if diff else None
                on = None if diff else sb(c, tag + "on", [P, heads * width])
                if blank is not None:
                    zero = sb(c, tag + "zero", [P, D])
                    bz, bd = sem(c, tag + "bz"), sem(c, tag + "bd")
                md, sc, mxd, exd, trp, cpd, pvd, rrd, ond, otd, oed, ch, dgd = (
                    sem(c, tag + n) for n in ("md", "sc", "mxd", "exd", "trp", "cpd", "pvd", "rrd", "ond", "otd",
                                              "oed", "ch", "dgd"))

                def obank(qt, h):
                    if mem:
                        return ps[4 + h // 2], (h % 2) * 256
                    return ps[4 + qt % 2], h * width

                with nc.Block() as block:
                    @block.sync
                    def _(sp):
                        if not mem:
                            sp.dma_start(mask[:, :], a["c_causal" if fox else "c_chunk"]).then_inc(md, 16)
                        if chunk_range:
                            load_chunks(sp, *chunk_range)
                        if blank is not None:
                            sp.wait_ge(bz, 1)
                            for i in range(blank.shape[0] // P):
                                sp.dma_start(blank[i * P:(i + 1) * P, :], zero[:, :]).then_inc(bd, 16)
                            sp.wait_ge(bd, 16 * (blank.shape[0] // P))

                    if blank is not None:
                        @block.gpsimd
                        def _(pool):
                            nc.gpsimd.memset(zero[:, :], 0.0).then_inc(bz, 1)

                    @block.tensor
                    def _(pe):
                        def scores(u):
                            qt, h, cc = units[u]
                            n = nk(qt) * P
                            b = sbank(u)
                            if u >= nsb:
                                pe.wait_ge(exd, u - nsb + 1)
                            if mem:
                                for j in range(2):
                                    ins = nc.tensor.matmul(b[:, 0:n], qT[:, 2 * h + j, qt * P:(qt + 1) * P],
                                                           kT[:, 2 * h + j, :], start=j == 0, stop=j == 1)
                            else:
                                x = h if fox else 2 * h + cc
                                r0, j = 64 * (x % 2), x // 2
                                nc.tensor.matmul(b[:, n - P:n], ident[:, :], mask[:, :], start=True, stop=False,
                                                 skip_group_check=True)
                                ins = nc.tensor.matmul(b[:, 0:n], qT[r0:r0 + 64, j, qt * P:(qt + 1) * P],
                                                       kT[r0:r0 + 64, j, 0:n], start=False, stop=not fox,
                                                       skip_group_check=True)
                                if fox:
                                    p0 = 32 * (h % 4)
                                    ins = nc.tensor.matmul(b[:, 0:n], RL[p0:p0 + 2, h // 4, qt * P:(qt + 1) * P],
                                                           RR[p0:p0 + 2, h // 4, 0:n], start=False, stop=True,
                                                           skip_group_check=True)
                            ins.then_inc(sc, 1)

                        def turn(i):
                            qt, h = pairs[i]
                            if i >= 2:
                                pe.wait_ge(cpd, i - 1)
                            b = ps[2 + i % 2]
                            if diff:
                                pe.wait_ge(dgd, i + 1)
                            else:
                                pe.wait_ge(exd, i + 1)
                            for k in range(nk(qt)):
                                if diff:
                                    for cc in range(2):
                                        s = (2 * i + cc) % 4
                                        ins = nc.tensor.matmul(b[:, k * P:(k + 1) * P], pb[:, s, k * P:(k + 1) * P],
                                                               dg[:, s, :], start=cc == 0, stop=cc == 1)
                                else:
                                    ins = nc.tensor.transpose(b[:, k * P:(k + 1) * P], pb[:, i % 4, k * P:(k + 1) * P],
                                                              ident[:, :])
                            ins.then_inc(trp, 1)

                        def values(i):
                            qt, h = pairs[i]
                            pe.wait_ge(cpd, i + 1)
                            b, o = obank(qt, h)
                            if h == 0 and (mem and qt or qt >= 2):
                                pe.wait_ge(ond, qt if mem else qt - 1)
                            for k in range(nk(qt)):
                                ins = nc.tensor.matmul(b[:, o:o + width], pt[:, i % 2, k * P:(k + 1) * P],
                                                       vN[:, k, h * width:(h + 1) * width], start=k == 0,
                                                       stop=k == nk(qt) - 1)
                            ins.then_inc(pvd, 1)
                            if h == heads - 1 and not diff:
                                finish.append(qt)

                        def out_turn(qt):
                            pe.wait_ge(ond, qt + 1)
                            for j in range(heads * width // P):
                                if j % 4 == 0:
                                    n = max(0, 2 * qt + j // 4 - 1) if mem else qt
                                    if n:
                                        pe.wait_ge(oed, n)
                                ins = nc.tensor.transpose(ps[6 if not mem else 6 + j // 4][:, (j % 4) * P:(j % 4 + 1) * P],
                                                          on[:, j * P:(j + 1) * P], ident[:, :])
                                if j % 4 == 3:
                                    ins.then_inc(otd, 1)

                        finish = []
                        if not mem:
                            warm_up(ps[0])
                            pe.wait_ge(md, 16)
                        for u in range(ahead * comps):
                            scores(u)
                        for i in range(len(pairs)):
                            for u in range((i + ahead) * comps, min((i + ahead + 1) * comps, len(units))):
                                scores(u)
                            turn(i)
                            if i:
                                values(i - 1)
                            if len(finish) and i % heads == 2:
                                out_turn(finish.pop(0))
                        values(len(pairs) - 1)
                        if finish:
                            out_turn(finish.pop(0))

                    def copy_pt(act, i):
                        qt, h = pairs[i]
                        act.wait_ge(trp, i + 1)
                        if i >= 2:
                            act.wait_ge(pvd, i - 1)
                        nc.scalar.copy(pt[:, i % 2, 0:nk(qt) * P], ps[2 + i % 2][:, 0:nk(qt) * P]).then_inc(cpd, 1)

                    @block.scalar
                    def _(act):
                        for u, (qt, h, cc) in enumerate(units):
                            n = nk(qt) * P
                            act.wait_ge(mxd, u + 1)
                            if u >= 4:
                                act.wait_ge(trp, (u - 4) // comps + 1)
                            nc.scalar.activation(pb[:, u % 4, 0:n], sbank(u)[:, 0:n], ACT.Exp, bias=mx[:, u % 4:u % 4 + 1],
                                                 scale=scale, accum_out=rs[:, u:u + 1]).then_inc(exd, 1)
                            if u % comps == comps - 1 and u // comps >= 1:
                                copy_pt(act, u // comps - 1)
                        copy_pt(act, len(pairs) - 1)

                    def after_exp(dve, link, u):
                        dve.wait_ge(exd, u + 1)
                        link(nc.vector.reciprocal(rr[:, u:u + 1], rs[:, u:u + 1]))
                        if diff:
                            if u >= 4:
                                dve.wait_ge(trp, (u - 4) // 2 + 1)
                            if u % 2:
                                link(nc.vector.tensor_tensor(rr[:, u:u + 1], rr[:, u:u + 1], lamcol, ALU.mult))
                            ins = nc.vector.tensor_scalar(dg[:, u % 4, :], ident[:, :], rr[:, u:u + 1], None, ALU.mult)
                            if u % 2:
                                ins.then_inc(dgd, 1)

                    @block.vector
                    def _(dve):
                        link = chain(dve, ch)
                        done = [0]

                        def tile_out(qt):
                            dve.wait_ge(pvd, heads * (qt + 1))
                            if diff:
                                nc.vector.tensor_copy(outN[:, qt, :], ps[4 + qt % 2][:, :]).then_inc(ond, 1)
                                return
                            if qt:
                                dve.wait_ge(otd, (heads * width // 512) * qt)
                            u0 = qt * heads
                            half = 1 if not mem else 2
                            for g in range(half):
                                hh = heads // half
                                ins = nc.vector.tensor_tensor(
                                    on[:, g * 512:(g + 1) * 512].rearrange("p (h d) -> p h d", h=hh),
                                    (ps[4 + qt % 2] if not mem else ps[4 + g])[:, :].rearrange("p (h d) -> p h d", h=hh),
                                    rr[:, u0 + g * hh:u0 + (g + 1) * hh].unsqueeze(2).broadcast_to([P, hh, width]), ALU.mult)
                            ins.then_inc(ond, 1)

                        def tile_turned(qt):
                            for g in range(heads * width // 512):
                                dve.wait_ge(otd, (heads * width // 512) * qt + g + 1)
                                nc.vector.tensor_copy(outT[:, 4 * g:4 * g + 4, qt * P:(qt + 1) * P],
                                                      ps[6 + g][:, :].rearrange("p (j n) -> p j n", j=4)).then_inc(oed, 1)

                        todo = []
                        for u, (qt, h, cc) in enumerate(units):
                            n = nk(qt) * P
                            dve.wait_ge(sc, u + 1)
                            if u >= 4:
                                dve.wait_ge(exd, u - 3)
                            link(nc.vector.reduce_max(mx[:, u % 4:u % 4 + 1], sbank(u)[:, 0:n], AX))
                            nc.vector.tensor_scalar(mx[:, u % 4:u % 4 + 1], mx[:, u % 4:u % 4 + 1], -scale, None,
                                                    ALU.mult).then_inc(mxd, 1)
                            if u >= comps:
                                after_exp(dve, link, u - comps)
                            if todo and todo[0][0] <= u:
                                t = todo.pop(0)
                                (tile_out if t[1] == 0 else tile_turned)(t[2])
                            if h == heads - 1 and cc == comps - 1:
                                todo += [(u + 2 * comps, 0, qt)] + ([] if diff else [(u + 4 * comps, 1, qt)])
                        for u in range(len(units) - comps, len(units)):
                            after_exp(dve, link, u)
                        for t in todo:
                            (tile_out if t[1] == 0 else tile_turned)(t[2])

        def decode_attention(tag, kind, qT, kT, vN, outN, c0, bias_l=None, CT=None, L2=None, lamcol=None,
                             chunk_range=None):
            fox, diff, mem = kind == "fox", kind == "diff", kind == "mem"
            J = 8 if mem else 4
            W = 256 if mem else 128
            n = PAST if mem else KS
            kb = 2 if mem else 3
            scale = MSC if mem else SC
            with ExitStack() as c:
                qb = sb(c, tag + "qb", [P, J, NB, 32])
                kt = sb(c, tag + "kt", [P, 2, J, n])
                vn = None if mem else sb(c, tag + "vn", [TD, 2, 512])
                pb = sb(c, tag + "p", [P, 2, n])
                at = sb(c, tag + "at", [P, kb, P])
                ob = sb(c, tag + "o", [P, 2, W])
                mx = sb(c, tag + "mx", [P, NB])
                rs = sb(c, tag + "rs", [P, NB])
                dg = sb(c, tag + "dg", [P, 2, P]) if diff else None
                ones = sb(c, tag + "ones", [64, KS]) if fox else None
                comb = sb(c, tag + "comb", [P, P]) if diff else None
                sgn = sb(c, tag + "sgn", [P, 3]) if diff else None

                def chunk(b):
                    return c0 + (b if mem else b // 2)

                def cached(b, i):
                    if mem:
                        return slot2(chunk(b))[:, 2 * i:2 * i + 2, :]
                    return slot(chunk(b))[:, 4 * (b % 2) + 2 * i:4 * (b % 2) + 2 * i + 2, :]

                vl = [sem(c, f"{tag}vl{i}") for i in range(2)]
                od = [sem(c, f"{tag}od{i}") for i in range(2)]
                qz, qd, tr, eva, evd, kn, sc, mxd, exd, dgd, atd, acp, pvd, ocd, ch, cl = (
                    sem(c, tag + x) for x in ("qz", "qd", "tr", "eva", "evd", "kn", "sc", "mxd", "exd", "dgd", "atd",
                                              "acp", "pvd", "ocd", "ch", "cl"))
                banks = J // 2
                streams_of_chunk = 1 if mem else 2

                def bank(b, g):
                    return ps[g if mem else 2 * (b % 2) + g]

                with nc.Block() as block:
                    @block.sync
                    def _(sp):
                        if diff:
                            sp.dma_start(comb[:, :], a["c_comb"]).then_inc(cl, 16)
                            sp.dma_start(sgn[:, 0:2], a["c_sgn"]).then_inc(cl, 16)
                        if not mem:
                            for b in range(2):
                                sp.dma_start(vn[:, b, :], vN[b * TD:(b + 1) * TD, TP, :]).then_inc(vl[b], 16)
                        next_chunk = chunk_range[0]
                        for b in range(NB):
                            sp.wait_ge(ocd, b + 1)
                            for h in range(8 if fox else 4):
                                p0 = TD * h if fox else 32 * h
                                o0 = (h % 2) * HD if fox else 0
                                w = HD if fox else W
                                sp.dma_start(outN[b * TD:(b + 1) * TD, h * w:(h + 1) * w],
                                             ob[p0:p0 + TD, b % 2, o0:o0 + w]).then_inc(od[b % 2], 16)
                            if b + 2 < NB and not mem:
                                sp.dma_start(vn[:, b % 2, :], vN[(b + 2) * TD:(b + 3) * TD, TP, :]).then_inc(vl[b % 2], 16)
                            if (b + 1) % streams_of_chunk == 0:
                                load_chunks(sp, next_chunk, next_chunk + 1)
                                next_chunk += 1
                        assert next_chunk == chunk_range[1]
                        for s in range(2):
                            sp.wait_ge(od[s], 16 * (8 if fox else 4) * (NB // 2))

                    @block.gpsimd
                    def _(pool):
                        nc.gpsimd.memset(qb[:, :, :, :], 0.0).then_inc(qz, 1)
                        if fox:
                            nc.gpsimd.memset(ones[:, :], 1.0).then_inc(qz, 1)
                        if not mem:
                            for b in range(NB):
                                if b >= 2:
                                    pool.wait_ge(sc, b - 1)
                                nc.gpsimd.tensor_copy(kt[:, b % 2, :, PAST:KS],
                                                      kT[:, :, SEQ + b * TD:SEQ + (b + 1) * TD]).then_inc(kn, 1)

                    @block.tensor
                    def _(pe):
                        def turn_keys(b):
                            wait_chunk(pe, chunk(b))
                            for g in range(banks):
                                before = b - 1 if mem else b - 2
                                if before >= 0:
                                    pe.wait_ge(evd if g % 2 == 0 else eva, (banks // 2) * before + g // 2 + 1)
                                for jj in range(2):
                                    for k in range(2):
                                        ins = nc.tensor.transpose(
                                            bank(b, g)[:, jj * PAST + k * P:jj * PAST + (k + 1) * P],
                                            cached(b, 0)[:, k, (2 * g + jj) * P:(2 * g + jj + 1) * P], ident[:, :])
                                ins.then_inc(tr, 1)

                        def scores(b):
                            pe.wait_ge(evd, (banks // 2) * (b + 1))
                            pe.wait_ge(eva, (banks // 2) * (b + 1))
                            S = ps[4 + b % 2]
                            if b >= 2:
                                pe.wait_ge(exd, b - 1)
                            if not mem:
                                pe.wait_ge(kn, b + 1)
                            for step in range(2 if mem else 1):
                                for j in range(4):
                                    f = 2 * j + step if mem else j
                                    ins = nc.tensor.matmul(S[32 * j:32 * j + 32, 0:n], qb[:, f, b, :],
                                                           kt[:, b % 2, f, :], start=step == 0,
                                                           stop=not fox and step == (1 if mem else 0),
                                                           skip_group_check=True)
                            if fox:
                                nc.tensor.matmul(S[:, 0:n], bias_l[:, b, :], CT[:, :], start=False, stop=False,
                                                 skip_group_check=True)
                                ins = nc.tensor.matmul(S[:, 0:n], L2[:, b, :], ones[:, :], start=False, stop=True,
                                                       skip_group_check=True)
                            ins.then_inc(sc, 1)

                        def turn(b):
                            pe.wait_ge(dgd if diff else exd, b + 1)
                            if b:
                                pe.wait_ge(acp, b)
                            for k in range(kb):
                                m = P if k < 2 else TD
                                ins = nc.tensor.matmul(ps[6][0:m, k * P:(k + 1) * P], pb[:, b % 2, k * P:k * P + m],
                                                       dg[:, b % 2, :] if diff else ident[:, :], start=True, stop=True)
                            ins.then_inc(atd, 1)

                        def values(b):
                            s = b % 2
                            pe.wait_ge(acp, b + 1)
                            if not mem:
                                pe.wait_ge(vl[s], 16 * (b // 2 + 1))
                            if b:
                                pe.wait_ge(ocd, b)
                            for k in range(kb):
                                for j in range(4):
                                    if k < 2:
                                        ins = nc.tensor.matmul(ps[7][32 * j:32 * j + 32, 0:W], at[:, k, 32 * j:32 * j + 32],
                                                               cached(b, 1)[:, k, j * W:(j + 1) * W], start=k == 0,
                                                               stop=k == kb - 1, skip_group_check=True)
                                    else:
                                        ins = nc.tensor.matmul(ps[7][32 * j:32 * j + 32, 0:W],
                                                               at[0:TD, k, 32 * j:32 * j + 32],
                                                               vn[:, s, j * W:(j + 1) * W], start=False, stop=True,
                                                               skip_group_check=True)
                            ins.then_inc(pvd, 1)

                        warm_up(ps[0])
                        pe.wait_ge(qd, 1)
                        if fox:
                            pe.wait_ge(qz, 2)
                        turn_keys(0)
                        scores(0)
                        turn_keys(1)
                        for b in range(NB):
                            if b + 1 < NB:
                                scores(b + 1)
                            if b + 2 < NB:
                                turn_keys(b + 2)
                            if b:
                                values(b - 1)
                            turn(b)
                        values(NB - 1)

                    @block.scalar
                    def _(act):
                        def keys(b):
                            for g in range(1, banks, 2):
                                act.wait_ge(tr, banks * b + g + 1)
                                if b >= 2:
                                    act.wait_ge(sc, b - 1)
                                nc.scalar.copy(kt[:, b % 2, 2 * g:2 * g + 2, 0:PAST],
                                               bank(b, g)[:, :].rearrange("p (j n) -> p j n", j=2)).then_inc(eva, 1)

                        def probabilities(b):
                            act.wait_ge(mxd, b + 1)
                            if b >= 2:
                                act.wait_ge(atd, b - 1)
                            nc.scalar.activation(pb[:, b % 2, :], ps[4 + b % 2][:, 0:n], ACT.Exp, bias=mx[:, b:b + 1],
                                                 scale=scale, accum_out=rs[:, b:b + 1]).then_inc(exd, 1)

                        keys(0)
                        probabilities(0)
                        keys(1)
                        for b in range(NB):
                            if b + 1 < NB:
                                probabilities(b + 1)
                            if b + 2 < NB:
                                keys(b + 2)
                            act.wait_ge(atd, b + 1)
                            if b:
                                act.wait_ge(pvd, b)
                            if not mem:
                                nc.scalar.copy(at[0:TD, 2, :], ps[6][0:TD, 2 * P:3 * P])
                            nc.scalar.copy(at[:, 0:2, :], ps[6][:, 0:2 * P].rearrange("p (k n) -> p k n", k=2)).then_inc(acp, 1)

                    @block.vector
                    def _(dve):
                        link = chain(dve, ch)

                        def keys(b):
                            for g in range(0, banks, 2):
                                dve.wait_ge(tr, banks * b + g + 1)
                                if b >= 2:
                                    dve.wait_ge(sc, b - 1)
                                nc.vector.tensor_copy(kt[:, b % 2, 2 * g:2 * g + 2, 0:PAST],
                                                      bank(b, g)[:, :].rearrange("p (j n) -> p j n", j=2)).then_inc(evd, 1)

                        def out(b):
                            dve.wait_ge(pvd, b + 1)
                            if b >= 2:
                                dve.wait_ge(od[b % 2], 16 * (8 if fox else 4) * (b // 2))
                            if diff:
                                nc.vector.tensor_copy(ob[:, b % 2, :], ps[7][:, 0:W]).then_inc(ocd, 1)
                            else:
                                nc.vector.tensor_scalar(ob[:, b % 2, :], ps[7][:, 0:W], rs[:, b:b + 1], None,
                                                        ALU.mult).then_inc(ocd, 1)
                            if (b + 1) % streams_of_chunk == 0:
                                dve.sem_inc(used, 1)

                        def maxima(b):
                            dve.wait_ge(sc, b + 1)
                            link(nc.vector.reduce_max(mx[:, b:b + 1], ps[4 + b % 2][:, 0:n], AX))
                            nc.vector.tensor_scalar(mx[:, b:b + 1], mx[:, b:b + 1], -scale, None, ALU.mult).then_inc(mxd, 1)

                        def factors(b):
                            dve.wait_ge(exd, b + 1)
                            link(nc.vector.reciprocal(rs[:, b:b + 1], rs[:, b:b + 1]))
                            if diff:
                                link(nc.vector.tensor_tensor(rs[:, b:b + 1], rs[:, b:b + 1], sgn[:, 2:3], ALU.mult))
                                if b >= 2:
                                    dve.wait_ge(atd, b - 1)
                                nc.vector.tensor_scalar(dg[:, b % 2, :], comb[:, :], rs[:, b:b + 1], None,
                                                        ALU.mult).then_inc(dgd, 1)

                        dve.wait_ge(qz, 1)
                        q = qT[:, :, SEQ:NTOK].rearrange("p j (b t) -> p j b t", b=NB)
                        if mem:
                            for j in range(J):
                                ins = nc.vector.tensor_copy(qb[:, j, :, 0:TD], q[:, j])
                        else:
                            for j in range(J):
                                nc.vector.tensor_copy(qb[0:64, j, :, 0:TD], q[0:64, j])
                                ins = nc.vector.tensor_copy(qb[64:P, j, :, TD:32], q[64:P, j])
                        ins.then_inc(qd, 1)
                        if diff:
                            dve.wait_ge(cl, 32)
                            link(nc.vector.scalar_tensor_tensor(out=sgn[:, 2:3], in0=sgn[:, 1:2], scalar=lamcol,
                                                                in1=sgn[:, 0:1], op0=ALU.mult, op1=ALU.add))
                        keys(0)
                        maxima(0)
                        keys(1)
                        factors(0)
                        for b in range(NB):
                            if b + 1 < NB:
                                maxima(b + 1)
                            if b + 2 < NB:
                                keys(b + 2)
                            if b:
                                out(b - 1)
                            if b + 1 < NB:
                                factors(b + 1)
                        out(NB - 1)

        def mix_block(foxN, diffN, mixT, chunk_range):
            with ExitStack() as c:
                sq = sb(c, "msq", [P, T, 512])
                ss = sb(c, "mss", [P, T * DH])
                gd = sb(c, "mgd", [P, P])
                sqd, ssd, sr, rd, nd, tr, ev, ld, ch = (sem(c, "m" + n) for n in ("sqd", "ssd", "sr", "rd", "nd", "tr",
                                                                                  "ev", "ld", "ch"))
                with nc.Block() as block:
                    @block.sync
                    def _(sp):
                        sp.dma_start(gd[:, :], a["g_diff"].partition_broadcast(P).rearrange("p l d -> p (l d)")).then_inc(ld, 16)
                        load_chunks(sp, *chunk_range)
                        sp.wait_ge(ld, 16)

                    @block.scalar
                    def _(act):
                        nc.scalar.activation(sq[:, :, :], diffN[:, :, :], ACT.Square).then_inc(sqd, 1)
                        act.wait_ge(ssd, 1)
                        nc.scalar.activation(ss[:, :], ss[:, :], ACT.Sqrt).then_inc(sr, 1)

                    @block.vector
                    def _(dve):
                        link = chain(dve, ch)
                        dve.wait_ge(sqd, 1)
                        link(nc.vector.reduce_sum(ss[:, :], sq[:, :, :].rearrange("p t (h d) -> p (t h) d", h=DH), AX))
                        nc.vector.tensor_scalar(ss[:, :], ss[:, :], 1.0 / 128, EPS, ALU.mult, ALU.add).then_inc(ssd, 1)
                        dve.wait_ge(ld, 16)
                        link(nc.vector.tensor_scalar(gd[:, :], gd[:, :], 1.0 - LAM_INIT, None, ALU.mult))
                        dve.wait_ge(sr, 1)
                        link(nc.vector.reciprocal(ss[:, :], ss[:, :]))
                        for t in range(T):
                            x = diffN[:, t, :].rearrange("p (h d) -> p h d", h=DH)
                            link(nc.vector.tensor_tensor(x, x, ss[:, t * DH:(t + 1) * DH].unsqueeze(2).broadcast_to([P, DH, P]),
                                                         ALU.mult))
                            nc.vector.tensor_tensor(x, x, gd[:, :].unsqueeze(1).broadcast_to([P, DH, P]), ALU.mult).then_inc(nd, 1)
                        for i in range(T + 1):
                            dve.wait_ge(tr, i + 1)
                            j0, t = (0, TP) if i == 0 else (4, i - 1)
                            nc.vector.tensor_copy(mixT[:, j0:j0 + 4, t * P:(t + 1) * P],
                                                  ps[i % 2][:, :].rearrange("p (j n) -> p j n", j=4)).then_inc(ev, 1)

                    @block.tensor
                    def _(pe):
                        for i in range(T + 1):
                            if i:
                                pe.wait_ge(nd, i)
                            if i >= 2:
                                pe.wait_ge(ev, i - 1)
                            src = foxN if i == 0 else diffN[:, i - 1, :]
                            for j in range(4):
                                ins = nc.tensor.transpose(ps[i % 2][:, j * P:(j + 1) * P], src[:, j * P:(j + 1) * P],
                                                          ident[:, :])
                            ins.then_inc(tr, 1)

        def residual_block(tag, xT, hN, c0, chunk_range, load=None):
            with ExitStack() as c:
                mm, ev = sem(c, tag + "mm"), sem(c, tag + "ev")
                ld = [sem(c, f"{tag}ld{t}") for t in range(T)]
                groups = [(half, t) for half in range(2) for t in range(T)]
                with nc.Block() as block:
                    @block.sync
                    def _(sp):
                        if load is not None:
                            for t in range(T):
                                sp.dma_start(hN[:, t, :], load(t)).then_inc(ld[t], 16)
                        load_chunks(sp, *chunk_range)

                    @block.tensor
                    def _(pe):
                        for g, (half, t) in enumerate(groups):
                            if t == 0:
                                wait_chunk(pe, c0 + half)
                            if g >= 8:
                                pe.wait_ge(ev, g - 7)
                            for k in range(KT):
                                ins = nc.tensor.matmul(ps[g % 8][:, :], xT[:, k, t * P:(t + 1) * P],
                                                       slot(c0 + half)[:, k, :], start=k == 0, stop=k == KT - 1)
                            ins.then_inc(mm, 1)
                            if t == T - 1:
                                pe.wait_ge(mm, g + 1)
                                pe.sem_inc(used, 1)

                    @block.vector
                    def _(dve):
                        for g, (half, t) in enumerate(groups):
                            dve.wait_ge(mm, g + 1)
                            if load is not None:
                                dve.wait_ge(ld[t], 16)
                            h = hN[:, t, half * 512:(half + 1) * 512]
                            nc.vector.tensor_tensor(h, ps[g % 8][:, :], h, ALU.add).then_inc(ev, 1)

        def memory_block(mT, mkT, mvN, chunk_range):
            with ExitStack() as c:
                mkN = sb(c, "mkN", [P, 2, D])
                mm, ev = sem(c, "kmm"), sem(c, "kev")
                out = [a["p_mk"], a["p_mv"]]
                groups = [("mm", m, half, t) for m in range(2) for half in range(2) for t in range(2)]
                groups = groups[:4] + groups[4:] + [("tr", t, half) for t in range(2) for half in range(2)]
                with nc.Block() as block:
                    @block.sync
                    def _(sp):
                        load_chunks(sp, *chunk_range)
                        for m, buf in enumerate((mkN, mvN)):
                            sp.wait_ge(ev, 4 * m + 4)
                            store(sp, out[m].rearrange("l b (k p) h d -> p (l b k) (h d)", p=P), buf[:, :, :])
                        sp.wait_ge(stored, ns[0])

                    @block.tensor
                    def _(pe):
                        for g, grp in enumerate(groups):
                            if g >= 8:
                                pe.wait_ge(ev, g - 7)
                            if grp[0] == "mm":
                                _, m, half, t = grp
                                ch = (W_MK, W_MV)[m] + half
                                if t == 0:
                                    wait_chunk(pe, ch)
                                for k in range(KT):
                                    ins = nc.tensor.matmul(ps[g % 8][:, :], mT[:, k, t * P:(t + 1) * P], slot(ch)[:, k, :],
                                                           start=k == 0, stop=k == KT - 1)
                            else:
                                _, t, half = grp
                                pe.wait_ge(ev, 4)
                                for j in range(4):
                                    o = half * 512 + j * P
                                    ins = nc.tensor.transpose(ps[g % 8][:, j * P:(j + 1) * P], mkN[:, t, o:o + P], ident[:, :])
                            ins.then_inc(mm, 1)
                            if grp[0] == "mm" and grp[3] == 1:
                                pe.wait_ge(mm, g + 1)
                                pe.sem_inc(used, 1)

                    @block.vector
                    def _(dve):
                        for g, grp in enumerate(groups):
                            dve.wait_ge(mm, g + 1)
                            if grp[0] == "mm":
                                _, m, half, t = grp
                                dst, src = (mkN, mvN)[m][:, t, half * 512:(half + 1) * 512], ps[g % 8][:, :]
                            else:
                                _, t, half = grp
                                dst = mkT[:, 4 * half:4 * half + 4, t * P:(t + 1) * P]
                                src = ps[g % 8][:, :].rearrange("p (j n) -> p j n", j=4)
                            nc.vector.tensor_copy(dst, src).then_inc(ev, 1)

        def query_block(nT, qT, chunk_range):
            with ExitStack() as c:
                mm, eva, evd = sem(c, "qmm"), sem(c, "qeva"), sem(c, "qevd")
                with nc.Block() as block:
                    @block.sync
                    def _(sp):
                        load_chunks(sp, *chunk_range)

                    @block.tensor
                    def _(pe):
                        for g in range(KT):
                            if g % 4 == 0:
                                wait_chunk(pe, W_MQ + g // 4)
                            if g >= 4:
                                pe.wait_ge(eva, g - 3)
                                pe.wait_ge(evd, g - 3)
                            w = slot(W_MQ + g // 4)
                            j = g % 4
                            for k in range(KT):
                                nc.tensor.matmul(ps[2 * (g % 4)][:, :], w[:, k, j * P:(j + 1) * P], nT[:, k, 0:SEQ],
                                                 start=k == 0, stop=k == KT - 1)
                                ins = nc.tensor.matmul(ps[2 * (g % 4) + 1][:, 0:P], w[:, k, j * P:(j + 1) * P],
                                                       nT[:, k, SEQ:NTOK], start=k == 0, stop=k == KT - 1)
                            ins.then_inc(mm, 1)
                            if j == 3:
                                pe.wait_ge(mm, g + 1)
                                pe.sem_inc(used, 1)

                    @block.scalar
                    def _(act):
                        for g in range(KT):
                            act.wait_ge(mm, g + 1)
                            nc.scalar.copy(qT[:, g, 0:SEQ], ps[2 * (g % 4)][:, :]).then_inc(eva, 1)

                    @block.vector
                    def _(dve):
                        for g in range(KT):
                            dve.wait_ge(mm, g + 1)
                            nc.vector.tensor_copy(qT[:, g, SEQ:NTOK], ps[2 * (g % 4) + 1][:, 0:P]).then_inc(evd, 1)

        def turn_block(xN, dstT):
            with ExitStack() as c:
                tr, ev = sem(c, "ttr"), sem(c, "tev")
                with nc.Block() as block:
                    @block.tensor
                    def _(pe):
                        for k in range(KT):
                            ins = nc.tensor.transpose(ps[k // 4][:, (k % 4) * P:(k % 4 + 1) * P], xN[:, k * P:(k + 1) * P],
                                                      ident[:, :])
                        ins.then_inc(tr, 1)

                    @block.vector
                    def _(dve):
                        dve.wait_ge(tr, 1)
                        for h in range(2):
                            ins = nc.vector.tensor_copy(dstT[:, 4 * h:4 * h + 4, SEQ:NTOK],
                                                        ps[h][:, :].rearrange("p (k n) -> p k n", k=4))
                        ins.then_inc(ev, 1)
                        dve.wait_ge(ev, 1)

        def lambda_block(lamcol, chunk_range):
            with ExitStack() as c:
                lv = sb(c, "lv", [P, 4, HD])
                pr = sb(c, "lpr", [P, 2, HD])
                s = sb(c, "ls", [P, 2])
                ld, ch, ed, sd = (sem(c, "l" + n) for n in ("ld", "ch", "ed", "sd"))
                with nc.Block() as block:
                    @block.sync
                    def _(sp):
                        for i, n in enumerate(("lam_q1", "lam_q2", "lam_k1", "lam_k2")):
                            sp.dma_start(lv[:, i, :], a[n].partition_broadcast(P).rearrange("p l d -> p (l d)")).then_inc(ld, 16)
                        load_chunks(sp, *chunk_range)

                    @block.vector
                    def _(dve):
                        link = chain(dve, ch)
                        dve.wait_ge(ld, 64)
                        link(nc.vector.tensor_tensor(pr[:, :, :], lv[:, 0:2, :], lv[:, 2:4, :], ALU.mult))
                        nc.vector.reduce_sum(s[:, :], pr[:, :, :], AX).then_inc(sd, 1)
                        dve.wait_ge(ed, 1)
                        link(nc.vector.tensor_tensor(lamcol, s[:, 1:2], s[:, 0:1], ALU.subtract))
                        link(nc.vector.tensor_scalar(lamcol, lamcol, -LAM_INIT, None, ALU.add))

                    @block.scalar
                    def _(act):
                        act.wait_ge(sd, 1)
                        nc.scalar.activation(s[:, :], s[:, :], ACT.Exp).then_inc(ed, 1)

        def route_block(nT, xg, gate, slots, idx, plan, tab):
            with ExitStack() as c:
                wr = sb(c, "wr", [P, KT, NG + NE])
                br = sb(c, "br", [P, NG + NE])
                cst = sb(c, "cst", [P, 128])
                tri = sb(c, "tri", [P, P])
                trib = sb(c, "trib", [P, P], BF16)
                oneb = sb(c, "oneb", [P, P], BF16)
                L = sb(c, "rL", [P, T, NG + NE])
                s5 = sb(c, "s5", [P, 12, T])
                g4 = sb(c, "g4", [P, 3, T, NG])
                Lm = sb(c, "Lm", [P, T, NG, EPG])
                e8 = sb(c, "e8", [P, 8, T, EPG])
                oh = sb(c, "oh", [P, 2, T, NE])
                pr = sb(c, "rpr", [P, 2, T, NE])
                M = sb(c, "rM", [P, T, NE], BF16)
                rk = sb(c, "rrk", [P, 4, 2, T])
                ov = sb(c, "rov", [P, 3, NE])
                bp = sb(c, "rbp", [P, 4, PAIRS])
                cmp = sb(c, "rcmp", [P, PAIRS, MAXB - 1])
                plx = sb(c, "rplx", [1, NBLK, PAIRS])
                pls = sb(c, "rpls", [1, NBLK])
                one32 = sb(c, "one32", [P, NE])
                ii = sb(c, "rii", [P, 4, 2, T], I32)
                addr = sb(c, "raddr", [P, 2 * T], U32)
                tok = sb(c, "rtok", [P, T], I32)
                blank = sb(c, "blank", [P, NBLK], U32)
                ld, mm, ex, exd, md, rd, pz, tin, sd, sc, ch, ach, ixl = (
                    sem(c, "r" + n) for n in ("ld", "mm", "ex", "exd", "md", "rd", "pz", "tin", "sd", "sc", "ch", "ach", "ixl"))
                with nc.Block() as block:
                    @block.sync
                    def _(sp):
                        with nc.allow_non_contiguous_dma("narrow router"):
                            sp.dma_start(wr[:, :, 0:NG], a["w_group"][0].rearrange("(k p) n -> p k n", p=P)).then_inc(ld, 16)
                            sp.dma_start(wr[:, :, NG:], a["w_erouter"][0].rearrange("(k p) n -> p k n", p=P)).then_inc(ld, 16)
                            sp.dma_start(br[:, 0:NG], a["b_group"].partition_broadcast(P).rearrange("p l d -> p (l d)")).then_inc(ld, 16)
                            sp.dma_start(br[:, NG:], a["b_erouter"].partition_broadcast(P).rearrange("p l d -> p (l d)")).then_inc(ld, 16)
                        sp.dma_start(cst[:, :], a["c_route"]).then_inc(ld, 16)
                        sp.dma_start(tri[:, :], a["c_tri"]).then_inc(ld, 16)
                        sp.dma_start(tok[:, :], a["c_tok"]).then_inc(ld, 16)
                        sp.wait_ge(pz, 2)
                        sp.dma_start(tab.rearrange("(p c) o -> p (c o)", p=P), blank[:, :]).then_inc(tin, 16)
                        sp.wait_ge(sc, 16 * 2 * T)
                        sp.dma_start(idx[:, :], tab.rearrange("(p c) o -> p (c o)", p=P)).then_inc(ixl, 16)
                        sp.wait_ge(ixl, 16)

                    @block.gpsimd
                    def _(pool):
                        nc.gpsimd.memset(oneb[:, :], 1.0).then_inc(pz, 1)
                        nc.gpsimd.memset(blank[:, :], 2 * NTOK).then_inc(pz, 1)
                        nc.gpsimd.memset(one32[:, :], 1.0).then_inc(pz, 1)
                        nc.gpsimd.memset(xg[:, :], 0.0).then_inc(pz, 1)
                        pool.wait_ge(tin, 16)
                        pool.wait_ge(ld, 112)
                        pool.wait_ge(sd, 1)
                        for k in range(2):
                            for t in range(T):
                                pool.indirect_dma_start(
                                    out=tab, out_offset=bass.IndirectOffsetOnAxis(ap=addr[:, k * T + t:k * T + t + 1], axis=0),
                                    in_=tok[:, t:t + 1], in_offset=None).then_inc(sc, 16)
                        pool.wait_ge(pz, 4)

                    @block.tensor
                    def _(pe):
                        pe.wait_ge(ld, 112)
                        for t in range(T):
                            for k in range(KT):
                                ins = nc.tensor.matmul(ps[0][:, t * 36:(t + 1) * 36], nT[:, k, t * P:(t + 1) * P], wr[:, k, :],
                                                       start=k == 0, stop=k == KT - 1)
                        ins.then_inc(mm, 1)
                        pe.wait_ge(md, 1)
                        pe.wait_ge(pz, 1)
                        for t in range(T):
                            for u in range(t + 1):
                                nc.tensor.matmul(ps[1][:, t * NE:(t + 1) * NE], (trib if u == t else oneb)[:, :], M[:, u, :],
                                                 start=u == 0, stop=u == t)
                        for t in range(T):
                            ins = nc.tensor.matmul(ps[2][:, 0:NE], oneb[:, :], M[:, t, :], start=t == 0, stop=t == T - 1)
                        ins.then_inc(mm, 1)

                    @block.scalar
                    def _(act):
                        act.wait_ge(ex, 1)
                        nc.scalar.activation(g4[:, 1], g4[:, 0], ACT.Exp).then_inc(exd, 1)
                        act.wait_ge(ex, 2)
                        nc.scalar.activation(e8[:, 1], e8[:, 0], ACT.Exp).then_inc(exd, 1)

                    @block.vector
                    def _(dve):
                        link = chain(dve, ch)
                        v = nc.vector
                        def bc(x, n):
                            return x.unsqueeze(2).broadcast_to([P, T, n])

                        def first(dst, src, top, w, n, eq, tmp):
                            link(v.tensor_tensor(eq, src, bc(top, n), ALU.is_equal))
                            link(v.tensor_tensor(eq, eq, w.unsqueeze(1).broadcast_to([P, T, n]), ALU.mult))
                            link(v.reduce_max(tmp, eq, AX))
                            link(v.tensor_tensor(dst, eq, bc(tmp, n), ALU.is_equal))

                        dve.wait_ge(ld, 112)
                        link(v.tensor_copy(trib[:, :], tri[:, :]))
                        dve.wait_ge(mm, 1)
                        link(v.tensor_tensor(L[:, :, :], ps[0][:, 0:T * 36].rearrange("p (t n) -> p t n", t=T),
                                             br[:, :].unsqueeze(1).broadcast_to([P, T, 36]), ALU.add))
                        g = L[:, :, 0:NG]
                        link(v.reduce_max(s5[:, 0], g, AX))
                        v.tensor_tensor(g4[:, 0], g, bc(s5[:, 0], NG), ALU.subtract).then_inc(ex, 1)
                        first(g4[:, 2], g, s5[:, 0], cst[:, 0:4], NG, e8[:, 7, :, 0:4], s5[:, 1])
                        dve.wait_ge(exd, 1)
                        link(v.reduce_sum(s5[:, 2], g4[:, 1], AX))
                        link(v.reciprocal(s5[:, 3], s5[:, 2]))
                        link(v.tensor_tensor(Lm[:, :, :, :], L[:, :, NG:].rearrange("p t (g j) -> p t g j", g=NG),
                                             g4[:, 2].unsqueeze(3).broadcast_to([P, T, NG, EPG]), ALU.mult))
                        link(v.reduce_sum(e8[:, 2], Lm[:, :, :, :].rearrange("p t g j -> p t j g"), AX))
                        link(v.reduce_max(s5[:, 4], e8[:, 2], AX))
                        v.tensor_tensor(e8[:, 0], e8[:, 2], bc(s5[:, 4], EPG), ALU.subtract).then_inc(ex, 1)
                        dve.wait_ge(exd, 2)
                        link(v.reduce_sum(s5[:, 5], e8[:, 1], AX))
                        link(v.reciprocal(s5[:, 5], s5[:, 5]))
                        link(v.tensor_tensor(e8[:, 3], e8[:, 1], bc(s5[:, 5], EPG), ALU.mult))
                        link(v.reduce_max(s5[:, 6], e8[:, 3], AX))
                        first(e8[:, 4], e8[:, 3], s5[:, 6], cst[:, 4:12], EPG, e8[:, 7], s5[:, 1])
                        link(v.scalar_tensor_tensor(out=e8[:, 6], in0=e8[:, 4], scalar=-2.0, in1=e8[:, 3], op0=ALU.mult,
                                                    op1=ALU.add))
                        link(v.reduce_max(s5[:, 7], e8[:, 6], AX))
                        first(e8[:, 5], e8[:, 6], s5[:, 7], cst[:, 4:12], EPG, e8[:, 7], s5[:, 1])
                        for k in range(2):
                            ins = v.tensor_tensor(oh[:, k].rearrange("p t (g j) -> p t g j", g=NG),
                                                  g4[:, 2].unsqueeze(3).broadcast_to([P, T, NG, EPG]),
                                                  e8[:, 4 + k].unsqueeze(2).broadcast_to([P, T, NG, EPG]), ALU.mult)
                        link(ins)
                        v.tensor_tensor(M[:, :, :], oh[:, 0], oh[:, 1], ALU.add).then_inc(md, 1)
                        link(v.tensor_tensor(s5[:, 8], s5[:, 6], s5[:, 7], ALU.add))
                        link(v.reciprocal(s5[:, 8], s5[:, 8]))
                        link(v.tensor_tensor(s5[:, 9:11], s5[:, 6:8], s5[:, 3].unsqueeze(1).broadcast_to([P, 2, T]), ALU.mult))
                        link(v.tensor_tensor(gate[:, :, :], s5[:, 9:11], s5[:, 8].unsqueeze(1).broadcast_to([P, 2, T]), ALU.mult))
                        dve.wait_ge(mm, 2)
                        dve.wait_ge(pz, 3)
                        link(v.tensor_copy(ov[:, 0], ps[2][:, 0:NE]))
                        link(v.reduce_max(bp[:, 0], ov[:, 0].rearrange("p (n x) -> p n x", x=2), AX))
                        link(v.tensor_tensor(cmp[:, :, :], bp[:, 0].unsqueeze(2).broadcast_to([P, PAIRS, MAXB - 1]),
                                             cst[:, 44:44 + MAXB - 1].unsqueeze(1).broadcast_to([P, PAIRS, MAXB - 1]),
                                             ALU.is_gt))
                        link(v.reduce_sum(bp[:, 1], cmp[:, :, :], AX))
                        link(v.tensor_scalar(bp[:, 1], bp[:, 1], 1.0, None, ALU.add))
                        link(v.tensor_tensor_scan(bp[:, 2], one32[:, 0:PAIRS], bp[:, 1], 0.0, ALU.mult, ALU.add))
                        link(v.tensor_tensor(bp[:, 3], bp[:, 2], bp[:, 1], ALU.subtract))
                        link(v.tensor_scalar(bp[:, 3], bp[:, 3], float(P), None, ALU.mult))
                        link(v.tensor_tensor(ov[:, 1].rearrange("p (n x) -> p n x", x=2),
                                             cst[:, 12:44].rearrange("p (n x) -> p n x", x=2),
                                             bp[:, 3].unsqueeze(2).broadcast_to([P, PAIRS, 2]), ALU.add))
                        for i, src in enumerate((ps[1][:, 0:T * NE].rearrange("p (t e) -> p t e", t=T),
                                                 ov[:, 1].unsqueeze(1).broadcast_to([P, T, NE]))):
                            for k in range(2):
                                ins = v.tensor_tensor(pr[:, k], oh[:, k], src, ALU.mult)
                            link(ins)
                            link(v.reduce_sum(rk[:, i], pr[:, :, :, :], AX))
                        link(v.tensor_copy(ii[:, 0], rk[:, 0]))
                        link(v.tensor_scalar(ii[:, 1], ii[:, 0], CAP.bit_length() - 1, CAP.bit_length() - 1,
                                             ALU.logical_shift_right, ALU.logical_shift_left))
                        link(v.tensor_tensor(rk[:, 0], rk[:, 0], rk[:, 1], ALU.add))
                        link(v.tensor_tensor(rk[:, 0], rk[:, 0], ii[:, 1], ALU.add))
                        link(v.tensor_copy(slots[:, :], rk[:, 0].rearrange("p k t -> p (k t)")))
                        link(v.tensor_copy(ii[:, 0], rk[:, 0]))
                        link(v.tensor_scalar(ii[:, 1], ii[:, 0], P - 1, None, ALU.bitwise_and))
                        link(v.tensor_scalar(ii[:, 2], ii[:, 0], 7, None, ALU.logical_shift_right))
                        v.scalar_tensor_tensor(out=addr[:, :], in0=ii[:, 1].rearrange("p k t -> p (k t)"), scalar=float(NBLK),
                                               in1=ii[:, 2].rearrange("p k t -> p (k t)"), op0=ALU.mult,
                                               op1=ALU.add).then_inc(sd, 1)
                        link(v.tensor_tensor(plx[:, :, :], bp[0:1, 2].unsqueeze(1).broadcast_to([1, NBLK, PAIRS]),
                                             cst[0:1, 53:53 + NBLK].unsqueeze(2).broadcast_to([1, NBLK, PAIRS]), ALU.is_le))
                        link(v.reduce_sum(pls[:, :], plx[:, :, :], AX))
                        link(v.tensor_copy(plan[:, 0:NBLK], pls[:, :]))
                        link(v.tensor_copy(plan[:, NBLK:NBLK + PAIRS], bp[0:1, 2]))
                        link(v.tensor_scalar(plan[:, NBLK + PAIRS:], bp[0:1, 2, PAIRS - 1:], 1.0, None, ALU.subtract))

        def expert_block(xg, idx, xs, ys, plan):
            with ExitStack() as c:
                xT = sb(c, "xT", [P, KT, P])
                sg = sb(c, "sg", [P, 512])
                hh = sb(c, "hh", [P, 512])
                hT = sb(c, "hT", [P, ET, P])
                yb = sb(c, "yb", [P, D])
                ix = sb(c, "ix", [P, 2], U32)
                copied, gathered, turned, xT_ready, w1_done, w3_done, silu_done, hid_done, hid_turned, hT_ready, w2_done, \
                    out_ready, out_stored, waited, all_stored = (sem(c, "e_" + n) for n in (
                        "copied", "gathered", "turned", "xT_ready", "w1_done", "w3_done", "silu_done", "hid_done",
                        "hid_turned", "hT_ready", "w2_done", "out_ready", "out_stored", "waited", "all_stored"))

                def w(j):
                    return slot(W_MOE + j) if j < 4 else slot2(W_MOE + j)

                def blocks(eng, first, body):
                    first()
                    n = eng.value_load(plan[0:1, NBLK + PAIRS - 1:NBLK + PAIRS], min_val=PAIRS, max_val=NBLK)
                    with eng.Fori(1, n) as q:
                        body(q)
                    return n

                with nc.Block() as block:
                    @block.sync
                    def _(sp):
                        with sp.Fori(0, PAIRS - 1) as p:
                            end = sp.value_load(plan[0:1, bass.ds(p + NBLK, 1)], min_val=1, max_val=NBLK)
                            for j in range(6):
                                if j % 2 == 0:
                                    sp.wait_ge((w1_done, w3_done, w2_done)[j // 2], end)
                                src = a["w1" if j < 2 else "w3" if j < 4 else "w2"][0][bass.ds(p * 2 + (2 + j % 2), 1)]
                                sp.dma_start(w(j), src.rearrange("a (k p) n -> p (a k) n", p=P)).then_inc(
                                    landed[(W_MOE + j) % SLOTS], 16)

                    @block.gpsimd
                    def _(pool):
                        bound = pool.to_reg(NTOK - 1)

                        def gather(q, column):
                            nc.gpsimd.tensor_copy(ix[:, 0:1], column).then_inc(copied, 1)
                            pool.wait_ge(copied, q + 1)
                            pool.sem_inc(waited, 1)
                            pool.indirect_dma_start(out=xg[:, :], out_offset=None, in_=xs,
                                                    in_offset=bass.IndirectOffsetOnAxis(ap=ix[:, 0:1], axis=0),
                                                    bounds_check=bound, oob_is_err=False).then_inc(gathered, 16)

                        def body(q):
                            pool.wait_ge(turned, q)
                            gather(q, idx[:, bass.ds(q, 1)])
                        blocks(pool, lambda: gather(0, idx[:, 0:1]), body)

                    @block.tensor
                    def _(pe):
                        def turn(q):
                            pe.wait_ge(gathered, q * 16 + 16)
                            for k in range(KT):
                                ins = nc.tensor.transpose(ps[k // 4][:, (k % 4) * P:(k % 4 + 1) * P], xg[:, k * P:(k + 1) * P],
                                                          ident[:, :])
                            ins.then_inc(turned, 1)

                        def up(q, pair):
                            pe.wait_ge(xT_ready, q + 1)
                            for m in range(2):
                                for x in range(2):
                                    c = W_MOE + 2 * m + x
                                    pe.wait_ge(landed[c % SLOTS], pair * 16 + landed_by[c])
                                for k in range(KT):
                                    for x in range(2):
                                        ins = nc.tensor.matmul(ps[2 + m][64 * x:64 * x + 64, :], xT[:, k, 64 * x:64 * x + 64],
                                                               w(2 * m + x)[:, k, :], start=k == 0, stop=k == KT - 1)
                                ins.then_inc((w1_done, w3_done)[m], 1)

                        def down(q, pair, free):
                            pe.wait_ge(hid_done, q + 1)
                            for k in range(ET):
                                ins = nc.tensor.transpose(ps[4][:, k * P:(k + 1) * P], hh[:, k * P:(k + 1) * P], ident[:, :])
                            ins.then_inc(hid_turned, 1)
                            for x in range(2):
                                c = W_MOE + 4 + x
                                pe.wait_ge(landed[c % SLOTS], pair * 16 + landed_by[c])
                            pe.wait_ge(hT_ready, q + 1)
                            if free is not None:
                                pe.wait_ge(out_ready, free)
                            for half in range(2):
                                for k in range(ET):
                                    for x in range(2):
                                        ins = nc.tensor.matmul(ps[5 + half][64 * x:64 * x + 64, :], hT[:, k, 64 * x:64 * x + 64],
                                                               w(4 + x)[:, k, half * 512:(half + 1) * 512], start=k == 0,
                                                               stop=k == ET - 1)
                            ins.then_inc(w2_done, 1)

                        warm_up(ps[0])
                        turn(0)
                        up(0, 0)
                        last = pe.value_load(plan[0:1, NBLK + PAIRS:NBLK + PAIRS + 1], min_val=PAIRS - 1, max_val=NBLK - 1)
                        pair1 = pe.value_load(plan[0:1, 1:2], min_val=0, max_val=PAIRS - 1)
                        turn(1)
                        down(0, 0, None)
                        up(1, pair1)
                        with pe.Fori(1, last) as q:
                            before = pe.value_load(plan[0:1, bass.ds(q, 1)], min_val=0, max_val=PAIRS - 1)
                            turn(q + 1)
                            down(q, before, q)
                            pair = pe.value_load(plan[0:1, bass.ds(q + 1, 1)], min_val=0, max_val=PAIRS - 1)
                            up(q + 1, pair)
                        down(last, PAIRS - 1, last)

                    @block.scalar
                    def _(act):
                        def silu(q):
                            act.wait_ge(w1_done, q + 1)
                            nc.scalar.activation(sg[:, :], ps[2][:, :], ACT.Silu).then_inc(silu_done, 1)

                        def hidden(q):
                            act.wait_ge(hid_turned, q + 1)
                            nc.scalar.copy(hT[:, :, :], ps[4][:, :].rearrange("p (k n) -> p k n", k=ET)).then_inc(hT_ready, 1)

                        def first():
                            silu(0)
                            hidden(0)

                        def store_rows(q):
                            act.wait_ge(out_ready, q)
                            act.dma_start(ys[bass.ds(q * P - P, P), :], yb[:, :]).then_inc(out_stored, 16)

                        def body(q):
                            store_rows(q)
                            silu(q)
                            hidden(q)
                        n = blocks(act, first, body)
                        store_rows(n)
                        act.wait_ge(out_stored, n * 16)
                        act.sem_inc(all_stored, 1)

                    @block.vector
                    def _(dve):
                        def rows(q):
                            dve.wait_ge(turned, q + 1)
                            for h in range(2):
                                ins = nc.vector.tensor_tensor(xT[:, 4 * h:4 * h + 4, :],
                                                              ps[h][:, :].rearrange("p (k n) -> p k n", k=4),
                                                              gcol[:, 3, 4 * h:4 * h + 4].unsqueeze(2).broadcast_to([P, 4, P]),
                                                              ALU.mult)
                            ins.then_inc(xT_ready, 1)

                        def hidden(q):
                            dve.wait_ge(silu_done, q + 1)
                            dve.wait_ge(w3_done, q + 1)
                            nc.vector.tensor_tensor(hh[:, :], ps[3][:, :], sg[:, :], ALU.mult).then_inc(hid_done, 1)

                        def out(n):
                            dve.wait_ge(w2_done, n)
                            nc.vector.tensor_copy(yb[:, 0:512], ps[5][:, :])
                            nc.vector.tensor_copy(yb[:, 512:D], ps[6][:, :]).then_inc(out_ready, 1)

                        rows(0)
                        hidden(0)
                        last = dve.value_load(plan[0:1, NBLK + PAIRS:NBLK + PAIRS + 1], min_val=PAIRS - 1, max_val=NBLK - 1)
                        rows(1)
                        dve.wait_ge(hid_turned, 1)
                        out(1)
                        hidden(1)
                        with dve.Fori(1, last) as q:
                            rows(q + 1)
                            dve.wait_ge(out_stored, q * 16)
                            out(q + 1)
                            dve.wait_ge(hid_turned, q + 1)
                            hidden(q + 1)
                        dve.wait_ge(out_stored, last * 16)
                        out(last + 1)

        def final_block(hN, gate, slots, ys):
            with ExitStack() as c:
                yg = sb(c, "yg", [P, 2 * T, D])
                sq = sb(c, "fsq", [P, D])
                ss = sb(c, "fss", [P, T])
                gf = sb(c, "gf", [P, D])
                gl = [sem(c, f"fgl{i}") for i in range(2 * T)]
                ld, sd, sqd, rd, yd, ch, sr = (sem(c, "f" + n) for n in ("ld", "sd", "sqd", "rd", "yd", "ch", "sr"))
                with nc.Block() as block:
                    @block.sync
                    def _(sp):
                        sp.dma_start(gf[:, :], a["g_final"].partition_broadcast(P)).then_inc(ld, 16)
                        for t in range(T):
                            sp.wait_ge(yd, t + 1)
                            dst = a["y_prompt"][0, t * P:(t + 1) * P, :] if t < TP else a["y_sample"].rearrange("b q d -> (b q) d")
                            store(sp, dst, hN[:, t, :])
                        sp.wait_ge(stored, ns[0])

                    @block.gpsimd
                    def _(pool):
                        for t in range(T):
                            for k in range(2):
                                i = 2 * t + k
                                pool.indirect_dma_start(
                                    out=yg[:, i, :], out_offset=None, in_=ys,
                                    in_offset=bass.IndirectOffsetOnAxis(ap=slots[:, k * T + t:k * T + t + 1], axis=0),
                                    bounds_check=NSLOT - 1, oob_is_err=False).then_inc(gl[i], 16)

                    @block.scalar
                    def _(act):
                        for t in range(T):
                            act.wait_ge(sd, t + 1)
                            if t:
                                act.wait_ge(sqd, t)
                            nc.scalar.activation(sq[:, :], hN[:, t, :], ACT.Square, accum_out=ss[:, t:t + 1]).then_inc(sqd, 1)
                        act.wait_ge(rd, 1)
                        nc.scalar.activation(ss[:, :], ss[:, :], ACT.Sqrt).then_inc(sr, 1)

                    @block.vector
                    def _(dve):
                        link = chain(dve, ch)
                        for t in range(T):
                            for k in range(2):
                                dve.wait_ge(gl[2 * t + k], 16)
                                ins = nc.vector.scalar_tensor_tensor(out=hN[:, t, :], in0=yg[:, 2 * t + k, :],
                                                                     scalar=gate[:, k, t:t + 1], in1=hN[:, t, :],
                                                                     op0=ALU.mult, op1=ALU.add)
                                if k == 0:
                                    link(ins)
                            ins.then_inc(sd, 1)
                        dve.wait_ge(sqd, T)
                        nc.vector.tensor_scalar(ss[:, :], ss[:, :], 1.0 / D, EPS, ALU.mult, ALU.add).then_inc(rd, 1)
                        dve.wait_ge(sr, 1)
                        link(nc.vector.reciprocal(ss[:, :], ss[:, :]))
                        dve.wait_ge(ld, 16)
                        for t in range(T):
                            nc.vector.scalar_tensor_tensor(out=hN[:, t, :], in0=hN[:, t, :], scalar=ss[:, t:t + 1],
                                                           in1=gf[:, :], op0=ALU.mult, op1=ALU.mult).then_inc(yd, 1)

        def x_tile(t):
            return a["x_prompt"][0, t * P:(t + 1) * P, :] if t < TP else a["x_sample"].rearrange("b q d -> (b q) d")

        def per_tile(prompt, sample, f):
            def at(t):
                if t < TP:
                    return a[prompt].rearrange(f"l b t {f} -> (l b t) ({f})")[t * P:(t + 1) * P, :]
                return a[sample].rearrange(f"l b t {f} -> (l b t) ({f})")
            return at

        tab = nc.dram_tensor("row_tokens", [NSLOT, 1], U32, kind="Internal").ap()
        xs = nc.dram_tensor("ffn_rows", [NTOK, D], F32, kind="Internal").ap()
        ys = nc.dram_tensor("expert_rows", [NSLOT, D], F32, kind="Internal").ap()

        lamcol = sb(top, "lamcol", [P, 1])[:, :]
        with ExitStack() as c1:
            mixT = sb(c1, "mixT", [P, KT, NTOK])
            foxN = sb(c1, "foxN", [P, 512])
            with ExitStack() as c2:
                nT = sb(c2, "nT", [P, KT, NTOK])
                with ExitStack() as c3:
                    xN = sb(c3, "xN", [P, T, D])
                    norm_block("n1", xN, T, 0, nT, load=x_tile, first=True, chunk_range=(0, 6))
                with ExitStack() as c3:
                    qT, kT, vN = (sb(c3, n, [P, 4, NTOK]) for n in ("fqT", "fkT", "fvN_"))
                    vN = vN[:, :, :].rearrange("p a b -> p (a b)").rearrange("p (t n) -> p t n", t=T)
                    project_block("pf", nT, qT, kT, vN, W_FOX, (6, 9), True,
                                  per_tile("p_fk", "s_fk", "h d"), per_tile("p_fv", "s_fv", "h d"))
                    CT = sb(c3, "CT", [80, KS])
                    L2 = sb(c3, "L2", [64, NB, P])
                    bias_l = sb(c3, "bias_l", [80, NB, P])
                    with ExitStack() as c4:
                        RL, RR = sb(c4, "RL", [P, 2, SEQ]), sb(c4, "RR", [P, 2, SEQ])
                        gates_block(nT, RL, RR, CT, L2, bias_l)
                        prompt_attention("fp", "fox", qT, kT, vN, None, mixT, RL=RL, RR=RR, blank=ys[PAIRS * P:, :])
                    decode_attention("fd", "fox", qT, kT, vN, foxN, C_FOX, bias_l=bias_l, CT=CT, L2=L2, chunk_range=(9, 13))
                recycle_semaphores()
                with ExitStack() as c3:
                    qT, kT, vN = (sb(c3, n, [P, 4, NTOK]) for n in ("dqT", "dkT", "dvN_"))
                    vN = vN[:, :, :].rearrange("p a b -> p (a b)").rearrange("p (t n) -> p t n", t=T)
                    project_block("pd", nT, qT, kT, vN, W_DIFF, (13, 16), False,
                                  per_tile("p_dk", "s_dk", "h c d"), per_tile("p_dv", "s_dv", "h d"))
                    lambda_block(lamcol, (16, 16))
                    diffN = nT[:, 0:4, :].rearrange("p a b -> p (a b)").rearrange("p (t n) -> p t n", t=T)
                    prompt_attention("dp", "diff", qT, kT, vN, diffN, None, lamcol=lamcol)
                    decode_attention("dd", "diff", qT, kT, vN, diffN[:, TP, :], C_DIFF, lamcol=lamcol, chunk_range=(16, 20))
                    mix_block(foxN, diffN, mixT, (20, 20))
            hN = sb(c1, "hN", [P, T, D])
            recycle_semaphores()
            residual_block("ro", mixT, hN, W_O, (20, 22), load=x_tile)
            nT = mixT
            with ExitStack() as c2:
                mkT, mvN = sb(c2, "mkT", [P, KT, MEM]), sb(c2, "mvN", [P, 2, D])
                with ExitStack() as c3:
                    memN, mT = sb(c3, "memN", [P, 2, D]), sb(c3, "mT", [P, KT, MEM])
                    norm_block("n2", memN, 2, 2, mT, load=lambda t: a["mem_prompt"][0, t * P:(t + 1) * P, :])
                    memory_block(mT, mkT, mvN, (22, 26))
                norm_block("n3", hN, T, 1, nT)
                qT = sb(c2, "mqT", [P, KT, NTOK])
                query_block(nT, qT, (26, 28))
                prompt_attention("mp", "mem", qT, mkT, mvN, None, nT)
                with ExitStack() as c3:
                    oN = sb(c3, "moN", [P, D])
                    decode_attention("md", "mem", qT, None, None, oN, C_MEM, chunk_range=(28, 36))
                    turn_block(oN, nT)
            recycle_semaphores()
            residual_block("rm", nT, hN, W_MO, (36, 38))
            norm_block("n4", hN, T, 3, nT, extra_dram=xs)
            with ExitStack() as c2:
                gate = sb(c2, "gate", [P, 2, T])
                slots = sb(c2, "slots", [P, 2 * T], U32)
                plan = sb(c2, "plan", [1, NBLK + PAIRS + 1], I32)
                with ExitStack() as c3:
                    xg = sb(c3, "xg", [P, D])
                    idx = sb(c3, "idx", [P, NBLK], U32)
                    route_block(nT, xg, gate, slots, idx, plan, tab)
                    expert_block(xg, idx, xs, ys, plan)
                final_block(hN, gate, slots, ys)


_INS = ["x_prompt", "x_sample", "cache_fox_k", "cache_fox_v", "cache_fox_logf", "cache_diff_k", "cache_diff_v",
        "cache_mem_k", "cache_mem_v", "mem_prompt", "g_mix", "w_in", "b_forget", "lam_q1", "lam_k1", "lam_q2", "lam_k2",
        "g_diff", "w_o", "g_mem_q", "g_mem_kv", "w_mq", "w_mk", "w_mv", "w_mo", "g_ffn", "w_group", "b_group",
        "w_erouter", "b_erouter", "w1", "w3", "w2", "g_final"]
_OUTS = [("y_prompt", (1, SEQ, D)), ("y_sample", (NB, TD, D)),
         ("p_fk", (1, 1, SEQ, FH, HD)), ("p_fv", (1, 1, SEQ, FH, HD)), ("p_logf", (1, 1, SEQ, FH)),
         ("p_dk", (1, 1, SEQ, DH, 2, HD)), ("p_dv", (1, 1, SEQ, DH, 128)),
         ("p_mk", (1, 1, MEM, MH, MD)), ("p_mv", (1, 1, MEM, MH, MD)),
         ("s_fk", (1, NB, TD, FH, HD)), ("s_fv", (1, NB, TD, FH, HD)), ("s_logf", (1, NB, TD, FH)),
         ("s_dk", (1, NB, TD, DH, 2, HD)), ("s_dv", (1, NB, TD, DH, 128))]


def constants(np):
    f = np.float32
    i = np.arange(P)
    big = f(-1e30)
    out = {"c_ident": np.eye(P, dtype=f),
           "c_causal": np.where(i[None, :] <= i[:, None], f(0), big),
           "c_chunk": np.where(i[None, :] // 64 <= i[:, None] // 64, f(0), big)}
    pos = np.concatenate([np.arange(SEQ), np.tile(PAST + np.arange(TD), NB)]).astype(f)
    inv = np.power(f(500000.0), -np.arange(8, dtype=f) / f(8)).astype(f)
    ang = (pos[:, None] * inv[None, :]).astype(f)
    cos, sin = np.cos(ang), np.sin(ang)
    tiles = lambda x: np.ascontiguousarray(x.reshape(T, P, 16).transpose(1, 0, 2)).astype(f)
    out["c_cos"] = tiles(np.concatenate([cos, cos], 1))
    out["c_sin"] = tiles(np.concatenate([-sin, sin], 1))
    sel = np.zeros((80, NB, FH, TD), f)
    for b in range(NB):
        for h in range(FH):
            sel[b * FH + h, b, h, :] = -1.0 / SC
    for q in range(TD):
        sel[64 + q, :, :, q] = 1.0
    out["c_sel"] = sel.reshape(80, NB, P)
    tri16 = np.zeros((TD, KS), f)
    tri16[:, PAST:] = np.where(np.arange(TD)[None, :] > np.arange(TD)[:, None], big, f(0))
    out["c_tri16"] = tri16
    comb = np.zeros((P, P), f)
    sgn = np.zeros((P, 2), f)
    for h in range(DH):
        for cc in range(2):
            for q in range(TD):
                comb[32 * h + 16 * cc + q, 32 * h + q] = 1.0
                sgn[32 * h + 16 * cc + q, cc] = 1.0
    out["c_comb"], out["c_sgn"] = comb, sgn
    out["c_tri"] = (i[:, None] < i[None, :]).astype(f)
    cst = np.zeros((P, 128), f)
    cst[:, 0:4] = np.arange(4, 0, -1)
    cst[:, 4:12] = np.arange(8, 0, -1)
    cst[:, 12:44] = CAP * (np.arange(NE) % 2)
    cst[:, 44:44 + MAXB - 1] = CAP * np.arange(1, MAXB)
    cst[:, 53:53 + NBLK] = np.arange(NBLK)
    out["c_route"] = cst
    out["c_tok"] = (np.arange(T, dtype=np.int32)[None, :] * P + i[:, None].astype(np.int32)).astype(np.int32)
    return {k: np.ascontiguousarray(v) for k, v in out.items()}


def kernel(**inputs):
    import numpy as np
    import concourse.bacc as bacc
    from concourse.bass_utils import run_bass_kernel_spmd

    nc = bacc.Bacc("TRN2", target_bir_lowering=False, num_devices=1)
    arrays, aps = {}, {}
    given = {n: np.ascontiguousarray(inputs[n]) for n in _INS}
    for n, x in {**given, **constants(np)}.items():
        arrays[f"in_{n}"] = x
        aps[n] = nc.dram_tensor(f"in_{n}", x.shape, mybir.dt.from_np(x.dtype), kind="ExternalInput").ap()
    for n, shape in _OUTS:
        aps[n] = nc.dram_tensor(f"out_{n}", shape, F32, kind="ExternalOutput").ap()
    build(nc, aps)
    r = run_bass_kernel_spmd(nc, [arrays], core_ids=[0])
    return tuple(r.results[0][f"out_{n}"] for n, _ in _OUTS)
```

```python
import concourse.bass as bass
import concourse.mybir as mybir
from contextlib import ExitStack

F32 = mybir.dt.float32
F32R = mybir.dt.float32r
BF16 = mybir.dt.bfloat16
I32 = mybir.dt.int32
U32 = mybir.dt.uint32
ALU = mybir.AluOpType
ACT = mybir.ActivationFunctionType
AX = mybir.AxisListType.X

P = 128
D = 1024
KT = D // P
SEQ = 512
NB = 8
TD = 16
PAST = 256
T = 5
TP = 4
NTOK = T * P
FH = 8
HD = 64
DH = 4
MEM = 256
MH = 4
MD = 256
NG = 4
EPG = 8
NE = NG * EPG
DE = 512
ET = DE // P
CAP = 64
PAIRS = NE // 2
MAXB = NTOK // CAP
NBLK = PAIRS + 2 * NTOK // CAP
NSLOT = NBLK * P
LAST = NBLK + PAIRS
ORDER = LAST + 1
IN_W = 3 * 512 + FH + 3 * 512
EPS = 1e-6
LAM_INIT = 0.8 - 0.6
KS = PAST + TD
SC = HD ** -0.5
MSC = MD ** -0.5
SLOTS = 6
GATES_AT, GATES_TURN = 7, 10
W_FOX, C_FOX, W_DIFF, C_DIFF, W_O, W_MK, W_MV, W_MQ, C_MEM, W_MO, W_MOE = 0, 6, 10, 16, 20, 24, 28, 32, 36, 44, 48
HIGH = {W_FOX: 3, W_DIFF: 3, W_O: 2, W_MK: 2, W_MV: 2, W_MQ: 2, W_MO: 2}


def build(nc, a):
    top = ExitStack()
    names = [0]

    def sb(ctx, name, shape, dt=F32):
        return ctx.enter_context(nc.sbuf_tensor(name, shape, dt))

    views = {}

    def dual(ctx, name, shape):
        tensor = sb(ctx, name, shape)
        size = 4
        for n in shape[1:]:
            size *= n
        views[tensor.name] = nc.alloc_sbuf_tensor_at(name + "_r", shape, F32R, offset=nc.sbuf_base - size)
        return tensor

    def r32(ap):
        return bass.AP(tensor=views[ap.tensor.name], offset=ap.offset, ap=[list(x) for x in ap.ap])

    finished = []

    def sem(ctx, name):
        s = nc.alloc_semaphore(name=name)
        if ctx is not top:
            ctx.callback(finished.append, s)
        return s

    def recycle_semaphores():
        nc.clear_and_free_semaphores(finished)
        finished.clear()
        nc.all_engine_barrier()

    with top:
        ps = [top.enter_context(nc.psum_tensor(f"bank{i}", [P, 512], F32)) for i in range(8)]
        ring = dual(top, "ring", [P, SLOTS, 4096])
        LOGITS = ps[5]
        ident = sb(top, "ident", [P, P])
        gcol = sb(top, "gcol", [P, 4, KT])
        landed = [sem(top, f"landed{i}") for i in range(SLOTS)]
        used = sem(top, "chunks_used")
        stored = sem(top, "stored")
        stored_v = sem(top, "stored_values")
        ns = [0]

        def store(eng, dst, src):
            ns[0] += 16
            eng.dma_start(dst, src).then_inc(stored, 16)

        w_in, w_o, w_mk, w_mv, w_mq, w_mo = (a[n][0] for n in ("w_in", "w_o", "w_mk", "w_mv", "w_mq", "w_mo"))

        def cols(w, c0):
            return w[:, c0:c0 + 512].rearrange("(k p) n -> p k n", p=P)

        fox_w = 3 * 512 + FH
        heads_of = {"cache_fox_k": "h d", "cache_fox_v": "h d", "cache_diff_k": "h c d", "cache_diff_v": "h d",
                    "cache_mem_k": "h d", "cache_mem_v": "h d"}

        def cache(name):
            f = heads_of[name]
            return a[name][0].rearrange(f"b t {f} -> b t ({f})")

        plain = {W_FOX + i: cols(w_in, 512 * i) for i in range(3)}
        plain |= {W_DIFF + i: cols(w_in, fox_w + 512 * i) for i in range(3)}
        for c, w in ((W_O, w_o), (W_MK, w_mk), (W_MV, w_mv), (W_MQ, w_mq), (W_MO, w_mo)):
            plain |= {c + i: cols(w, 512 * i) for i in range(2)}

        def slot(c):
            return ring[:, c % SLOTS, :].rearrange("p (k n) -> p k n", n=512)

        def slot2(c):
            return ring[:, c % SLOTS, :].rearrange("p (k n) -> p k n", n=1024)

        def parts(c):
            if c in plain:
                return [(slot(c), plain[c])]
            if any(w + n <= c < w + 2 * n for w, n in HIGH.items()):
                return []
            if c >= W_MOE:
                j = (c - W_MOE) % 6
                e = 2 * ((c - W_MOE) // 6) + j % 2
                name = "w1" if j < 2 else "w3" if j < 4 else "w2"
                return [(slot(c) if j < 4 else slot2(c), a[name][0, e].rearrange("(k p) n -> p k n", p=P))]
            if c >= C_MEM:
                b = c - C_MEM
                return [(slot2(c)[:, 2 * i:2 * i + 2, :], cache(n)[b].rearrange("(k p) f -> p k f", p=P))
                        for i, n in enumerate(("cache_mem_k", "cache_mem_v"))]
            kind, c0 = ("fox", C_FOX) if c < W_DIFF else ("diff", C_DIFF)
            out = []
            for s in range(2):
                for i, n in enumerate((f"cache_{kind}_k", f"cache_{kind}_v")):
                    out.append((slot(c)[:, 4 * s + 2 * i:4 * s + 2 * i + 2, :],
                                cache(n)[2 * (c - c0) + s].rearrange("(k p) f -> p k f", p=P)))
            return out

        landed_by = [0] * (W_MOE + SLOTS)
        for c in range(W_MOE + SLOTS):
            landed_by[c] = (landed_by[c - SLOTS] if c >= SLOTS else 0) + 16 * len(parts(c))

        def load_chunks(sp, c0, c1):
            for c in range(c0, c1):
                assert parts(c)
                if c >= SLOTS:
                    sp.wait_ge(used, c - SLOTS + 1)
                for dst, src in parts(c):
                    sp.dma_start(dst, src).then_inc(landed[c % SLOTS], 16)

        def wait_chunk(pe, c):
            pe.wait_ge(landed[c % SLOTS], landed_by[c])

        class Split:

            def __init__(self, c, tag):
                self.high_done, self.low_done = sem(c, tag + "high_done"), sem(c, tag + "low_done")
                self.n = {"act": 0, "dve": 0, "pe": 0}

            def high(self, act, dst, src):
                self.n["act"] += 1
                nc.scalar.copy(r32(dst), src).then_inc(self.high_done, 1)

            def low(self, dve, high, x):
                self.n["dve"] += 1
                dve.wait_ge(self.high_done, self.n["dve"])
                nc.vector.tensor_tensor(r32(x), x, r32(high), ALU.subtract).then_inc(self.low_done, 1)

            def ready(self, pe, pieces=1):
                self.n["pe"] += pieces
                pe.wait_ge(self.low_done, self.n["pe"])

            def high_chunk(self, act, ch, h, free=None):
                wait_chunk(act, ch)
                if free is not None:
                    act.wait_ge(used, free)
                for k in range(KT):
                    self.high(act, slot(h)[:, k, :], slot(ch)[:, k, :])

            def low_chunk(self, dve, ch, h):
                for k in range(KT):
                    self.low(dve, slot(h)[:, k, :], slot(ch)[:, k, :])

        def products(out, xh, xl, yh, yl, first, last):
            nc.tensor.matmul(out, r32(xh), r32(yh), start=first, stop=False)
            nc.tensor.matmul(out, r32(xh), r32(yl), start=False, stop=False)
            return nc.tensor.matmul(out, r32(xl), r32(yh), start=False, stop=last)

        def chain(eng, s):
            n = [0]

            def link(ins):
                n[0] += 1
                ins.then_inc(s, 1)
                eng.wait_ge(s, n[0])
            return link

        def warm_up(bank):
            for _ in range(9):
                nc.tensor.matmul(bank[:, 0:P], ident[:, :], ident[:, :], start=True, stop=True)

        g_names = ("g_mix", "g_mem_q", "g_mem_kv", "g_ffn")

        def norm_block(tag, src, nt, gi, dst_t, load, chunk_range):
            with ExitStack() as c:
                sq = sb(c, tag + "sq", [P, D])
                ss = sb(c, tag + "ss", [P, nt])
                rs = sb(c, tag + "rs", [P, nt])
                xs = sb(c, tag + "xs", [P, 2, D])
                ld, gain_in, others_in, ssd, msd, rtd, rsd, xsd, trd, evd, ch = (
                    sem(c, tag + n) for n in ("ld", "gain_in", "others_in", "ssd", "msd", "rtd", "rsd", "xsd", "trd", "evd", "ch"))
                lt = [sem(c, f"{tag}lt{t}") for t in range(nt)]
                with nc.Block() as block:
                    @block.sync
                    def _(sp):
                        for t in range(nt):
                            sp.dma_start(src[:, t, :], load(t)).then_inc(lt[t], 16)
                            if t == 1:
                                sp.dma_start(ident[:, :], a["c_ident"]).then_inc(ld, 16)
                        for i, n in enumerate(g_names):
                            with nc.allow_non_contiguous_dma("small gain vectors"):
                                sp.dma_start(gcol[:, i, :], a[n][0].rearrange("(k p) -> p k", p=P)).then_inc(
                                    gain_in if i == gi else others_in, 16)
                        load_chunks(sp, *chunk_range)
                        sp.wait_ge(others_in, 16 * (len(g_names) - 1))

                    @block.scalar
                    def _(act):
                        def squares(t):
                            act.wait_ge(lt[t], 16)
                            if t:
                                act.wait_ge(ssd, t)
                            nc.scalar.activation(sq[:, :], src[:, t, :], ACT.Square, accum_out=ss[:, t:t + 1]).then_inc(ssd, 1)

                        squares(0)
                        for t in range(nt):
                            if t + 1 < nt:
                                squares(t + 1)
                            act.wait_ge(msd, t + 1)
                            nc.scalar.activation(rs[:, t:t + 1], ss[:, t:t + 1], ACT.Sqrt).then_inc(rtd, 1)
                            act.wait_ge(rsd, t + 1)
                            if t >= 2:
                                act.wait_ge(trd, t - 1)
                            nc.scalar.activation(xs[:, t % 2, :], src[:, t, :], ACT.Copy, scale=rs[:, t:t + 1]).then_inc(xsd, 1)

                    @block.vector
                    def _(dve):
                        def stats(t):
                            dve.wait_ge(ssd, t + 1)
                            nc.vector.tensor_scalar(ss[:, t:t + 1], ss[:, t:t + 1], 1.0 / D, EPS, ALU.mult, ALU.add).then_inc(msd, 1)
                            dve.wait_ge(rtd, t + 1)
                            nc.vector.reciprocal(rs[:, t:t + 1], rs[:, t:t + 1]).then_inc(rsd, 1)

                        stats(0)
                        for t in range(nt):
                            if t + 1 < nt:
                                stats(t + 1)
                            if t == 0:
                                dve.wait_ge(gain_in, 16)
                            dve.wait_ge(trd, t + 1)
                            for h in range(2):
                                ins = nc.vector.tensor_tensor(
                                    dst_t[:, 4 * h:4 * h + 4, t * P:(t + 1) * P],
                                    ps[2 * (t % 2) + h][:, :].rearrange("p (k n) -> p k n", k=4),
                                    gcol[:, gi, 4 * h:4 * h + 4].unsqueeze(2).broadcast_to([P, 4, P]), ALU.mult)
                            ins.then_inc(evd, 1)

                    @block.tensor
                    def _(pe):
                        pe.wait_ge(ld, 16)
                        for t in range(nt):
                            pe.wait_ge(xsd, t + 1)
                            if t >= 2:
                                pe.wait_ge(evd, t - 1)
                            for k in range(KT):
                                ins = nc.tensor.transpose(ps[2 * (t % 2) + k // 4][:, (k % 4) * P:(k % 4 + 1) * P],
                                                          xs[:, t % 2, k * P:(k + 1) * P], ident[:, :])
                            ins.then_inc(trd, 1)

        class Gates:

            def __init__(self, c, nT, nH, RL, RR, CT, L2, bias_l, spare):
                self.nH = nH
                self.wh = dual(c, "wffh", [P, KT, FH])
                self.nT, self.RL, self.RR, self.CT, self.L2, self.bias_l = nT, RL, RR, CT, L2, bias_l
                self.w = dual(c, "wff", [P, KT, FH])
                self.bias = sb(c, "bf", [FH, 1])
                self.z = sb(c, "gz", [FH, NTOK])
                self.e = dual(c, "ge", [FH, NTOK])
                self.lf = self.z
                self.lfN = sb(c, "glfN", [P, T, FH])
                self.cc = dual(c, "gcc", [FH, 2, SEQ])
                self.high = (spare[0:FH, :], self.e[:, 0:SEQ])
                self.one = sb(c, "gone", [NB * FH, SEQ])
                self.lc = sb(c, "glc", [P, 2, NB * FH])
                self.raw = sb(c, "graw", [NB * FH, KS])
                self.cn = sb(c, "gcn", [NB * FH, TD])
                (self.weights_in, self.cache_in, self.set, self.z_done, self.z_read, self.exp_done, self.lf_done, self.sums_done,
                 self.cache_turned, self.cache_read, self.new_in, self.chained, self.act_chained, self.rows_in,
                 self.lf_turned, self.lfN_done, self.l2_done, self.split_done) = (sem(c, "g_" + n) for n in (
                     "weights_in", "cache_in", "set", "z_done", "z_read", "exp_done", "lf_done", "sums_done", "cache_turned",
                     "cache_read", "new_in", "chained", "act_chained", "rows_in", "lf_turned", "lfN_done", "l2_done", "split_done"))

            def load(self, sp):
                lc = self.lc
                with nc.allow_non_contiguous_dma("narrow gate columns"):
                    sp.dma_start(self.w[:, :, :],
                                 w_in[:, 1536:1536 + FH].rearrange("(k p) n -> p k n", p=P)).then_inc(self.weights_in, 16)
                    sp.dma_start(self.bias[:, :], a["b_forget"][0].rearrange("(h o) -> h o", o=1)).then_inc(self.weights_in, 16)
                    for h in range(2):
                        sp.dma_start(lc[:, h, :].rearrange("p (b f) -> p b f", b=NB),
                                     a["cache_fox_logf"][0, :, h * P:(h + 1) * P, :].rearrange("b p f -> p b f")).then_inc(
                                         self.cache_in, 16)
                sp.dma_start(self.CT[64:80, :], a["c_tri16"]).then_inc(self.cache_in, 16)
                sp.dma_start(self.bias_l[:, :, :], a["c_sel"]).then_inc(self.cache_in, 16)

            def move_gates(self, sp):
                sp.wait_ge(self.lf_done, 1)
                for b in range(NB):
                    sp.dma_start(self.raw[b * FH:(b + 1) * FH, PAST:KS],
                                 self.lf[:, SEQ + b * TD:SEQ + (b + 1) * TD]).then_inc(self.new_in, 16)

            def move_sums(self, pool):
                pool.wait_ge(self.set, 5)
                pool.wait_ge(self.sums_done, 1)
                for g in range(FH // 4):
                    for i, rows, row in ((0, self.RL, 2), (1, self.RR, 0)):
                        for x, part in enumerate((self.high[i], self.cc[:, i, :])):
                            pool.dma_start(r32(rows[row + x:P:32, g, :]), r32(part[4 * g:4 * g + 4, :])).then_inc(self.rows_in, 16)

            def store(self, sp):
                sp.wait_ge(self.lfN_done, 1)
                store(sp, a["p_logf"].rearrange("l b (t p) h -> p (l b t) h", p=P), self.lfN[:, 0:TP, :])
                store(sp, a["s_logf"].rearrange("l b q h -> (l b q) h"), self.lfN[:, TP, :])
                sp.wait_ge(self.rows_in, 16 * FH)
                sp.wait_ge(stored, ns[0])

            def constants(self, pool):
                nc.gpsimd.memset(self.one[:, :], 1.0).then_inc(self.set, 1)
                one = self.one[:, :].unsqueeze(1).broadcast_to([NB * FH, 2, SEQ])
                pool.wait_ge(self.set, 1)
                for rows in (self.RR, self.RL):
                    for p in (0, NB * FH):
                        nc.gpsimd.tensor_copy(r32(rows[p:p + NB * FH, :, :]), one).then_inc(self.set, 1)

            def products(self, pe):
                half = NTOK // 2
                pe.wait_ge(self.split_done, 1)
                for k in range(KT):
                    for b, o in ((1, 0), (3, half)):
                        ins = products(ps[b][0:FH, 0:half], self.wh[:, k, :], self.w[:, k, :], self.nH[:, k, o:o + half],
                                       self.nT[:, k, o:o + half], k == 0, k == KT - 1)
                ins.then_inc(self.z_done, 1)
                pe.wait_ge(self.cache_in, 64)
                for h in range(2):
                    ins = nc.tensor.transpose(ps[5][0:64, h * P:(h + 1) * P], self.lc[:, h, :], ident[:, :])
                ins.then_inc(self.cache_turned, 1)

            def turn_gates(self, pe):
                pe.wait_ge(self.lf_done, 1)
                for t in range(T):
                    ins = nc.tensor.transpose(ps[7][:, t * FH:(t + 1) * FH], self.lf[:, t * P:(t + 1) * P], ident[0:FH, 0:FH])
                ins.then_inc(self.lf_turned, 1)

            def split(self, dve, link):
                dve.wait_ge(self.weights_in, 32)
                link(nc.vector.tensor_copy(r32(self.wh[:, :, :]), self.w[:, :, :]))
                nc.vector.tensor_tensor(r32(self.w[:, :, :]), self.w[:, :, :], r32(self.wh[:, :, :]),
                                        ALU.subtract).then_inc(self.split_done, 1)

            def exponentials(self, act):
                link = chain(act, self.act_chained)
                act.wait_ge(self.z_read, 1)
                link(nc.scalar.activation(self.e[:, :], self.z[:, :], ACT.Abs))
                link(nc.scalar.activation(self.e[:, :], self.e[:, :], ACT.Exp, scale=-1.0))
                nc.scalar.activation(self.e[:, :], self.e[:, :], ACT.Ln, bias=1.0).then_inc(self.exp_done, 1)

            def gates(self, dve, link):
                z, cc = self.z, self.cc
                dve.wait_ge(self.z_done, 1)
                dve.wait_ge(self.weights_in, 32)
                half = NTOK // 2
                nc.vector.tensor_scalar(z[:, 0:half], ps[1][0:FH, 0:half], self.bias[:, 0:1], None, ALU.add)
                nc.vector.tensor_scalar(z[:, half:], ps[3][0:FH, 0:half], self.bias[:, 0:1], None, ALU.add).then_inc(self.z_read, 1)
                dve.wait_ge(self.cache_turned, 1)
                nc.vector.tensor_copy(self.raw[:, 0:PAST], ps[5][0:64, 0:PAST]).then_inc(self.cache_read, 1)
                dve.wait_ge(self.exp_done, 1)
                nc.vector.scalar_tensor_tensor(out=self.lf[:, :], in0=z[:, :], scalar=0.0, in1=self.e[:, :],
                                               op0=ALU.min, op1=ALU.subtract).then_inc(self.lf_done, 1)
                dve.wait_ge(self.lf_done, 1)
                dve.wait_ge(self.set, 1)
                link(nc.vector.tensor_tensor_scan(cc[:, 0, :], self.one[0:FH, :], self.lf[:, 0:SEQ], 0.0, ALU.mult, ALU.add))
                link(nc.vector.tensor_scalar(cc[:, 1, :], cc[:, 0, :], -1.0 / SC, None, ALU.mult))
                link(nc.vector.tensor_scalar(cc[:, 0, :], cc[:, 0, :], 1.0 / SC, None, ALU.mult))
                for i in range(2):
                    link(nc.vector.tensor_copy(r32(self.high[i]), cc[:, i, :]))
                    ins = nc.vector.tensor_tensor(r32(cc[:, i, :]), cc[:, i, :], r32(self.high[i]), ALU.subtract)
                ins.then_inc(self.sums_done, 1)

            def decode_sums(self, dve, link):
                CT = self.CT
                dve.wait_ge(self.new_in, 16 * NB)
                dve.wait_ge(self.cache_read, 1)
                link(nc.vector.tensor_tensor_scan(CT[0:64, :], self.one[:, 0:KS], self.raw[:, :], 0.0, ALU.mult, ALU.add))
                link(nc.vector.tensor_scalar(self.cn[:, :], CT[0:64, PAST:KS], -1.0, None, ALU.mult))
                dve.wait_ge(self.cache_in, 64)
                for b in range(NB):
                    ins = nc.vector.tensor_tensor(
                        self.L2[:, b, :].rearrange("p (h q) -> p h q", h=FH),
                        self.bias_l[0:64, b, :].rearrange("p (h q) -> p h q", h=FH),
                        self.cn[:, :].unsqueeze(1).broadcast_to([64, FH, TD]), ALU.mult)
                ins.then_inc(self.l2_done, 1)
                dve.wait_ge(self.lf_turned, 1)
                nc.vector.tensor_copy(self.lfN[:, :, :],
                                      ps[7][:, 0:T * FH].rearrange("p (t h) -> p t h", t=T)).then_inc(self.lfN_done, 1)
                dve.wait_ge(self.l2_done, 1)

        def project_block(tag, nT, nH, qT, kT, vN, c0, chunk_range, fox, k_out, v_out, lamcol=None,
                          gates=None):
            with ExitStack() as c:
                if not fox:
                    lv, lp, ls = sb(c, "lv", [P, 4, HD]), sb(c, "lpr", [P, 2, HD]), sb(c, "ls", [P, 2])
                    lv_loaded, l_chain, l_exp, l_sums = (sem(c, "l_" + n) for n in ("loaded", "chain", "exp", "sums"))
                st = sb(c, tag + "st", [P, 4, 512])
                rt = None if fox else sb(c, tag + "rt", [P, 2, 2, 8, 16])
                cs = None if fox else sb(c, tag + "cs", [P, 2, T, 16])
                mmd, eva, evd, trd, rop, csd, ch = (sem(c, tag + n) for n in ("mmd", "eva", "evd", "trd", "rop", "csd", "ch"))
                kst = [sem(c, f"{tag}kst{i}") for i in range(4)]
                split = Split(c, tag)
                half = NTOK // 2
                groups = []
                if fox:
                    groups += [("qT", j) for j in range(4)]
                nat = ([] if fox else [("q", t) for t in range(T)]) + [("k", t) for t in range(T)]
                for i, (w, t) in enumerate(nat):
                    groups.append(("mm", w, t, i))
                    if i >= 2:
                        groups.append(("tr",) + nat[i - 2] + (i - 2,))
                vs = [("mm", "v", t, None) for t in range(T)]
                groups += [vs[0], ("tr",) + nat[-2] + (len(nat) - 2,), vs[1], ("tr",) + nat[-1] + (len(nat) - 1,)] + vs[2:]
                chunk_of = {"q": c0, "k": c0 + 1, "v": c0 + 2}
                on_act = [g[0] == "mm" and g[1] != "v" or (g[0] == "tr" and fox and i % 2 == 0) for i, g in enumerate(groups)]
                nact = [sum(on_act[:i + 1]) for i in range(len(groups))]
                ndve = [i + 1 - nact[i] for i in range(len(groups))]
                where = {g[3]: i for i, g in enumerate(groups) if g[0] == "mm" and g[3] is not None}
                trw = {g[3]: i for i, g in enumerate(groups) if g[0] == "tr"}

                split_at = {1: 1, 5: 2}

                def column(x, i):
                    return x[:, i, :] if fox else x[:, :, i * P:(i + 1) * P]

                def drained(eng, g):
                    if on_act[g]:
                        eng.wait_ge(eva, nact[g])
                    else:
                        eng.wait_ge(evd, ndve[g])

                with nc.Block() as block:
                    @block.sync
                    def _(sp):
                        if not fox:
                            for i, n in enumerate(("lam_q1", "lam_q2", "lam_k1", "lam_k2")):
                                sp.dma_start(lv[:, i, :], a[n].partition_broadcast(P).rearrange(
                                    "p l d -> p (l d)")).then_inc(lv_loaded, 16)
                            sp.dma_start(cs[:, 0, :, :], a["c_cos"]).then_inc(csd, 16)
                            sp.dma_start(cs[:, 1, :, :], a["c_sin"]).then_inc(csd, 16)
                        if gates is None:
                            load_chunks(sp, *chunk_range)
                        else:
                            gates.load(sp)
                            load_chunks(sp, chunk_range[0], chunk_range[0] + 1)
                            gates.move_gates(sp)
                            load_chunks(sp, chunk_range[0] + 1, chunk_range[0] + 2)
                            gates.store(sp)
                            load_chunks(sp, chunk_range[0] + 2, chunk_range[1])

                    @block.gpsimd
                    def _(pool):
                        if gates is not None:
                            gates.constants(pool)
                        for i, (w, t) in enumerate(nat):
                            if w == "k":
                                if fox:
                                    drained(pool, where[i])
                                else:
                                    pool.wait_ge(rop, i + 1)
                                pool.dma_start(k_out(t), st[:, i % 4, :]).then_inc(kst[i % 4], 16)
                                if gates is not None and i == 2:
                                    gates.move_sums(pool)
                        for i, g in enumerate(groups):
                            if g[0] == "mm" and g[1] == "v":
                                drained(pool, i)
                                pool.dma_start(v_out(g[2]), vN[:, g[2], :]).then_inc(stored_v, 16)
                        pool.wait_ge(stored_v, 16 * T * (1 if fox else 2))
                        for i in range(4):
                            n = sum(1 for j, (w, t) in enumerate(nat) if w == "k" and j % 4 == i)
                            pool.wait_ge(kst[i], 16 * n)

                    @block.tensor
                    def _(pe):
                        warm_up(ps[0])
                        for g, grp in enumerate(groups):
                            if gates is not None and g == GATES_AT + 1:
                                gates.products(pe)
                            if gates is not None and g == GATES_TURN + 1:
                                gates.turn_gates(pe)
                            if g >= 4:
                                drained(pe, g - 4)
                            b0, b1 = ps[2 * (g % 4)], ps[2 * (g % 4) + 1]
                            if grp[0] == "qT":
                                j = grp[1]
                                w, wh = slot(c0)[:, :, j * P:(j + 1) * P], slot(c0 + 3)[:, :, j * P:(j + 1) * P]
                                for k in range(KT):
                                    if j == 0:
                                        split.ready(pe, 2)
                                    products(b0[:, 0:half], wh[:, k, :], w[:, k, :], nH[:, k, 0:half], nT[:, k, 0:half],
                                             k == 0, k == KT - 1)
                                    ins = products(b1[:, 0:half], wh[:, k, :], w[:, k, :], nH[:, k, half:], nT[:, k, half:],
                                                   k == 0, k == KT - 1)
                                ins.then_inc(mmd, 1)
                                if j == 3:
                                    pe.wait_ge(mmd, g + 1)
                                    pe.sem_inc(used, 1)
                            elif grp[0] == "mm":
                                _, w, t, _ = grp
                                wt, wh = slot(chunk_of[w]), slot(chunk_of[w] + 3)
                                if w == "q" and t == 0:
                                    split.ready(pe, 1)
                                for k in range(KT):
                                    if t == 0:
                                        split.ready(pe, 1)
                                    ins = products(b0[:, :], nH[:, k, t * P:(t + 1) * P], nT[:, k, t * P:(t + 1) * P],
                                                   wh[:, k, :], wt[:, k, :], k == 0, k == KT - 1)
                                if w == "q" and t == 0:
                                    split.ready(pe, T - 1)
                                ins.then_inc(mmd, 1)
                                if t == T - 1:
                                    pe.wait_ge(mmd, g + 1)
                                    pe.sem_inc(used, 4 if w == "v" else 1)
                            else:
                                _, w, t, i = grp
                                if fox:
                                    drained(pe, where[i])
                                else:
                                    pe.wait_ge(rop, i + 1)
                                for j in range(4):
                                    ins = nc.tensor.transpose(b0[:, j * P:(j + 1) * P], st[:, i % 4, j * P:(j + 1) * P],
                                                              ident[:, :])
                                ins.then_inc(mmd, 1)

                    def copy_out(eng, copy, g, grp):
                        eng.wait_ge(mmd, g + 1)
                        b0, b1 = ps[2 * (g % 4)], ps[2 * (g % 4) + 1]
                        if grp[0] == "qT":
                            copy(qT[:, grp[1], 0:half], b0[:, 0:half])
                            return copy(qT[:, grp[1], half:], b1[:, 0:half])
                        if grp[0] == "mm" and grp[1] == "v":
                            return copy(vN[:, grp[2], :], b0[:, :])
                        if grp[0] == "mm":
                            i = grp[3]
                            if i >= 4:
                                eng.wait_ge(mmd, trw[i - 4] + 1)
                                n = sum(1 for j in range(i - 3) if nat[j][0] == "k" and j % 4 == i % 4)
                                if n:
                                    eng.wait_ge(kst[i % 4], 16 * n)
                            return copy(st[:, i % 4, :], b0[:, :])
                        dst = qT if grp[1] == "q" else kT
                        return copy(dst[:, :, grp[2] * P:(grp[2] + 1) * P], b0[:, :].rearrange("p (j n) -> p j n", j=4))

                    @block.scalar
                    def _(act):
                        wait_chunk(act, c0)
                        if not fox:
                            split.high(act, column(nH, 0), column(nT, 0))
                        for k in range(KT):
                            if fox:
                                split.high(act, column(nH, k), column(nT, k))
                            split.high(act, slot(c0 + 3)[:, k, :], slot(c0)[:, k, :])
                        if not fox:
                            for t in range(1, T):
                                split.high(act, column(nH, t), column(nT, t))
                        for g, grp in enumerate(groups):
                            if g in split_at:
                                split.high_chunk(act, c0 + split_at[g], c0 + 3 + split_at[g])
                            if gates is not None and g == GATES_AT + 1:
                                gates.exponentials(act)
                            if on_act[g]:
                                copy_out(act, nc.scalar.copy, g, grp).then_inc(eva, 1)
                        if not fox:
                            act.wait_ge(l_sums, 1)
                            nc.scalar.activation(ls[:, :], ls[:, :], ACT.Exp).then_inc(l_exp, 1)

                    @block.vector
                    def _(dve):
                        link = chain(dve, ch)
                        if not fox:
                            split.low(dve, column(nH, 0), column(nT, 0))
                        for k in range(KT):
                            if fox:
                                split.low(dve, column(nH, k), column(nT, k))
                            split.low(dve, slot(c0 + 3)[:, k, :], slot(c0)[:, k, :])
                        if not fox:
                            for t in range(1, T):
                                split.low(dve, column(nH, t), column(nT, t))
                            dve.wait_ge(csd, 32)
                        for g, grp in enumerate(groups):
                            if g in split_at:
                                split.low_chunk(dve, c0 + split_at[g], c0 + 3 + split_at[g])
                                if gates is not None and g == 1:
                                    gates.split(dve, link)
                            if not on_act[g]:
                                copy_out(dve, nc.vector.tensor_copy, g, grp).then_inc(evd, 1)
                            elif not fox:
                                i, t = grp[3], grp[2]
                                drained(dve, g)
                                x = st[:, i % 4, :].rearrange("p (c d) -> p c d", c=8)
                                r = rt[:, i % 2]
                                cosv = cs[:, 0, t, :].unsqueeze(1).broadcast_to([P, 8, 16])
                                sinv = cs[:, 1, t, :].unsqueeze(1).broadcast_to([P, 8, 16])
                                nc.vector.tensor_tensor(r[:, 0], x[:, :, 0:16], cosv, ALU.mult)
                                nc.vector.tensor_tensor(r[:, 1, :, 0:8], x[:, :, 8:16], sinv[:, :, 0:8], ALU.mult)
                                link(nc.vector.tensor_tensor(r[:, 1, :, 8:16], x[:, :, 0:8], sinv[:, :, 8:16], ALU.mult))
                                nc.vector.tensor_tensor(x[:, :, 0:16], r[:, 0], r[:, 1], ALU.add).then_inc(rop, 1)
                            if gates is not None and g == GATES_AT:
                                gates.gates(dve, link)
                            if gates is not None and g == GATES_TURN + 3:
                                gates.decode_sums(dve, link)
                        if not fox:
                            l_link = chain(dve, l_chain)
                            dve.wait_ge(lv_loaded, 64)
                            l_link(nc.vector.tensor_tensor(lp[:, :, :], lv[:, 0:2, :], lv[:, 2:4, :], ALU.mult))
                            nc.vector.reduce_sum(ls[:, :], lp[:, :, :], AX).then_inc(l_sums, 1)
                            dve.wait_ge(l_exp, 1)
                            l_link(nc.vector.tensor_tensor(lamcol, ls[:, 1:2], ls[:, 0:1], ALU.subtract))
                            l_link(nc.vector.tensor_scalar(lamcol, lamcol, -LAM_INIT, None, ALU.add))

        def prompt_attention(tag, kind, qT, kT, vN, outN, outT, RL=None, RR=None, lamcol=None, chunk_range=None, blank=None,
                             join=None):
            fox, diff, mem = kind == "fox", kind == "diff", kind == "mem"
            comps = 2 if diff else 1
            heads = FH if fox else DH
            width = {"fox": 64, "diff": 128, "mem": 256}[kind]
            scale = MSC if mem else SC
            units = [(qt, h, cc) for qt in range(TP) for h in range(heads) for cc in range(comps)]
            pairs = [(qt, h) for qt in range(TP) for h in range(heads)]
            nk = (lambda qt: 2) if mem else (lambda qt: qt + 1)
            score_banks = {"fox": (0, 1, 7), "diff": (0, 1, 6, 7), "mem": (0, 1)}[kind]
            ahead = 1 if mem else 2
            nsb = len(score_banks)

            def sbank(u):
                return ps[score_banks[u % nsb]]

            with ExitStack() as c:
                mask = None if mem else sb(c, tag + "mask", [P, P])
                pb = sb(c, tag + "p", [P, 4, 512])
                pt = sb(c, tag + "pt", [P, 2, 512])
                mx = sb(c, tag + "mx", [P, 4])
                rs = sb(c, tag + "rs", [P, len(units)])
                rr = sb(c, tag + "rr", [P, len(units)])
                dg = sb(c, tag + "dg", [P, 4, P]) if diff else None
                on = None if diff else sb(c, tag + "on", [P, heads * width])
                if blank is not None:
                    zero = sb(c, tag + "zero", [P, D])
                    bz, bd, joined = sem(c, tag + "bz"), sem(c, tag + "bd"), sem(c, tag + "joined")
                md, sc, mxd, exd, trp, cpd, pvd, rrd, ond, otd, oed, ch, dgd = (
                    sem(c, tag + n) for n in ("md", "sc", "mxd", "exd", "trp", "cpd", "pvd", "rrd", "ond", "otd",
                                              "oed", "ch", "dgd"))

                def obank(qt, h):
                    if mem:
                        return ps[4 + h // 2], (h % 2) * 256
                    return ps[4 + qt % 2], h * width

                with nc.Block() as block:
                    @block.sync
                    def _(sp):
                        if not mem:
                            sp.dma_start(mask[:, :], a["c_causal" if fox else "c_chunk"]).then_inc(md, 16)
                        if chunk_range:
                            load_chunks(sp, *chunk_range)
                        if blank is not None:
                            sp.wait_ge(bz, 1)
                            for i in range(blank.shape[0] // P):
                                sp.dma_start(blank[i * P:(i + 1) * P, :], zero[:, :]).then_inc(bd, 16)
                            sp.wait_ge(bd, 16 * (blank.shape[0] // P))

                    if blank is not None:
                        @block.gpsimd
                        def _(pool):
                            nc.gpsimd.memset(zero[:, :], 0.0).then_inc(bz, 1)
                            nc.gpsimd.tensor_tensor(join[0][:, :, :], r32(join[0][:, :, :]), r32(join[1][:, :, :]), ALU.add).then_inc(joined, 1)

                    @block.tensor
                    def _(pe):
                        def scores(u):
                            qt, h, cc = units[u]
                            n = nk(qt) * P
                            b = sbank(u)
                            if u >= nsb:
                                pe.wait_ge(exd, u - nsb + 1)
                            if mem:
                                for j in range(2):
                                    ins = nc.tensor.matmul(b[:, 0:n], qT[:, 2 * h + j, qt * P:(qt + 1) * P],
                                                           kT[:, 2 * h + j, :], start=j == 0, stop=j == 1)
                            else:
                                x = h if fox else 2 * h + cc
                                r0, j = 64 * (x % 2), x // 2
                                nc.tensor.matmul(b[:, n - P:n], ident[:, :], mask[:, :], start=True, stop=False,
                                                 skip_group_check=True)
                                ins = nc.tensor.matmul(b[:, 0:n], qT[r0:r0 + 64, j, qt * P:(qt + 1) * P],
                                                       kT[r0:r0 + 64, j, 0:n], start=False, stop=not fox,
                                                       skip_group_check=True)
                                if fox:
                                    p0 = 32 * (h % 4)
                                    ins = nc.tensor.matmul(b[:, 0:n], r32(RL[p0:p0 + 4, h // 4, qt * P:(qt + 1) * P]),
                                                           r32(RR[p0:p0 + 4, h // 4, 0:n]), start=False, stop=True,
                                                           skip_group_check=True)
                            ins.then_inc(sc, 1)

                        def turn(i):
                            qt, h = pairs[i]
                            if i >= 2:
                                pe.wait_ge(cpd, i - 1)
                            b = ps[2 + i % 2]
                            if diff:
                                pe.wait_ge(dgd, i + 1)
                            else:
                                pe.wait_ge(exd, i + 1)
                            for k in range(nk(qt)):
                                if diff:
                                    for cc in range(2):
                                        s = (2 * i + cc) % 4
                                        ins = nc.tensor.matmul(b[:, k * P:(k + 1) * P], pb[:, s, k * P:(k + 1) * P],
                                                               dg[:, s, :], start=cc == 0, stop=cc == 1)
                                else:
                                    ins = nc.tensor.transpose(b[:, k * P:(k + 1) * P], pb[:, i % 4, k * P:(k + 1) * P],
                                                              ident[:, :])
                            ins.then_inc(trp, 1)

                        def values(i):
                            qt, h = pairs[i]
                            pe.wait_ge(cpd, i + 1)
                            b, o = obank(qt, h)
                            if h == 0 and (mem and qt or qt >= 2):
                                pe.wait_ge(ond, qt if mem else qt - 1)
                            for k in range(nk(qt)):
                                ins = nc.tensor.matmul(b[:, o:o + width], pt[:, i % 2, k * P:(k + 1) * P],
                                                       vN[:, k, h * width:(h + 1) * width], start=k == 0,
                                                       stop=k == nk(qt) - 1)
                            ins.then_inc(pvd, 1)
                            if h == heads - 1 and not diff:
                                finish.append(qt)

                        def out_turn(qt):
                            pe.wait_ge(ond, qt + 1)
                            for j in range(heads * width // P):
                                if j % 4 == 0:
                                    n = max(0, 2 * qt + j // 4 - 1) if mem else qt
                                    if n:
                                        pe.wait_ge(oed, n)
                                ins = nc.tensor.transpose(ps[6 if not mem else 6 + j // 4][:, (j % 4) * P:(j % 4 + 1) * P],
                                                          on[:, j * P:(j + 1) * P], ident[:, :])
                                if j % 4 == 3:
                                    ins.then_inc(otd, 1)

                        finish = []
                        if not mem:
                            warm_up(ps[0])
                            pe.wait_ge(md, 16)
                        for u in range(ahead * comps):
                            scores(u)
                        for i in range(len(pairs)):
                            for u in range((i + ahead) * comps, min((i + ahead + 1) * comps, len(units))):
                                scores(u)
                            turn(i)
                            if i:
                                values(i - 1)
                            if len(finish) and i % heads == 2:
                                out_turn(finish.pop(0))
                        values(len(pairs) - 1)
                        if finish:
                            out_turn(finish.pop(0))

                    def copy_pt(act, i):
                        qt, h = pairs[i]
                        act.wait_ge(trp, i + 1)
                        if i >= 2:
                            act.wait_ge(pvd, i - 1)
                        nc.scalar.copy(pt[:, i % 2, 0:nk(qt) * P], ps[2 + i % 2][:, 0:nk(qt) * P]).then_inc(cpd, 1)

                    @block.scalar
                    def _(act):
                        for u, (qt, h, cc) in enumerate(units):
                            n = nk(qt) * P
                            act.wait_ge(mxd, u + 1)
                            if u >= 4:
                                act.wait_ge(trp, (u - 4) // comps + 1)
                            nc.scalar.activation(pb[:, u % 4, 0:n], sbank(u)[:, 0:n], ACT.Exp, bias=mx[:, u % 4:u % 4 + 1],
                                                 scale=scale, accum_out=rs[:, u:u + 1]).then_inc(exd, 1)
                            if u % comps == comps - 1 and u // comps >= 1:
                                copy_pt(act, u // comps - 1)
                        copy_pt(act, len(pairs) - 1)

                    def after_exp(dve, link, u):
                        dve.wait_ge(exd, u + 1)
                        link(nc.vector.reciprocal(rr[:, u:u + 1], rs[:, u:u + 1]))
                        if diff:
                            if u >= 4:
                                dve.wait_ge(trp, (u - 4) // 2 + 1)
                            if u % 2:
                                link(nc.vector.tensor_tensor(rr[:, u:u + 1], rr[:, u:u + 1], lamcol, ALU.mult))
                            ins = nc.vector.tensor_scalar(dg[:, u % 4, :], ident[:, :], rr[:, u:u + 1], None, ALU.mult)
                            if u % 2:
                                ins.then_inc(dgd, 1)

                    @block.vector
                    def _(dve):
                        link = chain(dve, ch)
                        done = [0]

                        def tile_out(qt):
                            dve.wait_ge(pvd, heads * (qt + 1))
                            if diff:
                                nc.vector.tensor_copy(outN[:, qt, :], ps[4 + qt % 2][:, :]).then_inc(ond, 1)
                                return
                            if qt:
                                dve.wait_ge(otd, (heads * width // 512) * qt)
                            u0 = qt * heads
                            half = 1 if not mem else 2
                            for g in range(half):
                                hh = heads // half
                                ins = nc.vector.tensor_tensor(
                                    on[:, g * 512:(g + 1) * 512].rearrange("p (h d) -> p h d", h=hh),
                                    (ps[4 + qt % 2] if not mem else ps[4 + g])[:, :].rearrange("p (h d) -> p h d", h=hh),
                                    rr[:, u0 + g * hh:u0 + (g + 1) * hh].unsqueeze(2).broadcast_to([P, hh, width]), ALU.mult)
                            ins.then_inc(ond, 1)

                        def tile_turned(qt):
                            if join is not None and qt == 0:
                                dve.wait_ge(joined, 1)
                            for g in range(heads * width // 512):
                                dve.wait_ge(otd, (heads * width // 512) * qt + g + 1)
                                nc.vector.tensor_copy(outT[:, 4 * g:4 * g + 4, qt * P:(qt + 1) * P],
                                                      ps[6 + g][:, :].rearrange("p (j n) -> p j n", j=4)).then_inc(oed, 1)

                        todo = []
                        for u, (qt, h, cc) in enumerate(units):
                            n = nk(qt) * P
                            dve.wait_ge(sc, u + 1)
                            if u >= 4:
                                dve.wait_ge(exd, u - 3)
                            link(nc.vector.reduce_max(mx[:, u % 4:u % 4 + 1], sbank(u)[:, 0:n], AX))
                            nc.vector.tensor_scalar(mx[:, u % 4:u % 4 + 1], mx[:, u % 4:u % 4 + 1], -scale, None,
                                                    ALU.mult).then_inc(mxd, 1)
                            if u >= comps:
                                after_exp(dve, link, u - comps)
                            if todo and todo[0][0] <= u:
                                t = todo.pop(0)
                                (tile_out if t[1] == 0 else tile_turned)(t[2])
                            if h == heads - 1 and cc == comps - 1:
                                todo += [(u + 2 * comps, 0, qt)] + ([] if diff else [(u + 4 * comps, 1, qt)])
                        for u in range(len(units) - comps, len(units)):
                            after_exp(dve, link, u)
                        for t in todo:
                            (tile_out if t[1] == 0 else tile_turned)(t[2])

        def decode_attention(tag, kind, qT, kT, vN, outN, c0, bias_l=None, CT=None, L2=None, lamcol=None,
                             chunk_range=None):
            fox, diff, mem = kind == "fox", kind == "diff", kind == "mem"
            J = 8 if mem else 4
            W = 256 if mem else 128
            n = PAST if mem else KS
            kb = 2 if mem else 3
            scale = MSC if mem else SC
            with ExitStack() as c:
                qb = sb(c, tag + "qb", [P, J, NB, 32])
                kt = sb(c, tag + "kt", [P, 2, J, n])
                vn = None if mem else sb(c, tag + "vn", [TD, 2, 512])
                pb = sb(c, tag + "p", [P, 2, n])
                at = sb(c, tag + "at", [P, kb, P])
                ob = sb(c, tag + "o", [P, 2, W])
                mx = sb(c, tag + "mx", [P, NB])
                rs = sb(c, tag + "rs", [P, NB])
                dg = sb(c, tag + "dg", [P, 2, P]) if diff else None
                ones = sb(c, tag + "ones", [64, KS]) if fox else None
                comb = sb(c, tag + "comb", [P, P]) if diff else None
                sgn = sb(c, tag + "sgn", [P, 3]) if diff else None

                def chunk(b):
                    return c0 + (b if mem else b // 2)

                def cached(b, i):
                    if mem:
                        return slot2(chunk(b))[:, 2 * i:2 * i + 2, :]
                    return slot(chunk(b))[:, 4 * (b % 2) + 2 * i:4 * (b % 2) + 2 * i + 2, :]

                vl = [sem(c, f"{tag}vl{i}") for i in range(2)]
                od = [sem(c, f"{tag}od{i}") for i in range(2)]
                qz, qd, tr, eva, evd, kn, sc, mxd, exd, dgd, atd, acp, pvd, ocd, ch, cl = (
                    sem(c, tag + x) for x in ("qz", "qd", "tr", "eva", "evd", "kn", "sc", "mxd", "exd", "dgd", "atd",
                                              "acp", "pvd", "ocd", "ch", "cl"))
                banks = J // 2
                streams_of_chunk = 1 if mem else 2

                def bank(b, g):
                    return ps[g if mem else 2 * (b % 2) + g]

                with nc.Block() as block:
                    @block.sync
                    def _(sp):
                        if diff:
                            sp.dma_start(comb[:, :], a["c_comb"]).then_inc(cl, 16)
                            sp.dma_start(sgn[:, 0:2], a["c_sgn"]).then_inc(cl, 16)
                        if not mem:
                            for b in range(2):
                                sp.dma_start(vn[:, b, :], vN[b * TD:(b + 1) * TD, TP, :]).then_inc(vl[b], 16)
                        next_chunk = chunk_range[0]
                        for b in range(NB):
                            sp.wait_ge(ocd, b + 1)
                            for h in range(8 if fox else 4):
                                p0 = TD * h if fox else 32 * h
                                o0 = (h % 2) * HD if fox else 0
                                w = HD if fox else W
                                sp.dma_start(outN[b * TD:(b + 1) * TD, h * w:(h + 1) * w],
                                             ob[p0:p0 + TD, b % 2, o0:o0 + w]).then_inc(od[b % 2], 16)
                            if b + 2 < NB and not mem:
                                sp.dma_start(vn[:, b % 2, :], vN[(b + 2) * TD:(b + 3) * TD, TP, :]).then_inc(vl[b % 2], 16)
                            if (b + 1) % streams_of_chunk == 0 and next_chunk < chunk_range[1]:
                                load_chunks(sp, next_chunk, next_chunk + 1)
                                next_chunk += 1
                        assert next_chunk == chunk_range[1]
                        for s in range(2):
                            sp.wait_ge(od[s], 16 * (8 if fox else 4) * (NB // 2))

                    @block.gpsimd
                    def _(pool):
                        nc.gpsimd.memset(qb[:, :, :, :], 0.0).then_inc(qz, 1)
                        if fox:
                            nc.gpsimd.memset(ones[:, :], 1.0).then_inc(qz, 1)
                        if not mem:
                            for b in range(NB):
                                if b >= 2:
                                    pool.wait_ge(sc, b - 1)
                                nc.gpsimd.tensor_copy(kt[:, b % 2, :, PAST:KS],
                                                      kT[:, :, SEQ + b * TD:SEQ + (b + 1) * TD]).then_inc(kn, 1)

                    @block.tensor
                    def _(pe):
                        def turn_keys(b):
                            wait_chunk(pe, chunk(b))
                            for g in range(banks):
                                before = b - 1 if mem else b - 2
                                if before >= 0:
                                    pe.wait_ge(evd if g % 2 == 0 else eva, (banks // 2) * before + g // 2 + 1)
                                for jj in range(2):
                                    for k in range(2):
                                        ins = nc.tensor.transpose(
                                            bank(b, g)[:, jj * PAST + k * P:jj * PAST + (k + 1) * P],
                                            cached(b, 0)[:, k, (2 * g + jj) * P:(2 * g + jj + 1) * P], ident[:, :])
                                ins.then_inc(tr, 1)

                        def scores(b):
                            pe.wait_ge(evd, (banks // 2) * (b + 1))
                            pe.wait_ge(eva, (banks // 2) * (b + 1))
                            S = ps[4 + b % 2]
                            if b >= 2:
                                pe.wait_ge(exd, b - 1)
                            if not mem:
                                pe.wait_ge(kn, b + 1)
                            for step in range(2 if mem else 1):
                                for j in range(4):
                                    f = 2 * j + step if mem else j
                                    ins = nc.tensor.matmul(S[32 * j:32 * j + 32, 0:n], qb[:, f, b, :],
                                                           kt[:, b % 2, f, :], start=step == 0,
                                                           stop=not fox and step == (1 if mem else 0),
                                                           skip_group_check=True)
                            if fox:
                                nc.tensor.matmul(S[:, 0:n], bias_l[:, b, :], CT[:, :], start=False, stop=False,
                                                 skip_group_check=True)
                                ins = nc.tensor.matmul(S[:, 0:n], L2[:, b, :], ones[:, :], start=False, stop=True,
                                                       skip_group_check=True)
                            ins.then_inc(sc, 1)

                        def turn(b):
                            pe.wait_ge(dgd if diff else exd, b + 1)
                            if b:
                                pe.wait_ge(acp, b)
                            for k in range(kb):
                                m = P if k < 2 else TD
                                ins = nc.tensor.matmul(ps[6][0:m, k * P:(k + 1) * P], pb[:, b % 2, k * P:k * P + m],
                                                       dg[:, b % 2, :] if diff else ident[:, :], start=True, stop=True)
                            ins.then_inc(atd, 1)

                        def values(b):
                            s = b % 2
                            pe.wait_ge(acp, b + 1)
                            if not mem:
                                pe.wait_ge(vl[s], 16 * (b // 2 + 1))
                            if b:
                                pe.wait_ge(ocd, b)
                            for k in range(kb):
                                for j in range(4):
                                    if k < 2:
                                        ins = nc.tensor.matmul(ps[7][32 * j:32 * j + 32, 0:W], at[:, k, 32 * j:32 * j + 32],
                                                               cached(b, 1)[:, k, j * W:(j + 1) * W], start=k == 0,
                                                               stop=k == kb - 1, skip_group_check=True)
                                    else:
                                        ins = nc.tensor.matmul(ps[7][32 * j:32 * j + 32, 0:W],
                                                               at[0:TD, k, 32 * j:32 * j + 32],
                                                               vn[:, s, j * W:(j + 1) * W], start=False, stop=True,
                                                               skip_group_check=True)
                            ins.then_inc(pvd, 1)

                        warm_up(ps[0])
                        pe.wait_ge(qd, 1)
                        if fox:
                            pe.wait_ge(qz, 2)
                        turn_keys(0)
                        scores(0)
                        turn_keys(1)
                        for b in range(NB):
                            if b + 1 < NB:
                                scores(b + 1)
                            if b + 2 < NB:
                                turn_keys(b + 2)
                            if b:
                                values(b - 1)
                            turn(b)
                        values(NB - 1)

                    @block.scalar
                    def _(act):
                        def keys(b):
                            for g in range(1, banks, 2):
                                act.wait_ge(tr, banks * b + g + 1)
                                if b >= 2:
                                    act.wait_ge(sc, b - 1)
                                nc.scalar.copy(kt[:, b % 2, 2 * g:2 * g + 2, 0:PAST],
                                               bank(b, g)[:, :].rearrange("p (j n) -> p j n", j=2)).then_inc(eva, 1)

                        def probabilities(b):
                            act.wait_ge(mxd, b + 1)
                            if b >= 2:
                                act.wait_ge(atd, b - 1)
                            nc.scalar.activation(pb[:, b % 2, :], ps[4 + b % 2][:, 0:n], ACT.Exp, bias=mx[:, b:b + 1],
                                                 scale=scale, accum_out=rs[:, b:b + 1]).then_inc(exd, 1)

                        keys(0)
                        probabilities(0)
                        keys(1)
                        for b in range(NB):
                            if b + 1 < NB:
                                probabilities(b + 1)
                            if b + 2 < NB:
                                keys(b + 2)
                            act.wait_ge(atd, b + 1)
                            if b:
                                act.wait_ge(pvd, b)
                            if not mem:
                                nc.scalar.copy(at[0:TD, 2, :], ps[6][0:TD, 2 * P:3 * P])
                            nc.scalar.copy(at[:, 0:2, :], ps[6][:, 0:2 * P].rearrange("p (k n) -> p k n", k=2)).then_inc(acp, 1)

                    @block.vector
                    def _(dve):
                        link = chain(dve, ch)

                        def keys(b):
                            for g in range(0, banks, 2):
                                dve.wait_ge(tr, banks * b + g + 1)
                                if b >= 2:
                                    dve.wait_ge(sc, b - 1)
                                nc.vector.tensor_copy(kt[:, b % 2, 2 * g:2 * g + 2, 0:PAST],
                                                      bank(b, g)[:, :].rearrange("p (j n) -> p j n", j=2)).then_inc(evd, 1)

                        def out(b):
                            dve.wait_ge(pvd, b + 1)
                            if b >= 2:
                                dve.wait_ge(od[b % 2], 16 * (8 if fox else 4) * (b // 2))
                            if diff:
                                nc.vector.tensor_copy(ob[:, b % 2, :], ps[7][:, 0:W]).then_inc(ocd, 1)
                            else:
                                nc.vector.tensor_scalar(ob[:, b % 2, :], ps[7][:, 0:W], rs[:, b:b + 1], None,
                                                        ALU.mult).then_inc(ocd, 1)
                            if (b + 1) % streams_of_chunk == 0:
                                dve.sem_inc(used, 1)

                        def maxima(b):
                            dve.wait_ge(sc, b + 1)
                            link(nc.vector.reduce_max(mx[:, b:b + 1], ps[4 + b % 2][:, 0:n], AX))
                            nc.vector.tensor_scalar(mx[:, b:b + 1], mx[:, b:b + 1], -scale, None, ALU.mult).then_inc(mxd, 1)

                        def factors(b):
                            dve.wait_ge(exd, b + 1)
                            link(nc.vector.reciprocal(rs[:, b:b + 1], rs[:, b:b + 1]))
                            if diff:
                                link(nc.vector.tensor_tensor(rs[:, b:b + 1], rs[:, b:b + 1], sgn[:, 2:3], ALU.mult))
                                if b >= 2:
                                    dve.wait_ge(atd, b - 1)
                                nc.vector.tensor_scalar(dg[:, b % 2, :], comb[:, :], rs[:, b:b + 1], None,
                                                        ALU.mult).then_inc(dgd, 1)

                        dve.wait_ge(qz, 1)
                        q = qT[:, :, SEQ:NTOK].rearrange("p j (b t) -> p j b t", b=NB)
                        if mem:
                            for j in range(J):
                                ins = nc.vector.tensor_copy(qb[:, j, :, 0:TD], q[:, j])
                        else:
                            for j in range(J):
                                nc.vector.tensor_copy(qb[0:64, j, :, 0:TD], q[0:64, j])
                                ins = nc.vector.tensor_copy(qb[64:P, j, :, TD:32], q[64:P, j])
                        ins.then_inc(qd, 1)
                        if diff:
                            dve.wait_ge(cl, 32)
                            link(nc.vector.scalar_tensor_tensor(out=sgn[:, 2:3], in0=sgn[:, 1:2], scalar=lamcol,
                                                                in1=sgn[:, 0:1], op0=ALU.mult, op1=ALU.add))
                        keys(0)
                        maxima(0)
                        keys(1)
                        factors(0)
                        for b in range(NB):
                            if b + 1 < NB:
                                maxima(b + 1)
                            if b + 2 < NB:
                                keys(b + 2)
                            if b:
                                out(b - 1)
                            if b + 1 < NB:
                                factors(b + 1)
                        out(NB - 1)

        def mix_block(foxN, diffN, mixT, chunk_range):
            with ExitStack() as c:
                sq = sb(c, "msq", [P, T, 512])
                ss = sb(c, "mss", [P, T * DH])
                gd = sb(c, "mgd", [P, P])
                sqd, ssd, sr, rd, nd, tr, ev, ld, ch = (sem(c, "m" + n) for n in ("sqd", "ssd", "sr", "rd", "nd", "tr",
                                                                                  "ev", "ld", "ch"))
                with nc.Block() as block:
                    @block.sync
                    def _(sp):
                        sp.dma_start(gd[:, :], a["g_diff"].partition_broadcast(P).rearrange("p l d -> p (l d)")).then_inc(ld, 16)
                        load_chunks(sp, *chunk_range)
                        sp.wait_ge(ld, 16)

                    @block.scalar
                    def _(act):
                        nc.scalar.activation(sq[:, :, :], diffN[:, :, :], ACT.Square).then_inc(sqd, 1)
                        act.wait_ge(ssd, 1)
                        nc.scalar.activation(ss[:, :], ss[:, :], ACT.Sqrt).then_inc(sr, 1)
                        for i in range(T + 1):
                            act.wait_ge(tr, i + 1)
                            j0, t = (0, TP) if i == 0 else (4, i - 1)
                            nc.scalar.copy(mixT[:, j0:j0 + 4, t * P:(t + 1) * P],
                                           ps[i % 4][:, :].rearrange("p (j n) -> p j n", j=4)).then_inc(ev, 1)

                    @block.vector
                    def _(dve):
                        link = chain(dve, ch)
                        dve.wait_ge(sqd, 1)
                        link(nc.vector.reduce_sum(ss[:, :], sq[:, :, :].rearrange("p t (h d) -> p (t h) d", h=DH), AX))
                        nc.vector.tensor_scalar(ss[:, :], ss[:, :], 1.0 / 128, EPS, ALU.mult, ALU.add).then_inc(ssd, 1)
                        dve.wait_ge(ld, 16)
                        link(nc.vector.tensor_scalar(gd[:, :], gd[:, :], 1.0 - LAM_INIT, None, ALU.mult))
                        dve.wait_ge(sr, 1)
                        link(nc.vector.reciprocal(ss[:, :], ss[:, :]))
                        for t in range(T):
                            for h in range(DH):
                                x = diffN[:, t, h * P:(h + 1) * P]
                                ins = nc.vector.scalar_tensor_tensor(out=x, in0=x, scalar=ss[:, t * DH + h:t * DH + h + 1],
                                                                     in1=gd[:, :], op0=ALU.mult, op1=ALU.mult)
                            ins.then_inc(nd, 1)

                    @block.tensor
                    def _(pe):
                        for i in range(T + 1):
                            if i:
                                pe.wait_ge(nd, i)
                            if i >= 4:
                                pe.wait_ge(ev, i - 3)
                            src = foxN if i == 0 else diffN[:, i - 1, :]
                            for j in range(4):
                                ins = nc.tensor.transpose(ps[i % 4][:, j * P:(j + 1) * P], src[:, j * P:(j + 1) * P],
                                                          ident[:, :])
                            ins.then_inc(tr, 1)

        def residual_block(tag, xT, hN, c0, chunk_range, gain, load=None, mem=None, rows=None,
                           router=None):
            nm = 2 if mem is not None else 0
            nj = nm + T
            with ExitStack() as c:
                xH = dual(c, tag + "xH", [P, KT, NTOK])
                split = Split(c, tag)
                sq = sb(c, tag + "sq", [P, D])
                ss = sb(c, tag + "ss", [P, nj])
                rs = sb(c, tag + "rs", [P, nj])
                xs = sb(c, tag + "xs", [P, 2, D])
                mm, ev, squared, mean, root, inverse, scaled, turned, read = (
                    sem(c, tag + n) for n in ("mm", "ev", "squared", "mean", "root", "inverse", "scaled", "turned", "read"))
                ld = [sem(c, f"{tag}ld{t}") for t in range(T)]
                lm = [sem(c, f"{tag}lm{t}") for t in range(nm)]
                written = [sem(c, f"{tag}wr{i}") for i in range(2)] if rows is not None else None
                groups = [(t, half) for t in range(T) for half in range(2)]
                NBANKS = 5 if router is not None else 6
                rin = sem(c, tag + "rin") if router is not None else None

                def source(n):
                    return mem[0][:, n, :] if n < nm else hN[:, n - nm, :]

                with nc.Block() as block:
                    @block.sync
                    def _(sp):
                        for t in range(nm):
                            sp.dma_start(mem[0][:, t, :], a["mem_prompt"][0, t * P:(t + 1) * P, :]).then_inc(lm[t], 16)
                        if load is not None:
                            for t in range(T):
                                sp.dma_start(hN[:, t, :], load(t)).then_inc(ld[t], 16)
                        if router is not None:
                            with nc.allow_non_contiguous_dma("narrow router"):
                                sp.dma_start(router[:, :, 0:NG], a["w_group"][0].rearrange("(k p) n -> p k n", p=P)).then_inc(rin, 16)
                                sp.dma_start(router[:, :, NG:], a["w_erouter"][0].rearrange("(k p) n -> p k n", p=P)).then_inc(rin, 16)
                        load_chunks(sp, *chunk_range)
                        if rows is not None:
                            for t in range(T):
                                sp.wait_ge(scaled, nm + t + 1)
                                sp.dma_start(rows[t * P:(t + 1) * P, :], xs[:, (nm + t) % 2, :]).then_inc(
                                    written[(nm + t) % 2], 16)
                        if rows is not None:
                            for i in range(2):
                                sp.wait_ge(written[i], 16 * ((T + 1 - i) // 2))

                    @block.tensor
                    def _(pe):
                        def logits(t):
                            pe.wait_ge(rin, 32)
                            for k in range(KT):
                                nc.tensor.matmul(LOGITS[:, t * (NG + NE):(t + 1) * (NG + NE)], xT[:, k, t * P:(t + 1) * P],
                                                 router[:, k, :], start=k == 0, stop=k == KT - 1)

                        def turn(n):
                            pe.wait_ge(scaled, n + 1)
                            if n:
                                pe.wait_ge(read, n)
                            if router is not None and n > nm:
                                logits(n - 1 - nm)
                            for k in range(KT):
                                ins = nc.tensor.transpose(ps[6 + k // 4][:, (k % 4) * P:(k % 4 + 1) * P],
                                                          xs[:, n % 2, k * P:(k + 1) * P], ident[:, :])
                            ins.then_inc(turned, 1)

                        warm_up(ps[0])
                        for g, (t, half) in enumerate(groups):
                            if half == 0:
                                split.ready(pe)
                            if g >= NBANKS:
                                pe.wait_ge(ev, g - NBANKS + 1)
                            for k in range(KT):
                                if t == 0:
                                    split.ready(pe)
                                ins = products(ps[g % NBANKS][:, :], xH[:, k, t * P:(t + 1) * P], xT[:, k, t * P:(t + 1) * P],
                                               slot(c0 + 2 + half)[:, k, :], slot(c0 + half)[:, k, :], k == 0, k == KT - 1)
                            ins.then_inc(mm, 1)
                            if t == 0 and half < nm:
                                turn(half)
                            if half == 1 and t:
                                turn(nm + t - 1)
                        pe.wait_ge(mm, len(groups))
                        pe.sem_inc(used, 4)
                        turn(nj - 1)
                        if router is not None:
                            pe.wait_ge(read, nj)
                            logits(T - 1)

                    @block.scalar
                    def _(act):
                        split.high(act, xH[:, :, 0:P], xT[:, :, 0:P])
                        for half in range(2):
                            split.high_chunk(act, c0 + half, c0 + 2 + half)
                        for n in range(nj):
                            t = n - nm + 1
                            if 0 < t < T:
                                split.high(act, xH[:, :, t * P:(t + 1) * P], xT[:, :, t * P:(t + 1) * P])
                            if n < nm:
                                act.wait_ge(lm[n], 16)
                            else:
                                act.wait_ge(ev, 2 * (n - nm) + 2)
                            if n:
                                act.wait_ge(squared, n)
                            nc.scalar.activation(sq[:, :], source(n), ACT.Square, accum_out=ss[:, n:n + 1]).then_inc(squared, 1)
                            act.wait_ge(mean, n + 1)
                            nc.scalar.activation(rs[:, n:n + 1], ss[:, n:n + 1], ACT.Sqrt).then_inc(root, 1)
                            act.wait_ge(inverse, n + 1)
                            if n >= 2:
                                act.wait_ge(turned, n - 1)
                                if rows is not None:
                                    act.wait_ge(written[n % 2], 16 * (n // 2))
                            nc.scalar.activation(xs[:, n % 2, :], source(n), ACT.Copy, scale=rs[:, n:n + 1]).then_inc(scaled, 1)

                    @block.vector
                    def _(dve):
                        def stats(n):
                            dve.wait_ge(squared, n + 1)
                            nc.vector.tensor_scalar(ss[:, n:n + 1], ss[:, n:n + 1], 1.0 / D, EPS, ALU.mult,
                                                    ALU.add).then_inc(mean, 1)
                            dve.wait_ge(root, n + 1)
                            nc.vector.reciprocal(rs[:, n:n + 1], rs[:, n:n + 1]).then_inc(inverse, 1)

                        def read_out(n):
                            dve.wait_ge(turned, n + 1)
                            dst, t, gi = (mem[1], n, mem[2]) if n < nm else (xT, n - nm, gain)
                            for h in range(2):
                                ins = nc.vector.tensor_tensor(
                                    dst[:, 4 * h:4 * h + 4, t * P:(t + 1) * P],
                                    ps[6 + h][:, :].rearrange("p (k n) -> p k n", k=4),
                                    gcol[:, gi, 4 * h:4 * h + 4].unsqueeze(2).broadcast_to([P, 4, P]), ALU.mult)
                            ins.then_inc(read, 1)

                        split.low(dve, xH[:, :, 0:P], xT[:, :, 0:P])
                        for half in range(2):
                            split.low_chunk(dve, c0 + half, c0 + 2 + half)
                        for n in range(nm):
                            stats(n)
                        for g, (t, half) in enumerate(groups):
                            if half == 0 and t + 1 < T:
                                o = (t + 1) * P
                                split.low(dve, xH[:, :, o:o + P], xT[:, :, o:o + P])
                            dve.wait_ge(mm, g + 1)
                            if load is not None:
                                dve.wait_ge(ld[t], 16)
                            h = hN[:, t, half * 512:(half + 1) * 512]
                            nc.vector.tensor_tensor(h, ps[g % NBANKS][:, :], h, ALU.add).then_inc(ev, 1)
                            if half == 1:
                                stats(nm + t)
                            if t == 0 and half < nm:
                                read_out(half)
                            if half == 1 and t:
                                read_out(nm + t - 1)
                        read_out(nj - 1)

        def memory_block(mT, mkT, mvN):
            with ExitStack() as c:
                mkN = sb(c, "mkN", [P, 2, D])
                mH = dual(c, "mH", [P, KT, MEM])
                split = Split(c, "k")
                mm, ev, kst = sem(c, "kmm"), sem(c, "kev"), sem(c, "kst")
                out = [a["p_mk"], a["p_mv"]]
                groups = [("mm", m, half, t) for m in range(2) for half in range(2) for t in range(2)]
                groups = groups[:4] + groups[4:] + [("tr", t, half) for t in range(2) for half in range(2)]
                with nc.Block() as block:
                    @block.sync
                    def _(sp):
                        for m, buf in enumerate((mkN, mvN)):
                            c0 = (W_MV, W_MQ)[m]
                            load_chunks(sp, c0, c0 + 2)
                            sp.wait_ge(ev, 4 * m + 4)
                            rows_of = out[m].rearrange("l b (k p) h d -> p (l b k) (h d)", p=P)
                            if m == 0:
                                sp.dma_start(rows_of, buf[:, :, :]).then_inc(kst, 16)
                            else:
                                store(sp, rows_of, buf[:, :, :])
                        sp.wait_ge(kst, 16)

                    @block.tensor
                    def _(pe):
                        warm_up(ps[0])
                        for g, grp in enumerate(groups):
                            if g >= 8:
                                pe.wait_ge(ev, g - 7)
                            if grp[0] == "mm":
                                _, m, half, t = grp
                                ch = (W_MK, W_MV)[m] + half
                                if g == 0:
                                    split.ready(pe)
                                for k in range(KT):
                                    if t == 0:
                                        split.ready(pe)
                                    ins = products(ps[g % 8][:, :], mH[:, k, t * P:(t + 1) * P], mT[:, k, t * P:(t + 1) * P],
                                                   slot(ch + 2)[:, k, :], slot(ch)[:, k, :], k == 0, k == KT - 1)
                            else:
                                _, t, half = grp
                                pe.wait_ge(ev, 4)
                                for j in range(4):
                                    o = half * 512 + j * P
                                    ins = nc.tensor.transpose(ps[g % 8][:, j * P:(j + 1) * P], mkN[:, t, o:o + P], ident[:, :])
                            ins.then_inc(mm, 1)
                            if grp[0] == "mm" and grp[3] == 1:
                                pe.wait_ge(mm, g + 1)
                                pe.sem_inc(used, 3 if half else 1)

                    @block.scalar
                    def _(act):
                        split.high(act, mH[:, :, :], mT[:, :, :])
                        split.high_chunk(act, W_MK, W_MK + 2)
                        split.high_chunk(act, W_MK + 1, W_MK + 3)
                        split.high_chunk(act, W_MV, W_MV + 2, free=W_MK + 1)
                        split.high_chunk(act, W_MV + 1, W_MV + 3, free=W_MK + 2)

                    @block.vector
                    def _(dve):
                        split.low(dve, mH[:, :, :], mT[:, :, :])
                        split.low_chunk(dve, W_MK, W_MK + 2)
                        for g, grp in enumerate(groups):
                            if g in (0, 2, 4):
                                ch = {0: W_MK + 1, 2: W_MV, 4: W_MV + 1}[g]
                                split.low_chunk(dve, ch, ch + 2)
                            dve.wait_ge(mm, g + 1)
                            if grp[0] == "mm":
                                _, m, half, t = grp
                                dst, src = (mkN, mvN)[m][:, t, half * 512:(half + 1) * 512], ps[g % 8][:, :]
                            else:
                                _, t, half = grp
                                dst = mkT[:, 4 * half:4 * half + 4, t * P:(t + 1) * P]
                                src = ps[g % 8][:, :].rearrange("p (j n) -> p j n", j=4)
                            nc.vector.tensor_copy(dst, src).then_inc(ev, 1)

        def query_block(nT, qT, chunk_range):
            half = NTOK // 2
            with ExitStack() as c:
                nH = dual(c, "qnH", [P, KT, NTOK])
                split = Split(c, "q")
                mm, eva, evd = sem(c, "qmm"), sem(c, "qeva"), sem(c, "qevd")
                with nc.Block() as block:
                    @block.sync
                    def _(sp):
                        load_chunks(sp, *chunk_range)
                        sp.wait_ge(stored, ns[0])

                    @block.tensor
                    def _(pe):
                        warm_up(ps[0])
                        for g in range(KT):
                            if g >= 4:
                                pe.wait_ge(eva, g - 3)
                                pe.wait_ge(evd, g - 3)
                            j = g % 4
                            w = slot(W_MQ + g // 4)[:, :, j * P:(j + 1) * P]
                            wh = slot(W_MQ + 2 + g // 4)[:, :, j * P:(j + 1) * P]
                            for k in range(KT):
                                if j == 0:
                                    split.ready(pe, 2 if g == 0 else 1)
                                for x in range(2):
                                    o = x * half
                                    ins = products(ps[2 * j + x][:, 0:half], wh[:, k, :], w[:, k, :],
                                                   nH[:, k, o:o + half], nT[:, k, o:o + half], k == 0, k == KT - 1)
                            ins.then_inc(mm, 1)
                            if j == 3:
                                pe.wait_ge(mm, g + 1)
                                pe.sem_inc(used, 3 if g // 4 else 1)

                    @block.scalar
                    def _(act):
                        wait_chunk(act, W_MQ)
                        for k in range(KT):
                            split.high(act, nH[:, k, :], nT[:, k, :])
                            split.high(act, slot(W_MQ + 2)[:, k, :], slot(W_MQ)[:, k, :])
                        split.high_chunk(act, W_MQ + 1, W_MQ + 3)
                        for g in range(KT):
                            act.wait_ge(mm, g + 1)
                            nc.scalar.copy(qT[:, g, 0:half], ps[2 * (g % 4)][:, 0:half]).then_inc(eva, 1)

                    @block.vector
                    def _(dve):
                        for k in range(KT):
                            split.low(dve, nH[:, k, :], nT[:, k, :])
                            split.low(dve, slot(W_MQ + 2)[:, k, :], slot(W_MQ)[:, k, :])
                        split.low_chunk(dve, W_MQ + 1, W_MQ + 3)
                        for g in range(KT):
                            dve.wait_ge(mm, g + 1)
                            nc.vector.tensor_copy(qT[:, g, half:], ps[2 * (g % 4) + 1][:, 0:half]).then_inc(evd, 1)

        def turn_block(xN, dstT):
            with ExitStack() as c:
                tr, ev = sem(c, "ttr"), sem(c, "tev")
                with nc.Block() as block:
                    @block.tensor
                    def _(pe):
                        for k in range(KT):
                            ins = nc.tensor.transpose(ps[k // 4][:, (k % 4) * P:(k % 4 + 1) * P], xN[:, k * P:(k + 1) * P],
                                                      ident[:, :])
                        ins.then_inc(tr, 1)

                    @block.vector
                    def _(dve):
                        dve.wait_ge(tr, 1)
                        for h in range(2):
                            ins = nc.vector.tensor_copy(dstT[:, 4 * h:4 * h + 4, SEQ:NTOK],
                                                        ps[h][:, :].rearrange("p (k n) -> p k n", k=4))
                        ins.then_inc(ev, 1)
                        dve.wait_ge(ev, 1)

        def route_block(xg, gate, slots, idx, plan, tab):
            with ExitStack() as c:
                br = sb(c, "br", [P, NG + NE])
                cst = sb(c, "cst", [P, 128])
                tri = sb(c, "tri", [P, P])
                trib = sb(c, "trib", [P, P], BF16)
                oneb = sb(c, "oneb", [P, P], BF16)
                L = sb(c, "rL", [P, T, NG + NE])
                s5 = sb(c, "s5", [P, 12, T])
                g4 = sb(c, "g4", [P, 3, T, NG])
                Lm = sb(c, "Lm", [P, T, NG, EPG])
                e8 = sb(c, "e8", [P, 8, T, EPG])
                oh = sb(c, "oh", [P, 2, T, NE])
                pr = sb(c, "rpr", [P, 2, T, NE])
                M = sb(c, "rM", [P, T, NE], BF16)
                rk = sb(c, "rrk", [P, 4, 2, T])
                ov = sb(c, "rov", [P, 3, NE])
                place = sb(c, "rplace", [P, 4, NE])
                qm = sb(c, "rqm", [P, 2, NE, NE])
                bp = sb(c, "rbp", [P, 4, PAIRS])
                cmp = sb(c, "rcmp", [P, PAIRS, MAXB - 1])
                plx = sb(c, "rplx", [1, NBLK, PAIRS])
                pls = sb(c, "rpls", [1, NBLK])
                one32 = sb(c, "one32", [P, NE])
                ii = sb(c, "rii", [P, 4, 2, T], I32)
                addr = sb(c, "raddr", [P, 2 * T], U32)
                tok = sb(c, "rtok", [P, T], I32)
                blank = sb(c, "blank", [P, NBLK], U32)
                ld, mm, ex, exd, md, rd, pz, tin, sd, sc, ch, ach, ixl = (
                    sem(c, "r" + n) for n in ("ld", "mm", "ex", "exd", "md", "rd", "pz", "tin", "sd", "sc", "ch", "ach", "ixl"))
                with nc.Block() as block:
                    @block.sync
                    def _(sp):
                        sp.dma_start(br[:, 0:NG], a["b_group"].partition_broadcast(P).rearrange("p l d -> p (l d)")).then_inc(ld, 16)
                        sp.dma_start(br[:, NG:], a["b_erouter"].partition_broadcast(P).rearrange("p l d -> p (l d)")).then_inc(ld, 16)
                        sp.dma_start(cst[:, :], a["c_route"]).then_inc(ld, 16)
                        sp.dma_start(tri[:, :], a["c_tri"]).then_inc(ld, 16)
                        sp.dma_start(tok[:, :], a["c_tok"]).then_inc(ld, 16)
                        load_chunks(sp, W_MOE + 2, W_MOE + SLOTS)
                        sp.wait_ge(pz, 2)
                        sp.dma_start(tab.rearrange("(p c) o -> p (c o)", p=P), blank[:, :]).then_inc(tin, 16)
                        sp.wait_ge(sc, 16 * 2 * T)
                        sp.dma_start(idx[:, :], tab.rearrange("(p c) o -> p (c o)", p=P)).then_inc(ixl, 16)
                        sp.wait_ge(ixl, 16)

                    @block.gpsimd
                    def _(pool):
                        nc.gpsimd.memset(oneb[:, :], 1.0).then_inc(pz, 1)
                        nc.gpsimd.memset(blank[:, :], 2 * NTOK).then_inc(pz, 1)
                        nc.gpsimd.memset(one32[:, :], 1.0).then_inc(pz, 1)
                        nc.gpsimd.memset(xg[:, :], 0.0).then_inc(pz, 1)
                        pool.wait_ge(tin, 16)
                        pool.wait_ge(ld, 80)
                        pool.wait_ge(sd, 1)
                        for k in range(2):
                            for t in range(T):
                                pool.indirect_dma_start(
                                    out=tab, out_offset=bass.IndirectOffsetOnAxis(ap=addr[:, k * T + t:k * T + t + 1], axis=0),
                                    in_=tok[:, t:t + 1], in_offset=None).then_inc(sc, 16)
                        pool.wait_ge(pz, 4)

                    @block.tensor
                    def _(pe):
                        pe.wait_ge(md, 1)
                        pe.wait_ge(pz, 1)
                        for t in range(T):
                            for u in range(t + 1):
                                nc.tensor.matmul(ps[1][:, t * NE:(t + 1) * NE], (trib if u == t else oneb)[:, :], M[:, u, :],
                                                 start=u == 0, stop=u == t)
                        for t in range(T):
                            ins = nc.tensor.matmul(ps[2][:, 0:NE], oneb[:, :], M[:, t, :], start=t == 0, stop=t == T - 1)
                        ins.then_inc(mm, 1)

                    @block.scalar
                    def _(act):
                        act.wait_ge(ex, 1)
                        nc.scalar.activation(g4[:, 1], g4[:, 0], ACT.Exp).then_inc(exd, 1)
                        act.wait_ge(ex, 2)
                        nc.scalar.activation(e8[:, 1], e8[:, 0], ACT.Exp).then_inc(exd, 1)

                    @block.vector
                    def _(dve):
                        link = chain(dve, ch)
                        v = nc.vector
                        def bc(x, n):
                            return x.unsqueeze(2).broadcast_to([P, T, n])

                        def first(dst, src, top, w, n, eq, tmp):
                            link(v.tensor_tensor(eq, src, bc(top, n), ALU.is_equal))
                            link(v.tensor_tensor(eq, eq, w.unsqueeze(1).broadcast_to([P, T, n]), ALU.mult))
                            link(v.reduce_max(tmp, eq, AX))
                            link(v.tensor_tensor(dst, eq, bc(tmp, n), ALU.is_equal))

                        dve.wait_ge(ld, 80)
                        link(v.tensor_copy(trib[:, :], tri[:, :]))
                        link(v.tensor_tensor(L[:, :, :], LOGITS[:, 0:T * 36].rearrange("p (t n) -> p t n", t=T),
                                             br[:, :].unsqueeze(1).broadcast_to([P, T, 36]), ALU.add))
                        g = L[:, :, 0:NG]
                        link(v.reduce_max(s5[:, 0], g, AX))
                        v.tensor_tensor(g4[:, 0], g, bc(s5[:, 0], NG), ALU.subtract).then_inc(ex, 1)
                        first(g4[:, 2], g, s5[:, 0], cst[:, 0:4], NG, e8[:, 7, :, 0:4], s5[:, 1])
                        dve.wait_ge(exd, 1)
                        link(v.reduce_sum(s5[:, 2], g4[:, 1], AX))
                        link(v.reciprocal(s5[:, 3], s5[:, 2]))
                        link(v.tensor_tensor(Lm[:, :, :, :], L[:, :, NG:].rearrange("p t (g j) -> p t g j", g=NG),
                                             g4[:, 2].unsqueeze(3).broadcast_to([P, T, NG, EPG]), ALU.mult))
                        link(v.reduce_sum(e8[:, 2], Lm[:, :, :, :].rearrange("p t g j -> p t j g"), AX))
                        link(v.reduce_max(s5[:, 4], e8[:, 2], AX))
                        v.tensor_tensor(e8[:, 0], e8[:, 2], bc(s5[:, 4], EPG), ALU.subtract).then_inc(ex, 1)
                        dve.wait_ge(exd, 2)
                        link(v.reduce_sum(s5[:, 5], e8[:, 1], AX))
                        link(v.reciprocal(s5[:, 5], s5[:, 5]))
                        link(v.tensor_tensor(e8[:, 3], e8[:, 1], bc(s5[:, 5], EPG), ALU.mult))
                        link(v.reduce_max(s5[:, 6], e8[:, 3], AX))
                        first(e8[:, 4], e8[:, 3], s5[:, 6], cst[:, 4:12], EPG, e8[:, 7], s5[:, 1])
                        link(v.scalar_tensor_tensor(out=e8[:, 6], in0=e8[:, 4], scalar=-2.0, in1=e8[:, 3], op0=ALU.mult,
                                                    op1=ALU.add))
                        link(v.reduce_max(s5[:, 7], e8[:, 6], AX))
                        first(e8[:, 5], e8[:, 6], s5[:, 7], cst[:, 4:12], EPG, e8[:, 7], s5[:, 1])
                        for k in range(2):
                            ins = v.tensor_tensor(oh[:, k].rearrange("p t (g j) -> p t g j", g=NG),
                                                  g4[:, 2].unsqueeze(3).broadcast_to([P, T, NG, EPG]),
                                                  e8[:, 4 + k].unsqueeze(2).broadcast_to([P, T, NG, EPG]), ALU.mult)
                        link(ins)
                        v.tensor_tensor(M[:, :, :], oh[:, 0], oh[:, 1], ALU.add).then_inc(md, 1)
                        link(v.tensor_tensor(s5[:, 8], s5[:, 6], s5[:, 7], ALU.add))
                        link(v.reciprocal(s5[:, 8], s5[:, 8]))
                        link(v.tensor_tensor(s5[:, 9:11], s5[:, 6:8], s5[:, 3].unsqueeze(1).broadcast_to([P, 2, T]), ALU.mult))
                        link(v.tensor_tensor(gate[:, :, :], s5[:, 9:11], s5[:, 8].unsqueeze(1).broadcast_to([P, 2, T]), ALU.mult))
                        dve.wait_ge(mm, 1)
                        dve.wait_ge(pz, 3)
                        link(v.tensor_copy(ov[:, 0], ps[2][:, 0:NE]))
                        iota = cst[:, 53:53 + NE]
                        link(v.scalar_tensor_tensor(out=ov[:, 2], in0=ov[:, 0], scalar=float(NE), in1=iota, op0=ALU.mult,
                                                    op1=ALU.subtract))
                        key = ov[:, 2, 2:]
                        link(v.tensor_tensor(qm[:, 0, 2:, 2:], key.unsqueeze(1).broadcast_to([P, NE - 2, NE - 2]),
                                             key.unsqueeze(2).broadcast_to([P, NE - 2, NE - 2]), ALU.is_gt))
                        link(v.tensor_copy(place[:, 0], iota))
                        link(v.reduce_sum(place[:, 0, 2:], qm[:, 0, 2:, 2:], AX))
                        link(v.tensor_scalar(place[:, 0, 2:], place[:, 0, 2:], 2.0, None, ALU.add))
                        link(v.tensor_tensor(qm[:, 0], iota.unsqueeze(2).broadcast_to([P, NE, NE]),
                                             place[:, 0].unsqueeze(1).broadcast_to([P, NE, NE]), ALU.is_equal))
                        link(v.tensor_tensor(qm[:, 1], qm[:, 0], ov[:, 0].unsqueeze(1).broadcast_to([P, NE, NE]), ALU.mult))
                        link(v.reduce_sum(place[:, 1], qm[:, 1], AX))
                        link(v.reduce_max(bp[:, 0], place[:, 1].rearrange("p (n x) -> p n x", x=2), AX))
                        link(v.tensor_tensor(cmp[:, :, :], bp[:, 0].unsqueeze(2).broadcast_to([P, PAIRS, MAXB - 1]),
                                             cst[:, 44:44 + MAXB - 1].unsqueeze(1).broadcast_to([P, PAIRS, MAXB - 1]),
                                             ALU.is_gt))
                        link(v.reduce_sum(bp[:, 1], cmp[:, :, :], AX))
                        link(v.tensor_scalar(bp[:, 1], bp[:, 1], 1.0, None, ALU.add))
                        link(v.tensor_tensor_scan(bp[:, 2], one32[:, 0:PAIRS], bp[:, 1], 0.0, ALU.mult, ALU.add))
                        link(v.tensor_tensor(bp[:, 3], bp[:, 2], bp[:, 1], ALU.subtract))
                        link(v.tensor_scalar(bp[:, 3], bp[:, 3], float(P), None, ALU.mult))
                        link(v.tensor_tensor(place[:, 2].rearrange("p (n x) -> p n x", x=2),
                                             cst[:, 12:44].rearrange("p (n x) -> p n x", x=2),
                                             bp[:, 3].unsqueeze(2).broadcast_to([P, PAIRS, 2]), ALU.add))
                        link(v.tensor_tensor(qm[:, 1], qm[:, 0], place[:, 2].unsqueeze(2).broadcast_to([P, NE, NE]), ALU.mult))
                        link(v.reduce_sum(ov[:, 1], qm[:, 1].rearrange("p a e -> p e a"), AX))
                        for i, src in enumerate((ps[1][:, 0:T * NE].rearrange("p (t e) -> p t e", t=T),
                                                 ov[:, 1].unsqueeze(1).broadcast_to([P, T, NE]))):
                            for k in range(2):
                                ins = v.tensor_tensor(pr[:, k], oh[:, k], src, ALU.mult)
                            link(ins)
                            link(v.reduce_sum(rk[:, i], pr[:, :, :, :], AX))
                        link(v.tensor_copy(ii[:, 0], rk[:, 0]))
                        link(v.tensor_scalar(ii[:, 1], ii[:, 0], CAP.bit_length() - 1, CAP.bit_length() - 1,
                                             ALU.logical_shift_right, ALU.logical_shift_left))
                        link(v.tensor_tensor(rk[:, 0], rk[:, 0], rk[:, 1], ALU.add))
                        link(v.tensor_tensor(rk[:, 0], rk[:, 0], ii[:, 1], ALU.add))
                        link(v.tensor_copy(slots[:, :], rk[:, 0].rearrange("p k t -> p (k t)")))
                        link(v.tensor_copy(ii[:, 0], rk[:, 0]))
                        link(v.tensor_scalar(ii[:, 1], ii[:, 0], P - 1, None, ALU.bitwise_and))
                        link(v.tensor_scalar(ii[:, 2], ii[:, 0], 7, None, ALU.logical_shift_right))
                        v.scalar_tensor_tensor(out=addr[:, :], in0=ii[:, 1].rearrange("p k t -> p (k t)"), scalar=float(NBLK),
                                               in1=ii[:, 2].rearrange("p k t -> p (k t)"), op0=ALU.mult,
                                               op1=ALU.add).then_inc(sd, 1)
                        link(v.tensor_tensor(plx[:, :, :], bp[0:1, 2].unsqueeze(1).broadcast_to([1, NBLK, PAIRS]),
                                             cst[0:1, 53:53 + NBLK].unsqueeze(2).broadcast_to([1, NBLK, PAIRS]), ALU.is_le))
                        link(v.reduce_sum(pls[:, :], plx[:, :, :], AX))
                        link(v.tensor_copy(plan[:, 0:NBLK], pls[:, :]))
                        link(v.tensor_copy(plan[:, NBLK:NBLK + PAIRS], bp[0:1, 2]))
                        link(v.tensor_scalar(plan[:, LAST:LAST + 1], bp[0:1, 2, PAIRS - 1:], 1.0, None, ALU.subtract))
                        link(v.tensor_tensor(qm[0:1, 1], qm[0:1, 0], iota[0:1].unsqueeze(1).broadcast_to([1, NE, NE]), ALU.mult))
                        link(v.reduce_sum(place[0:1, 3], qm[0:1, 1], AX))
                        link(v.tensor_copy(plan[:, ORDER:], place[0:1, 3]))

        def expert_block(xg, idx, xs, ys, plan):
            with ExitStack() as c:
                xT = sb(c, "xT", [P, KT, P])
                sg = sb(c, "sg", [P, 512])
                hh = sb(c, "hh", [P, 512])
                hT = sb(c, "hT", [P, ET, P])
                yb = sb(c, "yb", [P, D])
                ix = sb(c, "ix", [P, 2], U32)
                copied, gathered, turned, xT_ready, w1_done, w3_done, silu_done, hid_done, hid_turned, hT_ready, w2_done, \
                    out_ready, out_stored, waited, all_stored = (sem(c, "e_" + n) for n in (
                        "copied", "gathered", "turned", "xT_ready", "w1_done", "w3_done", "silu_done", "hid_done",
                        "hid_turned", "hT_ready", "w2_done", "out_ready", "out_stored", "waited", "all_stored"))

                def w(j):
                    return slot(W_MOE + j) if j < 4 else slot2(W_MOE + j)

                def blocks(eng, first, body):
                    first()
                    n = eng.value_load(plan[0:1, NBLK + PAIRS - 1:NBLK + PAIRS], min_val=PAIRS, max_val=NBLK)
                    with eng.Fori(1, n) as q:
                        body(q)
                    return n

                with nc.Block() as block:
                    @block.sync
                    def _(sp):
                        with sp.Fori(0, PAIRS - 1) as p:
                            end = sp.value_load(plan[0:1, bass.ds(p + NBLK, 1)], min_val=1, max_val=NBLK)
                            experts = [sp.value_load(plan[0:1, bass.ds(p * 2 + (ORDER + 2 + x), 1)], min_val=0, max_val=NE - 1)
                                       for x in range(2)]
                            for j in range(6):
                                if j % 2 == 0:
                                    sp.wait_ge((w1_done, w3_done, w2_done)[j // 2], end)
                                src = a["w1" if j < 2 else "w3" if j < 4 else "w2"][0][bass.ds(experts[j % 2], 1)]
                                sp.dma_start(w(j), src.rearrange("a (k p) n -> p (a k) n", p=P)).then_inc(
                                    landed[(W_MOE + j) % SLOTS], 16)

                    @block.gpsimd
                    def _(pool):
                        bound = pool.to_reg(NTOK - 1)

                        def gather(q, column):
                            nc.gpsimd.tensor_copy(ix[:, 0:1], column).then_inc(copied, 1)
                            pool.wait_ge(copied, q + 1)
                            pool.sem_inc(waited, 1)
                            pool.indirect_dma_start(out=xg[:, :], out_offset=None, in_=xs,
                                                    in_offset=bass.IndirectOffsetOnAxis(ap=ix[:, 0:1], axis=0),
                                                    bounds_check=bound, oob_is_err=False).then_inc(gathered, 16)

                        def body(q):
                            pool.wait_ge(turned, q)
                            gather(q, idx[:, bass.ds(q, 1)])
                        blocks(pool, lambda: gather(0, idx[:, 0:1]), body)

                    @block.tensor
                    def _(pe):
                        def turn(q):
                            pe.wait_ge(gathered, q * 16 + 16)
                            for k in range(KT):
                                ins = nc.tensor.transpose(ps[k // 4][:, (k % 4) * P:(k % 4 + 1) * P], xg[:, k * P:(k + 1) * P],
                                                          ident[:, :])
                            ins.then_inc(turned, 1)

                        def up(q, pair):
                            pe.wait_ge(xT_ready, q + 1)
                            for m in range(2):
                                for x in range(2):
                                    c = W_MOE + 2 * m + x
                                    pe.wait_ge(landed[c % SLOTS], pair * 16 + landed_by[c])
                                for k in range(KT):
                                    for x in range(2):
                                        ins = nc.tensor.matmul(ps[2 + m][64 * x:64 * x + 64, :], xT[:, k, 64 * x:64 * x + 64],
                                                               w(2 * m + x)[:, k, :], start=k == 0, stop=k == KT - 1)
                                ins.then_inc((w1_done, w3_done)[m], 1)

                        def down(q, pair, free):
                            pe.wait_ge(hid_done, q + 1)
                            for k in range(ET):
                                ins = nc.tensor.transpose(ps[4][:, k * P:(k + 1) * P], hh[:, k * P:(k + 1) * P], ident[:, :])
                            ins.then_inc(hid_turned, 1)
                            for x in range(2):
                                c = W_MOE + 4 + x
                                pe.wait_ge(landed[c % SLOTS], pair * 16 + landed_by[c])
                            pe.wait_ge(hT_ready, q + 1)
                            if free is not None:
                                pe.wait_ge(out_ready, free)
                            for half in range(2):
                                for k in range(ET):
                                    for x in range(2):
                                        ins = nc.tensor.matmul(ps[5 + half][64 * x:64 * x + 64, :], hT[:, k, 64 * x:64 * x + 64],
                                                               w(4 + x)[:, k, half * 512:(half + 1) * 512], start=k == 0,
                                                               stop=k == ET - 1)
                            ins.then_inc(w2_done, 1)

                        warm_up(ps[0])
                        turn(0)
                        up(0, 0)
                        last = pe.value_load(plan[0:1, LAST:LAST + 1], min_val=PAIRS - 1, max_val=NBLK - 1)
                        pair1 = pe.value_load(plan[0:1, 1:2], min_val=0, max_val=PAIRS - 1)
                        turn(1)
                        down(0, 0, None)
                        up(1, pair1)
                        with pe.Fori(1, last) as q:
                            before = pe.value_load(plan[0:1, bass.ds(q, 1)], min_val=0, max_val=PAIRS - 1)
                            turn(q + 1)
                            down(q, before, q)
                            pair = pe.value_load(plan[0:1, bass.ds(q + 1, 1)], min_val=0, max_val=PAIRS - 1)
                            up(q + 1, pair)
                        down(last, PAIRS - 1, last)

                    @block.scalar
                    def _(act):
                        def silu(q):
                            act.wait_ge(w1_done, q + 1)
                            nc.scalar.activation(sg[:, :], ps[2][:, :], ACT.Silu).then_inc(silu_done, 1)

                        def hidden(q):
                            act.wait_ge(hid_turned, q + 1)
                            nc.scalar.copy(hT[:, :, :], ps[4][:, :].rearrange("p (k n) -> p k n", k=ET)).then_inc(hT_ready, 1)

                        def first():
                            silu(0)
                            hidden(0)

                        def store_rows(q):
                            act.wait_ge(out_ready, q)
                            act.dma_start(ys[bass.ds(q * P - P, P), :], yb[:, :]).then_inc(out_stored, 16)

                        def body(q):
                            store_rows(q)
                            silu(q)
                            hidden(q)
                        n = blocks(act, first, body)
                        store_rows(n)
                        act.wait_ge(out_stored, n * 16)
                        act.sem_inc(all_stored, 1)

                    @block.vector
                    def _(dve):
                        def rows(q):
                            dve.wait_ge(turned, q + 1)
                            for h in range(2):
                                ins = nc.vector.tensor_tensor(xT[:, 4 * h:4 * h + 4, :],
                                                              ps[h][:, :].rearrange("p (k n) -> p k n", k=4),
                                                              gcol[:, 3, 4 * h:4 * h + 4].unsqueeze(2).broadcast_to([P, 4, P]),
                                                              ALU.mult)
                            ins.then_inc(xT_ready, 1)

                        def hidden(q):
                            dve.wait_ge(silu_done, q + 1)
                            dve.wait_ge(w3_done, q + 1)
                            nc.vector.tensor_tensor(hh[:, :], ps[3][:, :], sg[:, :], ALU.mult).then_inc(hid_done, 1)

                        def out(n):
                            dve.wait_ge(w2_done, n)
                            nc.vector.tensor_copy(yb[:, 0:512], ps[5][:, :])
                            nc.vector.tensor_copy(yb[:, 512:D], ps[6][:, :]).then_inc(out_ready, 1)

                        rows(0)
                        hidden(0)
                        last = dve.value_load(plan[0:1, LAST:LAST + 1], min_val=PAIRS - 1, max_val=NBLK - 1)
                        rows(1)
                        dve.wait_ge(hid_turned, 1)
                        out(1)
                        hidden(1)
                        with dve.Fori(1, last) as q:
                            rows(q + 1)
                            dve.wait_ge(out_stored, q * 16)
                            out(q + 1)
                            dve.wait_ge(hid_turned, q + 1)
                            hidden(q + 1)
                        dve.wait_ge(out_stored, last * 16)
                        out(last + 1)

        def final_block(hN, gate, slots, ys):
            with ExitStack() as c:
                yg = sb(c, "yg", [P, 2 * T, D])
                sq = sb(c, "fsq", [P, D])
                ss = sb(c, "fss", [P, T])
                gf = sb(c, "gf", [P, D])
                gl = [sem(c, f"fgl{i}") for i in range(2 * T)]
                ld, sd, sqd, rd, yd, ch, sr = (sem(c, "f" + n) for n in ("ld", "sd", "sqd", "rd", "yd", "ch", "sr"))
                with nc.Block() as block:
                    @block.sync
                    def _(sp):
                        sp.dma_start(gf[:, :], a["g_final"].partition_broadcast(P)).then_inc(ld, 16)
                        for t in range(T):
                            sp.wait_ge(yd, t + 1)
                            dst = a["y_prompt"][0, t * P:(t + 1) * P, :] if t < TP else a["y_sample"].rearrange("b q d -> (b q) d")
                            store(sp, dst, hN[:, t, :])
                        sp.wait_ge(stored, ns[0])

                    @block.gpsimd
                    def _(pool):
                        for t in range(T):
                            for k in range(2):
                                i = 2 * t + k
                                pool.indirect_dma_start(
                                    out=yg[:, i, :], out_offset=None, in_=ys,
                                    in_offset=bass.IndirectOffsetOnAxis(ap=slots[:, k * T + t:k * T + t + 1], axis=0),
                                    bounds_check=NSLOT - 1, oob_is_err=False).then_inc(gl[i], 16)

                    @block.scalar
                    def _(act):
                        for t in range(T):
                            act.wait_ge(sd, t + 1)
                            if t:
                                act.wait_ge(sqd, t)
                            nc.scalar.activation(sq[:, :], hN[:, t, :], ACT.Square, accum_out=ss[:, t:t + 1]).then_inc(sqd, 1)
                            act.wait_ge(rd, t + 1)
                            nc.scalar.activation(ss[:, t:t + 1], ss[:, t:t + 1], ACT.Sqrt).then_inc(sr, 1)

                    @block.vector
                    def _(dve):
                        link = chain(dve, ch)

                        def combine(t):
                            for k in range(2):
                                dve.wait_ge(gl[2 * t + k], 16)
                                ins = nc.vector.scalar_tensor_tensor(out=hN[:, t, :], in0=yg[:, 2 * t + k, :],
                                                                     scalar=gate[:, k, t:t + 1], in1=hN[:, t, :],
                                                                     op0=ALU.mult, op1=ALU.add)
                                if k == 0:
                                    link(ins)
                            ins.then_inc(sd, 1)

                        def norm(t):
                            dve.wait_ge(sqd, t + 1)
                            nc.vector.tensor_scalar(ss[:, t:t + 1], ss[:, t:t + 1], 1.0 / D, EPS, ALU.mult, ALU.add).then_inc(rd, 1)
                            dve.wait_ge(sr, t + 1)
                            link(nc.vector.reciprocal(ss[:, t:t + 1], ss[:, t:t + 1]))
                            nc.vector.scalar_tensor_tensor(out=hN[:, t, :], in0=hN[:, t, :], scalar=ss[:, t:t + 1],
                                                           in1=gf[:, :], op0=ALU.mult, op1=ALU.mult).then_inc(yd, 1)

                        combine(0)
                        dve.wait_ge(ld, 16)
                        for t in range(T):
                            if t + 1 < T:
                                combine(t + 1)
                            norm(t)

        def x_tile(t):
            return a["x_prompt"][0, t * P:(t + 1) * P, :] if t < TP else a["x_sample"].rearrange("b q d -> (b q) d")

        def per_tile(prompt, sample, f):
            def at(t):
                if t < TP:
                    return a[prompt].rearrange(f"l b t {f} -> (l b t) ({f})")[t * P:(t + 1) * P, :]
                return a[sample].rearrange(f"l b t {f} -> (l b t) ({f})")
            return at

        tab = nc.dram_tensor("row_tokens", [NSLOT, 1], U32, kind="Internal").ap()
        xs = nc.dram_tensor("ffn_rows", [NTOK, D], F32, kind="Internal").ap()
        ys = nc.dram_tensor("expert_rows", [NSLOT, D], F32, kind="Internal").ap()

        lamcol = sb(top, "lamcol", [P, 1])[:, :]
        with ExitStack() as c1:
            mixT = dual(c1, "mixT", [P, KT, NTOK])
            foxN = dual(c1, "foxN", [P, 512])
            with ExitStack() as c2:
                nT = dual(c2, "nT", [P, KT, NTOK])
                with ExitStack() as c3:
                    xN = sb(c3, "xN", [P, T, D])
                    norm_block("n1", xN, T, 0, nT, x_tile, (0, 3))
                with ExitStack() as c3:
                    qT, kT, vN = (sb(c3, n, [P, 4, NTOK]) for n in ("fqT", "fkT", "fvN_"))
                    vN = vN[:, :, :].rearrange("p a b -> p (a b)").rearrange("p (t n) -> p t n", t=T)
                    CT = sb(c3, "CT", [80, KS])
                    L2 = sb(c3, "L2", [64, NB, P])
                    bias_l = sb(c3, "bias_l", [80, NB, P])
                    with ExitStack() as c4:
                        RL, RR = dual(c4, "RL", [P, 2, SEQ]), dual(c4, "RR", [P, 2, SEQ])
                        with ExitStack() as c5:
                            project_block("pf", nT, mixT, qT, kT, vN, W_FOX, (6, 9), True,
                                          per_tile("p_fk", "s_fk", "h d"), per_tile("p_fv", "s_fv", "h d"),
                                          gates=Gates(c5, nT, mixT, RL, RR, CT, L2, bias_l, foxN))
                        prompt_attention("fp", "fox", qT, kT, vN, None, mixT, RL=RL, RR=RR, blank=ys[PAIRS * P:, :],
                                         chunk_range=(9, 12), join=(nT, mixT))
                    decode_attention("fd", "fox", qT, kT, vN, foxN, C_FOX, bias_l=bias_l, CT=CT, L2=L2, chunk_range=(12, 13))
                recycle_semaphores()
                with ExitStack() as c3:
                    qT, kT, vN = (sb(c3, n, [P, 4, NTOK]) for n in ("dqT", "dkT", "dvN_"))
                    vN = vN[:, :, :].rearrange("p a b -> p (a b)").rearrange("p (t n) -> p t n", t=T)
                    with ExitStack() as c4:
                        nH = dual(c4, "nH", [P, KT, NTOK])
                        project_block("pd", nT, nH, qT, kT, vN, W_DIFF, (16, 19), False,
                                      per_tile("p_dk", "s_dk", "h c d"), per_tile("p_dv", "s_dv", "h d"), lamcol=lamcol)
                    diffN = nT[:, 0:4, :].rearrange("p a b -> p (a b)").rearrange("p (t n) -> p t n", t=T)
                    prompt_attention("dp", "diff", qT, kT, vN, diffN, None, lamcol=lamcol, chunk_range=(19, 22))
                    decode_attention("dd", "diff", qT, kT, vN, diffN[:, TP, :], C_DIFF, lamcol=lamcol, chunk_range=(0, 0))
                    mix_block(foxN, diffN, mixT, (24, 26))
            hN = sb(c1, "hN", [P, T, D])
            recycle_semaphores()
            nT = mixT
            with ExitStack() as c2:
                mkT, mvN = sb(c2, "mkT", [P, KT, MEM]), sb(c2, "mvN", [P, 2, D])
                with ExitStack() as c3:
                    memN, mT = sb(c3, "memN", [P, 2, D]), dual(c3, "mT", [P, KT, MEM])
                    residual_block("ro", mixT, hN, W_O, (0, 0), 1, load=x_tile, mem=(memN, mT, 2))
                    memory_block(mT, mkT, mvN)
                qT = sb(c2, "mqT", [P, KT, NTOK])
                query_block(nT, qT, (36, 39))
                prompt_attention("mp", "mem", qT, mkT, mvN, None, nT, chunk_range=(39, 42))
                with ExitStack() as c3:
                    oN = sb(c3, "moN", [P, D])
                    decode_attention("md", "mem", qT, None, None, oN, C_MEM, chunk_range=(42, 46))
                    turn_block(oN, nT)
            recycle_semaphores()
            with ExitStack() as c2:
                router = sb(c2, "router", [P, KT, NG + NE])
                residual_block("rm", nT, hN, W_MO, (48, 50), 3, rows=xs, router=router)
            with ExitStack() as c2:
                gate = sb(c2, "gate", [P, 2, T])
                slots = sb(c2, "slots", [P, 2 * T], U32)
                plan = sb(c2, "plan", [1, ORDER + NE], I32)
                with ExitStack() as c3:
                    xg = sb(c3, "xg", [P, D])
                    idx = sb(c3, "idx", [P, NBLK], U32)
                    route_block(xg, gate, slots, idx, plan, tab)
                    expert_block(xg, idx, xs, ys, plan)
                final_block(hN, gate, slots, ys)


_INS = ["x_prompt", "x_sample", "cache_fox_k", "cache_fox_v", "cache_fox_logf", "cache_diff_k", "cache_diff_v",
        "cache_mem_k", "cache_mem_v", "mem_prompt", "g_mix", "w_in", "b_forget", "lam_q1", "lam_k1", "lam_q2", "lam_k2",
        "g_diff", "w_o", "g_mem_q", "g_mem_kv", "w_mq", "w_mk", "w_mv", "w_mo", "g_ffn", "w_group", "b_group",
        "w_erouter", "b_erouter", "w1", "w3", "w2", "g_final"]
_OUTS = [("y_prompt", (1, SEQ, D)), ("y_sample", (NB, TD, D)),
         ("p_fk", (1, 1, SEQ, FH, HD)), ("p_fv", (1, 1, SEQ, FH, HD)), ("p_logf", (1, 1, SEQ, FH)),
         ("p_dk", (1, 1, SEQ, DH, 2, HD)), ("p_dv", (1, 1, SEQ, DH, 128)),
         ("p_mk", (1, 1, MEM, MH, MD)), ("p_mv", (1, 1, MEM, MH, MD)),
         ("s_fk", (1, NB, TD, FH, HD)), ("s_fv", (1, NB, TD, FH, HD)), ("s_logf", (1, NB, TD, FH)),
         ("s_dk", (1, NB, TD, DH, 2, HD)), ("s_dv", (1, NB, TD, DH, 128))]


def constants(np):
    f = np.float32
    i = np.arange(P)
    big = f(-1e30)
    out = {"c_ident": np.eye(P, dtype=f),
           "c_causal": np.where(i[None, :] <= i[:, None], f(0), big),
           "c_chunk": np.where(i[None, :] // 64 <= i[:, None] // 64, f(0), big)}
    pos = np.concatenate([np.arange(SEQ), np.tile(PAST + np.arange(TD), NB)]).astype(f)
    inv = np.power(f(500000.0), -np.arange(8, dtype=f) / f(8)).astype(f)
    ang = (pos[:, None] * inv[None, :]).astype(f)
    cos, sin = np.cos(ang), np.sin(ang)
    tiles = lambda x: np.ascontiguousarray(x.reshape(T, P, 16).transpose(1, 0, 2)).astype(f)
    out["c_cos"] = tiles(np.concatenate([cos, cos], 1))
    out["c_sin"] = tiles(np.concatenate([-sin, sin], 1))
    sel = np.zeros((80, NB, FH, TD), f)
    for b in range(NB):
        for h in range(FH):
            sel[b * FH + h, b, h, :] = -1.0 / SC
    for q in range(TD):
        sel[64 + q, :, :, q] = 1.0
    out["c_sel"] = sel.reshape(80, NB, P)
    tri16 = np.zeros((TD, KS), f)
    tri16[:, PAST:] = np.where(np.arange(TD)[None, :] > np.arange(TD)[:, None], big, f(0))
    out["c_tri16"] = tri16
    comb = np.zeros((P, P), f)
    sgn = np.zeros((P, 2), f)
    for h in range(DH):
        for cc in range(2):
            for q in range(TD):
                comb[32 * h + 16 * cc + q, 32 * h + q] = 1.0
                sgn[32 * h + 16 * cc + q, cc] = 1.0
    out["c_comb"], out["c_sgn"] = comb, sgn
    out["c_tri"] = (i[:, None] < i[None, :]).astype(f)
    cst = np.zeros((P, 128), f)
    cst[:, 0:4] = np.arange(4, 0, -1)
    cst[:, 4:12] = np.arange(8, 0, -1)
    cst[:, 12:44] = CAP * (np.arange(NE) % 2)
    cst[:, 44:44 + MAXB - 1] = CAP * np.arange(1, MAXB)
    cst[:, 53:53 + NBLK] = np.arange(NBLK)
    out["c_route"] = cst
    out["c_tok"] = (np.arange(T, dtype=np.int32)[None, :] * P + i[:, None].astype(np.int32)).astype(np.int32)
    return {k: np.ascontiguousarray(v) for k, v in out.items()}


def kernel(**inputs):
    import numpy as np
    import concourse.bacc as bacc
    from concourse.bass_utils import run_bass_kernel_spmd

    nc = bacc.Bacc("TRN2", target_bir_lowering=False, num_devices=1)
    arrays, aps = {}, {}
    given = {n: np.ascontiguousarray(inputs[n]) for n in _INS}
    for n, x in {**given, **constants(np)}.items():
        arrays[f"in_{n}"] = x
        aps[n] = nc.dram_tensor(f"in_{n}", x.shape, mybir.dt.from_np(x.dtype), kind="ExternalInput").ap()
    for n, shape in _OUTS:
        aps[n] = nc.dram_tensor(f"out_{n}", shape, F32, kind="ExternalOutput").ap()
    build(nc, aps)
    r = run_bass_kernel_spmd(nc, [arrays], core_ids=[0])
    return tuple(r.results[0][f"out_{n}"] for n, _ in _OUTS)
```
